# Optimizing a Trainium2 kernel written in Bass

```python
import jax, jax.numpy as jnp
from jax import lax
import numpy as np
import jax
import jax.numpy as jnp

D_MODEL = 1024
BATCH = 1
SEQ = 256
DEPTH = 2

F_WIDTH = D_MODEL
F_GROUP_DIM = 128
F_GROUPS = F_WIDTH // F_GROUP_DIM
RET_HEADS = 4
RET_DK = D_MODEL // RET_HEADS
RET_DV = D_MODEL // RET_HEADS
RET_QK = RET_HEADS * RET_DK
RET_V = RET_HEADS * RET_DV
CHUNK = 128
ROPE_BASE = 10000.0
DECAY_OFFSET_FWD = 0.0
DECAY_OFFSET_BWD = 0.5
D_FF = 2816
CONV_WIDTH = 3
N_MOD = 6
EPS = 1e-6
IN_SIZES = (F_WIDTH, RET_QK, RET_QK, RET_V, RET_V, D_MODEL, D_MODEL)
D_IN = F_WIDTH + 2 * RET_QK + 2 * RET_V + 2 * D_MODEL


def rmsnorm(x, g):
    xf = x.astype(jnp.float32)
    y = xf * lax.rsqrt(jnp.mean(xf * xf, axis=-1, keepdims=True) + EPS)
    return (y * g.astype(jnp.float32)).astype(x.dtype)

def decay_logs(offset):
    expo = -(5.0 + offset) - jnp.arange(RET_HEADS, dtype=jnp.float32)
    return jnp.log1p(-jnp.exp2(expo))

def fourier_mix(u):
    B, S, _ = u.shape
    ug = u.astype(jnp.float32).reshape(B, S, F_GROUPS, F_GROUP_DIM)
    y = jnp.fft.fft2(ug, axes=(1, 3), norm='ortho').real
    return y.reshape(B, S, F_WIDTH).astype(u.dtype)

def rotary(t):
    S = t.shape[1]
    half = t.shape[-1] // 2
    inv_freq = ROPE_BASE ** (-jnp.arange(half, dtype=jnp.float32) / half)
    ang = jnp.arange(S, dtype=jnp.float32)[:, None] * inv_freq[None, :]
    cos = jnp.cos(ang)[None, :, None, :]
    sin = jnp.sin(ang)[None, :, None, :]
    t1, t2 = t[..., :half], t[..., half:]
    return jnp.concatenate([t1 * cos - t2 * sin, t1 * sin + t2 * cos], axis=-1)

def chunk_retention(q, k, v, log_gamma, strict):
    B, H, S, dk = q.shape
    dv = v.shape[-1]
    n_chunks = S // CHUNK
    qc = q.reshape(B, H, n_chunks, CHUNK, dk)
    kc = k.reshape(B, H, n_chunks, CHUNK, dk)
    vc = v.reshape(B, H, n_chunks, CHUNK, dv)
    j = jnp.arange(CHUNK, dtype=jnp.float32)
    diff = j[:, None] - j[None, :]
    keep = (diff > 0) if strict else (diff >= 0)
    dmask = jnp.where(keep[None], jnp.exp(log_gamma[:, None, None] * jnp.maximum(diff, 0.0)[None]), 0.0)
    scores = jnp.einsum('bhncd,bhnld->bhncl', qc, kc) * dmask[None, :, None]
    intra = jnp.einsum('bhncl,bhnle->bhnce', scores, vc)
    q_decay = jnp.exp(log_gamma[:, None] * (j + 1.0))[None, :, :, None]
    k_decay = jnp.exp(log_gamma[:, None] * (CHUNK - 1.0 - j))[None, :, :, None]
    chunk_decay = jnp.exp(log_gamma * CHUNK)[None, :, None, None]

    def step(state, xs):
        qi, ki, vi = xs
        cross = jnp.einsum('bhcd,bhde->bhce', qi, state) * q_decay
        state = state * chunk_decay + jnp.einsum('bhcd,bhce->bhde', ki * k_decay, vi)
        return state, cross

    state0 = jnp.zeros((B, H, dk, dv), jnp.float32)
    xs = (jnp.moveaxis(qc, 2, 0), jnp.moveaxis(kc, 2, 0), jnp.moveaxis(vc, 2, 0))
    _, cross = lax.scan(step, state0, xs)
    out = intra + jnp.moveaxis(cross, 0, 2)
    return out.reshape(B, H, S, dv)

def retention_branch(q, k, v, g):
    B, S, _ = q.shape
    dt = q.dtype
    qh = rotary(q.astype(jnp.float32).reshape(B, S, RET_HEADS, RET_DK)) * (RET_DK ** -0.5)
    kh = rotary(k.astype(jnp.float32).reshape(B, S, RET_HEADS, RET_DK))
    vh = v.astype(jnp.float32).reshape(B, S, RET_HEADS, RET_DV)
    qh = jnp.transpose(qh, (0, 2, 1, 3))
    kh = jnp.transpose(kh, (0, 2, 1, 3))
    vh = jnp.transpose(vh, (0, 2, 1, 3))
    fwd = chunk_retention(qh, kh, vh, decay_logs(DECAY_OFFSET_FWD), strict=False)
    bwd = jnp.flip(chunk_retention(jnp.flip(qh, axis=2), jnp.flip(kh, axis=2), jnp.flip(vh, axis=2),
                                   decay_logs(DECAY_OFFSET_BWD), strict=True), axis=2)
    y = jnp.transpose(fwd + bwd, (0, 2, 1, 3))
    mu = jnp.mean(y, axis=-1, keepdims=True)
    var = jnp.mean(jnp.square(y - mu), axis=-1, keepdims=True)
    y = (y - mu) * lax.rsqrt(var + EPS)
    y = y.reshape(B, S, RET_V) * jax.nn.silu(g.astype(jnp.float32))
    return y.astype(dt)

def token_mix(h, w_in, w_fourier, w_ret, w_out):
    proj = h @ w_in
    offsets = np.cumsum(IN_SIZES)[:-1].tolist()
    u_f, q, k, v, g, a_f, a_r = jnp.split(proj, offsets, axis=-1)
    y_f = fourier_mix(u_f) @ w_fourier
    y_r = retention_branch(q, k, v, g) @ w_ret
    merged = jax.nn.sigmoid(a_f) * y_f + jax.nn.sigmoid(a_r) * y_r
    return merged @ w_out

def conv_ffn(h, w_up, conv_w, conv_b, w_down):
    S = h.shape[1]
    u = h @ w_up
    pad = CONV_WIDTH // 2
    up = jnp.pad(u, ((0, 0), (pad, pad), (0, 0)))
    u = sum(up[:, i:i + S] * conv_w[i] for i in range(CONV_WIDTH)) + conv_b
    a, b = jnp.split(u, 2, axis=-1)
    return (jax.nn.gelu(a, approximate=False) * b) @ w_down

def first_inputs(seed: int = 0) -> dict:
    key = jax.random.key(seed)
    ks = jax.random.split(key, 15)

    def nrm(k, shape, scale):
        return jax.random.normal(k, shape, jnp.float32) * scale

    return {
        'x': nrm(ks[0], (BATCH, SEQ, D_MODEL), 1.0),
        'c': nrm(ks[1], (BATCH, D_MODEL), 1.0),
        'norm1_g': 1.0 + nrm(ks[2], (DEPTH, D_MODEL), 0.02),
        'norm2_g': 1.0 + nrm(ks[3], (DEPTH, D_MODEL), 0.02),
        'ada_w': nrm(ks[4], (DEPTH, D_MODEL, N_MOD * D_MODEL), 0.5 * D_MODEL ** -0.5),
        'ada_b': nrm(ks[5], (DEPTH, N_MOD * D_MODEL), 0.02),
        'w_in': nrm(ks[6], (DEPTH, D_MODEL, D_IN), D_MODEL ** -0.5),
        'w_fourier': nrm(ks[7], (DEPTH, F_WIDTH, D_MODEL), F_WIDTH ** -0.5),
        'w_ret': nrm(ks[8], (DEPTH, RET_V, D_MODEL), RET_V ** -0.5),
        'w_out': nrm(ks[9], (DEPTH, D_MODEL, D_MODEL), D_MODEL ** -0.5),
        'ffn_up': nrm(ks[10], (DEPTH, D_MODEL, 2 * D_FF), D_MODEL ** -0.5),
        'conv_w': nrm(ks[11], (DEPTH, CONV_WIDTH, 2 * D_FF), CONV_WIDTH ** -0.5),
        'conv_b': nrm(ks[12], (DEPTH, 2 * D_FF), 0.02),
        'ffn_down': nrm(ks[13], (DEPTH, D_FF, D_MODEL), D_FF ** -0.5),
        'final_g': 1.0 + nrm(ks[14], (D_MODEL,), 0.02),
    }

def first_block(x, c, norm1_g, norm2_g, ada_w, ada_b, w_in, w_fourier, w_ret, w_out,
              ffn_up, conv_w, conv_b, ffn_down, final_g):
    c_act = jax.nn.silu(c)
    for l in range(DEPTH):
        mod = (c_act @ ada_w[l] + ada_b[l])[:, None, :]
        sh1, sc1, g1, sh2, sc2, g2 = jnp.split(mod, N_MOD, axis=-1)
        h = rmsnorm(x, norm1_g[l]) * (1.0 + sc1) + sh1
        x = x + g1 * token_mix(h, w_in[l], w_fourier[l], w_ret[l], w_out[l])
        h = rmsnorm(x, norm2_g[l]) * (1.0 + sc2) + sh2
        x = x + g2 * conv_ffn(h, ffn_up[l], conv_w[l], conv_b[l], ffn_down[l])
    return rmsnorm(x, final_g)


GRID_W = 64
CTX_LEN = 256

POOL_WINDOWS = (2, 4, 8, 16)
POOL_GROUPS = 4
POOL_GROUP_DIM = D_MODEL // 16
POOL_WIDTH = POOL_GROUPS * POOL_GROUP_DIM

SGU_CHUNK = 128
SGU_HEADS = 4
SGU_HEAD_DIM = D_MODEL // 16
SGU_WIDTH = SGU_HEADS * SGU_HEAD_DIM

NA_HEAD_DIM = 64
NA_HEADS = D_MODEL // 128
NA_WIDTH = NA_HEADS * NA_HEAD_DIM
NA_KH = 8
NA_KW = 16
ROPE_THETA = 10000.0

N_BRANCH = 3
D_FF_2 = 4 * D_MODEL

P_END = POOL_WIDTH
U_END = P_END + SGU_WIDTH
VS_END = U_END + SGU_WIDTH
Q_END = VS_END + NA_WIDTH
K_END = Q_END + NA_WIDTH
V_END = K_END + NA_WIDTH
PROJ_COLS = V_END + N_BRANCH * D_MODEL
SPLIT_POINTS = (P_END, U_END, VS_END, Q_END, K_END, V_END)


def rms_norm(x, g):
    x32 = x.astype(jnp.float32)
    y = x32 * lax.rsqrt(jnp.mean(x32 * x32, axis=-1, keepdims=True) + EPS)
    return (y * g.astype(jnp.float32)).astype(x.dtype)

def modulate(h, shift, scale):
    return h * (1 + scale) + shift

def to_heads(t):
    return t.reshape(t.shape[0], t.shape[1], NA_HEADS, NA_HEAD_DIM)

def pool_mix(p, w_pool, pool_scale):
    B, L, _ = p.shape
    pg = p.reshape(B, L, POOL_GROUPS, POOL_GROUP_DIM).astype(jnp.float32)
    csum = jnp.concatenate([jnp.zeros((B, 1, POOL_GROUPS, POOL_GROUP_DIM), jnp.float32),
                            jnp.cumsum(pg, axis=1)], axis=1)
    t = jnp.arange(L)
    outs = []
    for g, w in enumerate(POOL_WINDOWS):
        lo = jnp.clip(t - w // 2, 0, L)
        hi = jnp.clip(t + (w - w // 2), 0, L)
        cg = csum[:, :, g]
        win_sum = jnp.take(cg, hi, axis=1) - jnp.take(cg, lo, axis=1)
        cnt = (hi - lo).astype(jnp.float32)[None, :, None]
        outs.append(win_sum / cnt - pg[:, :, g])
    pooled = jnp.stack(outs, axis=2).astype(p.dtype)
    y = jnp.einsum('blgd,gde->blge', pooled, w_pool)
    return y.reshape(B, L, POOL_WIDTH) * pool_scale

def sgu_mix(u, v, sgu_w, sgu_b):
    B, L, _ = v.shape
    n_chunks = L // SGU_CHUNK
    v32 = v.astype(jnp.float32)
    mu = jnp.mean(v32, axis=-1, keepdims=True)
    var = jnp.mean(jnp.square(v32 - mu), axis=-1, keepdims=True)
    vn = ((v32 - mu) * lax.rsqrt(var + EPS)).astype(v.dtype)
    vc = vn.reshape(B, n_chunks, SGU_CHUNK, SGU_HEADS, SGU_HEAD_DIM)
    mixed = jnp.einsum('hpq,bcqhd->bcphd', sgu_w, vc) + sgu_b.T[None, None, :, :, None]
    return u * mixed.reshape(B, L, SGU_WIDTH)

def axial_rope(L):
    t = jnp.arange(L)
    row = (t // GRID_W).astype(jnp.float32)
    col = (t % GRID_W).astype(jnp.float32)
    n_freq = NA_HEAD_DIM // 4
    inv_freq = ROPE_THETA ** (-jnp.arange(n_freq, dtype=jnp.float32) / n_freq)
    ang = jnp.concatenate([row[:, None] * inv_freq, col[:, None] * inv_freq], axis=-1)
    return jnp.cos(ang), jnp.sin(ang)

def apply_rope(x, cos, sin):
    x32 = x.astype(jnp.float32)
    x1, x2 = x32[..., 0::2], x32[..., 1::2]
    c = cos[None, :, None, :]
    s = sin[None, :, None, :]
    y = jnp.stack([x1 * c - x2 * s, x1 * s + x2 * c], axis=-1)
    return y.reshape(x.shape).astype(x.dtype)

def context_attention(q, k, v):
    s = jnp.einsum('bqhd,bkhd->bhqk', q, k).astype(jnp.float32) * (NA_HEAD_DIM ** -0.5)
    p = jax.nn.softmax(s, axis=-1).astype(v.dtype)
    return jnp.einsum('bhqk,bkhd->bqhd', p, v)

def neighbourhood_attention(q, k, v, k_ctx, v_ctx, rpb, rows):
    B, L, H, Dh = q.shape
    kh = min(NA_KH, rows)
    kw = NA_KW
    scale = Dh ** -0.5
    kg = k.reshape(B, rows, GRID_W, H, Dh)
    vg = v.reshape(B, rows, GRID_W, H, Dh)
    q_rows = q.reshape(B, rows, GRID_W, H, Dh).transpose(1, 0, 2, 3, 4)
    col = np.arange(GRID_W)
    col_start = np.clip(col - kw // 2, 0, GRID_W - kw)
    col_idx = col_start[:, None] + np.arange(kw)[None, :]
    dc = col_idx - col[:, None] + (NA_KW - 1)
    n_win = kh * kw

    def row_block(args):
        r, q_row = args
        rs = jnp.clip(r - kh // 2, 0, rows - kh)
        k_rows = lax.dynamic_slice_in_dim(kg, rs, kh, axis=1)
        v_rows = lax.dynamic_slice_in_dim(vg, rs, kh, axis=1)
        k_win = k_rows[:, :, col_idx]
        v_win = v_rows[:, :, col_idx]
        dr = rs + jnp.arange(kh) - r + (NA_KH - 1)
        bias = rpb[:, dr][:, :, dc].astype(jnp.float32)
        s_win = jnp.einsum('bqhd,biqjhd->bhqij', q_row, k_win).astype(jnp.float32) * scale
        s_win = s_win + bias.transpose(0, 2, 1, 3)[None]
        s_ctx = jnp.einsum('bqhd,bchd->bhqc', q_row, k_ctx).astype(jnp.float32) * scale
        s = jnp.concatenate([s_win.reshape(B, H, GRID_W, n_win), s_ctx], axis=-1)
        p = jax.nn.softmax(s, axis=-1).astype(v.dtype)
        p_win = p[..., :n_win].reshape(B, H, GRID_W, kh, kw)
        p_ctx = p[..., n_win:]
        return (jnp.einsum('bhqij,biqjhd->bqhd', p_win, v_win)
                + jnp.einsum('bhqc,bchd->bqhd', p_ctx, v_ctx))

    out = lax.map(row_block, (jnp.arange(rows), q_rows))
    return out.transpose(1, 0, 2, 3, 4).reshape(B, L, H, Dh)

def merge_branches(pool_o, sgu_o, attn_o, gate_logits, w_po, w_so, w_ao, w_o):
    gp, gs, ga = jnp.split(jax.nn.sigmoid(gate_logits), N_BRANCH, axis=-1)
    y = gp * (pool_o @ w_po) + gs * (sgu_o @ w_so) + ga * (attn_o @ w_ao)
    return y @ w_o

def sq_relu_mlp(h, w1, w2):
    return jnp.square(jax.nn.relu(h @ w1)) @ w2

def second_inputs(seed: int = 0) -> dict:
    key = jax.random.key(seed)
    ks = jax.random.split(key, 21)
    D = D_MODEL

    def nrm(k, shape, scale):
        return jax.random.normal(k, shape, jnp.float32) * scale

    return {
        'x': nrm(ks[0], (BATCH, SEQ, D), 1.0),
        'c': nrm(ks[1], (BATCH, D), 1.0),
        'ctx': nrm(ks[2], (BATCH, CTX_LEN, D), 1.0),
        'c_ctx': nrm(ks[3], (D,), 1.0),
        'norm1_g': 1.0 + nrm(ks[4], (DEPTH, D), 0.05),
        'norm2_g': 1.0 + nrm(ks[5], (DEPTH, D), 0.05),
        'w_mod': nrm(ks[6], (DEPTH, D, 6 * D), 0.5 * D ** -0.5),
        'b_mod': nrm(ks[7], (DEPTH, 6 * D), 0.02),
        'w_in': nrm(ks[8], (DEPTH, D, PROJ_COLS), D ** -0.5),
        'w_pool': nrm(ks[9], (DEPTH, POOL_GROUPS, POOL_GROUP_DIM, POOL_GROUP_DIM), POOL_GROUP_DIM ** -0.5),
        'pool_scale': 1.0 + nrm(ks[10], (DEPTH, POOL_WIDTH), 0.1),
        'sgu_w': nrm(ks[11], (DEPTH, SGU_HEADS, SGU_CHUNK, SGU_CHUNK), SGU_CHUNK ** -0.5),
        'sgu_b': 1.0 + nrm(ks[12], (DEPTH, SGU_HEADS, SGU_CHUNK), 0.1),
        'na_rpb': nrm(ks[13], (DEPTH, NA_HEADS, 2 * NA_KH - 1, 2 * NA_KW - 1), 0.5),
        'w_pool_out': nrm(ks[14], (DEPTH, POOL_WIDTH, D), POOL_WIDTH ** -0.5),
        'w_sgu_out': nrm(ks[15], (DEPTH, SGU_WIDTH, D), SGU_WIDTH ** -0.5),
        'w_attn_out': nrm(ks[16], (DEPTH, NA_WIDTH, D), NA_WIDTH ** -0.5),
        'w_o': nrm(ks[17], (DEPTH, D, D), D ** -0.5),
        'w_ff1': nrm(ks[18], (DEPTH, D, D_FF_2), D ** -0.5),
        'w_ff2': nrm(ks[19], (DEPTH, D_FF_2, D), D_FF_2 ** -0.5),
        'final_g': 1.0 + nrm(ks[20], (D,), 0.05),
    }

def second_block(x, c, ctx, c_ctx, norm1_g, norm2_g, w_mod, b_mod, w_in, w_pool, pool_scale,
              sgu_w, sgu_b, na_rpb, w_pool_out, w_sgu_out, w_attn_out, w_o, w_ff1, w_ff2, final_g):
    n_lat = x.shape[1]
    rows = n_lat // GRID_W
    cos, sin = axial_rope(n_lat)
    silu_c = jax.nn.silu(c)
    silu_cc = jax.nn.silu(c_ctx)
    h, hc = x, ctx
    for l in range(DEPTH):
        mod = silu_c @ w_mod[l] + b_mod[l]
        mod_c = silu_cc @ w_mod[l] + b_mod[l]
        sh1, sc1, g1, sh2, sc2, g2 = jnp.split(mod[:, None, :], 6, axis=-1)
        csh1, csc1, cg1, csh2, csc2, cg2 = jnp.split(mod_c, 6, axis=-1)
        has_ctx_out = l < DEPTH - 1

        ac = modulate(rms_norm(hc, norm1_g[l]), csh1, csc1)
        if has_ctx_out:
            p, u, vs, q, k, v, gl = jnp.split(ac @ w_in[l], SPLIT_POINTS, axis=-1)
            k_ctx, v_ctx = to_heads(k), to_heads(v)
            attn_c = context_attention(to_heads(q), k_ctx, v_ctx).reshape(hc.shape[0], hc.shape[1], NA_WIDTH)
            mix_c = merge_branches(pool_mix(p, w_pool[l], pool_scale[l]), sgu_mix(u, vs, sgu_w[l], sgu_b[l]),
                                   attn_c, gl, w_pool_out[l], w_sgu_out[l], w_attn_out[l], w_o[l])
        else:
            k, v = jnp.split(ac @ w_in[l][:, Q_END:V_END], 2, axis=-1)
            k_ctx, v_ctx = to_heads(k), to_heads(v)

        a = modulate(rms_norm(h, norm1_g[l]), sh1, sc1)
        p, u, vs, q, k, v, gl = jnp.split(a @ w_in[l], SPLIT_POINTS, axis=-1)
        attn = neighbourhood_attention(apply_rope(to_heads(q), cos, sin), apply_rope(to_heads(k), cos, sin),
                                       to_heads(v), k_ctx, v_ctx, na_rpb[l], rows)
        mix = merge_branches(pool_mix(p, w_pool[l], pool_scale[l]), sgu_mix(u, vs, sgu_w[l], sgu_b[l]),
                             attn.reshape(h.shape[0], n_lat, NA_WIDTH), gl,
                             w_pool_out[l], w_sgu_out[l], w_attn_out[l], w_o[l])
        h = h + g1 * mix
        h = h + g2 * sq_relu_mlp(modulate(rms_norm(h, norm2_g[l]), sh2, sc2), w_ff1[l], w_ff2[l])

        if has_ctx_out:
            hc = hc + cg1 * mix_c
            hc = hc + cg2 * sq_relu_mlp(modulate(rms_norm(hc, norm2_g[l]), csh2, csc2), w_ff1[l], w_ff2[l])
    return rms_norm(h, final_g)


def setup_inputs(seed=0):
    out = dict(first_inputs(seed))
    for name, value in second_inputs(seed + 1).items():
        if name != "x":
            out[name + "_2"] = value
    return out


def reference(
    x, c, norm1_g, norm2_g, ada_w, ada_b, w_in, w_fourier, w_ret, w_out, ffn_up, conv_w, conv_b,
    ffn_down, final_g, c_2, ctx_2, c_ctx_2, norm1_g_2, norm2_g_2, w_mod_2, b_mod_2, w_in_2,
    w_pool_2, pool_scale_2, sgu_w_2, sgu_b_2, na_rpb_2, w_pool_out_2, w_sgu_out_2, w_attn_out_2,
    w_o_2, w_ff1_2, w_ff2_2, final_g_2,
):
    x = first_block(
        x, c, norm1_g, norm2_g, ada_w, ada_b, w_in, w_fourier, w_ret, w_out, ffn_up, conv_w,
        conv_b, ffn_down, final_g,
    )
    return second_block(
        x, c_2, ctx_2, c_ctx_2, norm1_g_2, norm2_g_2, w_mod_2, b_mod_2, w_in_2, w_pool_2,
        pool_scale_2, sgu_w_2, sgu_b_2, na_rpb_2, w_pool_out_2, w_sgu_out_2, w_attn_out_2,
        w_o_2, w_ff1_2, w_ff2_2, final_g_2,
    )


_drawn_inputs = setup_inputs


def setup_inputs(seed=0):
    import zlib

    import numpy as np

    out = dict(_drawn_inputs(seed))
    spreads = {}
    factors = {'norm1_g': 7.263,
     'norm2_g': 5.8,
     'conv_b': 6.13,
     'final_g': 7.514,
     'ctx_2': 21.432,
     'pool_scale_2': 2.693,
     'na_rpb_2': 61.472,
     'c_ctx_2': 8.0,
     'norm1_g_2': 3.673,
     'norm2_g_2': 4.448,
     'sgu_b_2': 5.993}
    for name, (base, spread) in spreads.items():
        noise = np.random.default_rng([zlib.crc32(name.encode()), seed]).standard_normal(out[name].shape)
        drawn = base * np.exp(spread * noise) if base else spread * noise
        out[name] = jnp.asarray(drawn.astype(out[name].dtype))
    for name, factor in factors.items():
        out[name] = (out[name] * factor).astype(out[name].dtype)
    return out
```

```python
from contextlib import ExitStack

import numpy as np

import concourse.bass as bass
from concourse import mybir

F32 = mybir.dt.float32
F32R = mybir.dt.float32r
ALU = mybir.AluOpType
ACT = mybir.ActivationFunctionType
AX_X = mybir.AxisListType.X

P = 128
D = 1024
DC = D // P
S = 256
T2 = 2 * S
COLS = 512
KC = 2
UNIT = KC * COLS
D_FF = 2816
FC = D_FF // P
D_FF2 = 4096
EPS = 1e-6
HEADS1, DK1 = 4, 256
HEADS2, DK2 = 8, 64
GRID_W, NA_KW, NA_KH = 64, 16, 8
N_MOD = 6
MODC = N_MOD * DC
NS = 5
NR = 4
MASKED = -1.0e30


ATTENTION_FILL = [["v"], ["gp0"], ["po0", "gs0"], ["so0", "gp1"], ["po1", "gs1"], ["so1"], ["ga0"], ["ga1"]]


def layer_steps(layer):
    if layer < 2:
        s = [("n1", 0, 1)]
        s += [("uf0", 4, 4), ("uf1", 4, 4), ("q0", 4, 4), ("q1", 4, 4), ("F1", 0, 8)]
        s += [("k0", 4, 4), ("k1", 4, 4), ("F2", 0, 4), ("v0", 4, 2), ("v1", 4, 2)]
        s += [("af0", 4, 4), ("S0", 0, 1), ("S1", 0, 1), ("af1", 4, 4), ("V0", 0, 1), ("V1", 0, 1)]
        s += [("S2", 0, 1), ("S3", 0, 1), ("wf0", 4, 4), ("V2", 0, 1), ("V3", 0, 1), ("wf1", 4, 4)]
        s += [("M0", 0, 1), ("M1", 0, 1), ("g0", 4, 4), ("R0", 0, 1), ("R1", 0, 1)]
        s += [("g1", 4, 4), ("ar0", 4, 4), ("ar1", 4, 4), ("wr0", 4, 4), ("wr1", 4, 4)]
        s += [("wo0", 4, 4), ("wo1", 4, 4), ("n2", 0, 1)]
        s += [(f"up{b}", 4, 4) for b in range(FC // 2)] + [("dn0", FC // 2, 4), ("dn1", FC // 2, 4)]
        if layer == 1:
            s += [("nf", 0, 1)]
        return s
    s = [("n1", 0, 1), ("pu", 4, 4), ("vs", 4 // 2, 4 if layer == 2 else 2), ("q", 4, 4), ("k", 4, 4)]
    s += [("rq0", 0, 1), ("rq1", 0, 1), ("rk0", 0, 1), ("rk1", 0, 1)]
    fill = [[("v", 4, 4), ("pool", 0, 2), ("mix", 0, 2)]] + [
        [(n, 4 if n[0] == "g" else 1, 4) for n in names] for names in ATTENTION_FILL[1:]]
    ctx = layer == 2
    for h in range(HEADS2):
        s += [(f"X{h}a", 0, 1), (f"X{h}b", 0, 1)] + ([(f"C{h}", 0, 1)] if ctx else [])
        s += ([(f"O{h - 1}", 0, 1)] if h else []) + fill[h]
        s += [(f"T{h}a", 0, 1), (f"T{h}b", 0, 1)] + ([(f"U{h}", 0, 1)] if ctx else [])
    s += [(f"O{HEADS2 - 1}", 0, 1)]
    s += [("ao0", 2, 4), ("ao1", 2, 4), ("wo0", 4, 4), ("wo1", 4, 4), ("n2", 0, 1)]
    for half in range(2):
        s += [(f"f{b}", 4, 4) for b in range(4 * half, 4 * half + 4)]
        s += [(f"d{half}0", 8, 4), (f"d{half}1", 8, 4)]
    if layer == 3:
        s += [("nf", 0, 1)]
    return s


SCHEDULE = [
    (0, "uf1", 2, [(0, j) for j in range(4, 12)]), (0, "up1", 5, [(1, 0), (1, 1)]), (0, "dn0", 2, [(1, 2), (1, 3)]),
    (1, "uf1", 2, [(1, j) for j in range(4, 12)]), (1, "up1", 5, [(2, 0), (2, 1)]), (1, "dn0", 2, [(2, 2), (2, 3)]),
    (2, "pu", 1, [(2, j) for j in range(4, 12)] + [(3, j) for j in range(9)]), (3, "pu", 2, [(3, 9), (3, 10), (3, 11)]),
]


def mod_vectors(layer, j):
    if layer < 2:
        return (0,)
    return (1, 2) if layer == 2 or j < 4 else (1,)


class Plan:

    def __init__(self):
        self.step, self.stream = {}, []
        steps = [(layer,) + x for layer in range(4) for x in layer_steps(layer)]
        first, unit = {}, 0
        for layer, name, units, groups in steps:
            first[layer, name] = unit
            unit += units
        self.units = unit
        self.schedule(first)
        self.index, self.free_at, self.mods = [], [], {}
        unit = group = partial = 0
        for j in range(4):
            self.step["pro", j] = (0, 0, group, 1)
            self.stream += [("mod", 0, j, i) for i in range(4)]
            group += 1
        for layer, name, units, groups in steps:
            ends = []
            self.step[layer, name] = (unit, units, group, groups)
            for i in range(units):
                if unit + i in self.ahead:
                    target, j, part = self.ahead[unit + i]
                    self.stream.append(("mod", target, j, part))
                    if part == 3:
                        ends.append(i)
                        self.mods[layer, name, i] = (target, j)
                self.index.append(len(self.stream))
                self.stream.append(("weights", layer, name, i))
                partial += i < units - 1
                self.free_at.append(("used", partial) if i < units - 1 else ("group", group + groups - 1))
            unit += units
            group += groups
            for i in ends:
                self.step[layer, name, i] = (0, 0, group, 1)
                group += 1

    def schedule(self, first):
        self.ahead, self.rows = {}, {(0, j): j % 2 for j in range(4)}
        end = [-NR - 1, -NR - 1]
        at = 0
        for layer, name, rate, blocks in SCHEDULE:
            at = max(at, first[layer, name])
            for n, (target, j) in enumerate(blocks):
                both = len(mod_vectors(target, j)) == 2
                row = 0 if both else (0 if end[0] < end[1] else 1)
                rows = (0, 1) if both else (row,)
                at = max([at] + [end[r] + NR + 1 for r in rows])
                for part in range(4):
                    self.ahead[at + rate * part] = (target, j, part)
                for r in rows:
                    end[r] = at + 3 * rate
                self.rows[target, j] = row
                at += 4 * rate
                need = (first[target, "n1"] if j < 4 else first[target, "n2"] if j < 10 else first[target, "dn0" if target < 2 else "d00"])
                if j in (4, 5):
                    need = first[target, "wo0"]
                assert end[row] < need - 1, (target, j, end, need)


PLAN = Plan()


COLUMNS = {}


def _columns():
    at = 0

    def add(name, n):
        nonlocal at
        COLUMNS[name] = at
        at += n

    add("c", 3 * DC)
    for layer in range(4):
        add(f"n1_{layer}", DC)
        add(f"n2_{layer}", DC)
        add(f"bmod_{layer}", MODC)
    for layer in range(2):
        add(f"convw_{layer}", 3 * 2 * FC)
        add(f"convb_{layer}", 2 * FC)
    for layer in range(2, 4):
        add(f"pscale_{layer}", 2)
    add("final1", DC)
    add("final2", DC)
    return at


NCOL = _columns()


def program(nc, t):
    with ExitStack() as ctx:
        where = [nc.sbuf_base]

        def sb(name, shape, dt=F32, at=None):
            size = int(np.prod(shape[1:])) * 4
            if at is None:
                at = -(-where[0] // 32) * 32
                where[0] = at + size
            return nc.alloc_sbuf_tensor_at(name, shape, dt, offset=at)

        stage = sb("stage", [P, NS, UNIT])
        w_hi = sb("w_hi", [P, NR, UNIT], F32R)
        w_lo = sb("w_lo", [P, NR, UNIT], F32R)
        X = sb("X", [P, DC, T2])
        h_hi = sb("h_hi", [P, DC, T2], F32R)
        h_lo = sb("h_lo", [P, DC, T2], F32R)
        cols = sb("cols", [P, NCOL])
        csil = sb("csil", [P, 3 * DC])
        acc = sb("acc", [P, 2, COLS])
        MOD = sb("MOD", [P, 2, 2, MODC])
        MUL = sb("MUL", [P, 2, 2, 2, DC])
        eps = sb("eps", [1, P])
        mean_D = sb("mean_D", [P, P])
        mean_H = sb("mean_H", [P, P])
        ones = sb("ones", [P, P])
        idle = sb("idle", [1, 16])
        rstd = sb("rstd", [P, T2])

        tmp = -(-where[0] // 32) * 32
        KB = 1024
        sq = sb("sq", [P, 4, T2], F32, tmp)
        tt = sb("tt", [P, 4, T2], F32, tmp + 8 * KB)
        var = sb("var", [P, T2], F32, tmp + 16 * KB)
        rope_q = sb("rope_q", [P, DC, S], F32, tmp)
        rope_k = sb("rope_k", [P, DC, S], F32, tmp + 8 * KB)
        probs1 = sb("probs1", [P, 2, 2, S], F32, tmp + 16 * KB)
        sq2 = sb("sq2", [P, 2, 4, S], F32, tmp)
        var2 = sb("var2", [P, 2, 2, S], F32, tmp + 8 * KB)
        rstd2 = sb("rstd2", [P, 2, 2, S], F32, tmp + 12 * KB)
        conv = sb("conv", [P, 2, 4, S], F32, tmp)
        relu = sb("relu", [P, 4, T2], F32, tmp)
        ropeA = sb("ropeA", [P, 4, 2, S], F32, tmp)
        stats = sb("stats", [P, 4, 12], F32, tmp + 20 * KB + 512)
        sc = sb("sc", [P, 2, T2], F32, tmp)
        scc = sb("scc", [P, 2, S], F32, tmp + 4 * KB)
        pT = sb("pT", [P, 4, S], F32, tmp + 6 * KB)
        pTc = sb("pTc", [P, 2, S], F32, tmp + 10 * KB)
        bias = sb("bias", [P, 2, 2, S], F32, tmp + 12 * KB)
        small = sb("small", [P, 4, 4], F32, tmp + 16 * KB)
        gt2 = sb("gt2", [P, 2, T2], F32, tmp + 16 * KB + 512)
        where[0] = tmp + 21 * KB

        ph = where[0]
        q1 = sb("q1", [P, DC, S], F32, ph)
        k1 = sb("k1", [P, DC, S], F32, ph + 8 * KB)
        v1 = sb("v1", [P, 2, D], F32, ph + 16 * KB)
        uf = sb("uf", [P, DC, S], F32, ph + 24 * KB)
        AB = sb("AB", [P, 2, DC, 2 * P], F32, ph + 32 * KB)
        r_hi = sb("r_hi", [P, DC, S], F32R, ph + 24 * KB)
        r_lo = sb("r_lo", [P, DC, S], F32R, ph + 32 * KB)
        g1 = sb("g1", [P, DC, S], F32, ph + 40 * KB)
        y1 = sb("y1", [P, DC, S], F32, ph + 48 * KB)
        rope1 = sb("rope1", [P, 2, S], F32, ph + 56 * KB)
        decay = sb("decay", [P, HEADS1, 2, S], F32, ph + 58 * KB)
        dftg = sb("dftg", [P, 2 * P], F32, ph + 66 * KB)
        dfts = sb("dfts", [P, 2, 2, S], F32, ph + 67 * KB)
        u_hi = sb("u_hi", [P, FC, S], F32R, ph)
        u_lo = sb("u_lo", [P, FC, S], F32R, ph + 22 * KB)

        q2 = sb("q2", [P, 4, T2], F32, ph)
        k2 = sb("k2", [P, 4, T2], F32, ph + 8 * KB)
        v2 = sb("v2", [P, 4, COLS], F32, ph + 16 * KB)
        y2 = sb("y2", [P, DC, T2], F32, ph + 24 * KB)
        b_hi = sb("b_hi", [P, 4, T2], F32R, ph + 40 * KB)
        b_lo = sb("b_lo", [P, 4, T2], F32R, ph + 48 * KB)
        PADW = S + 2 * 8
        pp = sb("pp", [P, 2, 2, PADW], F32, ph + 24 * KB)
        ps2 = sb("ps2", [P, 2, 2, PADW], F32, ph + 24 * KB + 4352)
        ps4 = sb("ps4", [P, 2, 2, PADW], F32, ph + 24 * KB + 2 * 4352)
        u2 = sb("u2", [P, 2, T2], F32, ph + 56 * KB)
        vn = sb("vn", [P, 4, 2 * P], F32, ph + 60 * KB)
        pooled = sb("pooled", [P, 2, T2], F32, tmp + 8 * KB)
        gt = sb("gt", [P, 4, T2], F32, ph + 56 * KB)
        gtb = sb("gtb", [P, 4, T2], F32, ph + 8 * KB)
        f_hi = sb("f_hi", [P, 16, T2], F32R, ph)
        f_lo = sb("f_lo", [P, 16, T2], F32R, ph + 32 * KB)
        rope2 = sb("rope2", [P, 2, S], F32, ph + 64 * KB)
        rinv = sb("rinv", [P, 2, S], F32, ph + 66 * KB)
        rotm = sb("rotm", [P, P], F32, ph + 68 * KB)
        wpool = sb("wpool", [P, 2, P], F32, ph + 68 * KB + 512)
        wsgu = sb("wsgu", [P, 4, P], F32, ph + 69 * KB + 512)
        ident = sb("ident", [P, P], F32, ph + 71 * KB + 512)
        sgub = sb("sgub", [1, 4 * P], F32, ph + 72 * KB)
        assert ph + 74 * KB <= nc.sbuf_usable_end, (ph + 74 * KB, nc.sbuf_usable_end)

        banks = [ctx.enter_context(nc.psum_tensor(f"bank{b}", [P, 512], F32)) for b in range(8)]

        def sem(name):
            return ctx.enter_context(nc.semaphore(name))

        filled = [sem(f"filled{b}") for b in range(8)]
        taken = [sem(f"taken{b}") for b in range(8)]
        arrived = [sem(f"arrived{i}") for i in range(NS)]
        hi_ready = sem("hi_ready")
        unit_done = sem("unit_done")
        units_used = sem("units_used")
        s = {n: sem(n) for n in (
            "loaded", "idle", "y_added", "x_loaded", "loaded1", "loaded2", "small2", "bias_in0", "bias_in1", "csil_ready", "const_ready", "sq_ready", "sq_used", "var_ready",
            "rstd_ready", "t_ready", "hhi_ready", "h_ready", "xf_ready", "uq_rot", "uk_rot",
            "fhi_ready", "g_sig", "dev_ready", "sq2_ready", "var2_ready", "rstd2_ready", "yn_ready",
            "rhi_ready", "r_ready", "m_ready", "mhi_ready", "mm_ready", "lin_ready", "gelu_ready",
            "u_ready", "uhi_ready", "uu_ready", "pooled_ready", "phi_ready", "vvar_ready", "vstd_ready",
            "vn_ready", "so_ready", "sohi_ready", "b_ready", "pad_ready", "q2_rot", "ctx_copied",
            "nmax_ready", "exp_ready", "rsum_ready", "p_ready", "gate_ready", "ao_ready", "aohi_ready", "a_ready",
            "relu_ready", "fhid_ready", "fhihi_ready", "ff_ready", "out_ready", "stored")}

        def bank_of(g):
            return banks[g % 8]

        def wait_filled(eng, g):
            eng.wait_ge(filled[g % 8], g // 8 + 1)

        def wait_taken(eng, g):
            eng.wait_ge(taken[g % 8], g // 8 + 1)

        def grp(layer, name, i=0, at=None):
            return PLAN.step[(layer, name) if at is None else (layer, name, at)][2] + i

        def halves(T):
            return [(0, slice(0, S))] + ([(1, slice(S, T2))] if T == T2 else [])

        def col(name, i, n=1):
            return cols[:, COLUMNS[name] + i:COLUMNS[name] + i + n]

        block = ctx.enter_context(nc.Block())

        @block.sync
        def _(sp):
            sp.dma_start(cols[:, :], t["cols"]).then_inc(s["loaded"], 16)
            for n in range(NS):
                sp.dma_start(stage[:, n, :], t["stream"][n]).then_inc(arrived[n], 16)
            sp.dma_start(X[:, :, :], t["x"]).then_inc(s["x_loaded"], 16)
            total = len(PLAN.stream)

            def refills(a, b):
                with sp.Fori(a, b) as it:
                    for i in range(NS):
                        slot = i % NS
                        sp.wait_ge(unit_done, it * NS + (i + 1))
                        sp.dma_start(stage[:, slot, :],
                                     t["stream"][bass.ds(it * NS + (i + NS), 1)].rearrange("a p n -> (a p) n")
                                     ).then_inc(arrived[slot], 16)

            left = total - NS
            cut = (PLAN.index[PLAN.step[2, "pu"][0]] - NS) // NS
            refills(0, 4)
            for dst, name in ((rope1, "rope1"), (decay, "decay"), (dftg, "dftg"), (dfts, "dfts")):
                sp.dma_start(dst.ap(), t[name]).then_inc(s["loaded1"], 16)
            refills(4, cut)
            wait_taken(sp, grp(1, "up0"))
            for dst, name in ((rope2, "rope2"), (rinv, "rinv"), (rotm, "rotm"), (ident, "ident")):
                sp.dma_start(dst.ap(), t[name]).then_inc(s["loaded2"], 16)

            def small_tables(layer):
                sp.dma_start(wpool[:, :, :], t["wpool"][layer - 2]).then_inc(s["small2"], 16)
                sp.dma_start(wsgu[:, :, :], t["wsgu"][layer - 2]).then_inc(s["small2"], 16)
                sp.dma_start(sgub[:, :], t["sgub"][layer - 2]).then_inc(s["small2"], 16)

            small_tables(2)
            cut2 = PLAN.index[PLAN.step[2, "f0"][0]] // NS
            refills(cut, cut2)
            wait_taken(sp, grp(2, "mix", 1))
            wait_taken(sp, grp(2, "pool", 1))
            small_tables(3)
            refills(cut2, left // NS)
            for r in range(left // NS * NS, left):
                sp.wait_ge(unit_done, r + 1)
                n = r + NS
                sp.dma_start(stage[:, n % NS, :], t["stream"][n]).then_inc(arrived[n % NS], 16)
            sp.wait_ge(s["out_ready"], DC)
            sp.dma_start(t["out"], X[:, :, 0:S]).then_inc(s["stored"], 16)
            sp.wait_ge(s["stored"], 16)

        @block.tensor
        def _(pe):
            mm = nc.tensor.matmul

            def open_group(g):
                if g >= 8:
                    pe.wait_ge(taken[g % 8], g // 8)
                return banks[g % 8]

            def close_group(ins, g):
                ins.then_inc(filled[g % 8], 1)

            def unit_ready(m):
                pe.wait_ge(unit_done, PLAN.index[m] + 1)

            def mod_sums(layer, name, unit):
                if (layer, name, unit) in PLAN.mods:
                    sum_partitions(grp(layer, name, at=unit), *PLAN.mods[layer, name, unit])

            def sum_partitions(g, target, j):
                    row = PLAN.rows[target, j]
                    bank = open_group(g)
                    pe.wait_ge(unit_done, MOD_LAST[target, j] + 1)
                    for v in range(len(mod_vectors(target, j))):
                        for n in range(4):
                            last = mm(bank[:, 4 * v + n:4 * v + n + 1], acc[:, row + v, n * P:(n + 1) * P], ones[:, 0:1],
                                      start=True, stop=True)
                    close_group(last, g)

            def feature_block(layer, name, xh, xl, T, x_ready, k0=0, before_last=None):
                m0, nu, g0, ng = PLAN.step[layer, name]
                for i in range(nu):
                    if i == nu - 1 and before_last:
                        before_last()
                    unit_ready(m0 + i)
                    slot = (m0 + i) % NR
                    x_ready(i)
                    for n in range(ng):
                        if i == 0:
                            open_group(g0 + n)
                        out = bank_of(g0 + n)[:, 0:T]
                        for k in range(KC):
                            c = k0 + KC * i + k
                            w = slice(k * COLS + n * P, k * COLS + (n + 1) * P)
                            first, final = i == 0 and k == 0, i == nu - 1 and k == KC - 1
                            mm(out, w_hi[:, slot, w], xh[:, c, 0:T], start=first, stop=False)
                            mm(out, w_hi[:, slot, w], xl[:, c, 0:T], start=False, stop=False)
                            last = mm(out, w_lo[:, slot, w], xh[:, c, 0:T], start=False, stop=final)
                        if i == nu - 1:
                            close_group(last, g0 + n)
                    if i < nu - 1:
                        last.then_inc(units_used, 1)
                    mod_sums(layer, name, i)

            def token_block(layer, name, xh, xl, x_ready, width=COLS):
                m0, nu, g0, ng = PLAN.step[layer, name]
                kc = UNIT // width
                for i in range(nu):
                    unit_ready(m0 + i)
                    slot = (m0 + i) % NR
                    x_ready(i)
                    for n in range(ng):
                        if i == 0:
                            open_group(g0 + n)
                        out = bank_of(g0 + n)[:, 0:width]
                        tok = slice(n * P, (n + 1) * P)
                        for k in range(kc):
                            c = kc * i + k
                            w = slice(k * width, (k + 1) * width)
                            first, final = i == 0 and k == 0, i == nu - 1 and k == kc - 1
                            mm(out, xh[:, c, tok], w_hi[:, slot, w], start=first, stop=False)
                            mm(out, xh[:, c, tok], w_lo[:, slot, w], start=False, stop=False)
                            last = mm(out, xl[:, c, tok], w_hi[:, slot, w], start=False, stop=final)
                        if i == nu - 1:
                            close_group(last, g0 + n)
                    if i < nu - 1:
                        last.then_inc(units_used, 1)
                    mod_sums(layer, name, i)

            def epsilon(out, T):
                row = ones[0:1, :].rearrange("p (a n) -> p a n", a=1).to_broadcast([1, T // P, P])
                mm(out, eps[0:1, :], row, start=True, stop=False)

            def norm_sums(layer, name, T, chunks=range(DC)):
                g = grp(layer, name)
                nth = NORMS.index((layer, name))
                if 0 in chunks:
                    open_group(g)
                    epsilon(bank_of(g)[:, 0:T], T)
                for c in chunks:
                    pe.wait_ge(s["sq_ready"], nth * DC + c + 1)
                    ins = mm(bank_of(g)[:, 0:T], mean_D[:, :], sq[:, c % 4, 0:T], start=False, stop=c == DC - 1)
                    if c < DC - 1:
                        ins.then_inc(s["sq_used"], 1)
                    else:
                        close_group(ins, g)

            EARLY, LATE = range(DC // 2), range(DC // 2, DC)

            def h_ready(layer, name, per=KC):
                base = HREADY[layer, name]
                return lambda i: pe.wait_ge(s["h_ready"], base + min(per * (i + 1), DC))

            def nothing(i):
                pass

            def count(name, base, per=KC):
                return lambda i: pe.wait_ge(s[name], base + per * (i + 1))

            pe.wait_ge(s["const_ready"], 4)
            sum_partitions(grp("pro", 0), 0, 0)
            norm_sums(0, "n1", S)
            for j in range(1, 4):
                sum_partitions(grp("pro", j), 0, j)

            for L in range(2):
                hh, hl = h_hi[:, :, 0:S], h_lo[:, :, 0:S]
                if L:
                    norm_sums(L, "n1", S, LATE)
                feature_block(L, "uf0", hh, hl, S, h_ready(L, "n1"))
                for name in ("uf1", "q0", "q1"):
                    feature_block(L, name, hh, hl, S, nothing)
                if L == 0:
                    pe.wait_ge(s["loaded1"], 64)
                for c in range(DC):
                    g = grp(L, "F1", c)
                    wait_taken(pe, grp(L, f"uf{c // 4}", c % 4))
                    out = open_group(g)
                    for st in range(2):
                        last = mm(out[:, st * S:(st + 1) * S], uf[:, c, st * P:(st + 1) * P], dftg[:, :],
                                  start=True, stop=True)
                    close_group(last, g)
                for name in ("k0", "k1"):
                    feature_block(L, name, hh, hl, S, nothing)
                for cc in range(DC // 2):
                    g = grp(L, "F2", cc)
                    out = open_group(g)
                    for half in range(2):
                        c = 2 * cc + half
                        wait_taken(pe, grp(L, "F1", c))
                        for st in range(2):
                            for part in range(2):
                                last = mm(out[:, half * S:(half + 1) * S], AB[:, st, c, part * P:(part + 1) * P],
                                          dfts[:, part, st, :], start=st == 0 and part == 0,
                                          stop=st == 1 and part == 1)
                    close_group(last, g)
                for name in ("v0", "v1"):
                    token_block(L, name, hh, hl, nothing)

                def scores(h):
                    if h == 0:
                        pe.wait_ge(s["uq_rot"], L + 1)
                        pe.wait_ge(s["uk_rot"], L + 1)
                    g = grp(L, f"S{h}")
                    out = open_group(g)
                    for jt in range(2):
                        for dc in range(2):
                            last = mm(out[:, jt * S:(jt + 1) * S], k1[:, 2 * h + dc, jt * P:(jt + 1) * P],
                                      q1[:, 2 * h + dc, :], start=dc == 0, stop=dc == 1)
                    close_group(last, g)

                def values(h):
                    if h == 0:
                        for nb in range(2):
                            for tk in range(2):
                                wait_taken(pe, grp(L, f"v{nb}", tk))
                    wait_taken(pe, grp(L, f"S{h}"))
                    g = grp(L, f"V{h}")
                    out = open_group(g)
                    for dc in range(2):
                        for jt in range(2):
                            last = mm(out[:, dc * S:(dc + 1) * S],
                                      v1[:, jt, h * DK1 + dc * P:h * DK1 + (dc + 1) * P],
                                      probs1[:, h % 2, jt, :], start=jt == 0, stop=jt == 1)
                    close_group(last, g)

                def head_means(hp):
                    g = grp(L, f"M{hp}")
                    out = open_group(g)
                    for i in range(2):
                        wait_taken(pe, grp(L, f"V{2 * hp + i}"))
                        for dc in range(2):
                            last = mm(out[:, i * S:(i + 1) * S], mean_H[:, :], q1[:, 4 * hp + 2 * i + dc, :],
                                      start=dc == 0, stop=dc == 1)
                    close_group(last, g)

                def head_vars(hp):
                    g = grp(L, f"R{hp}")
                    out = open_group(g)
                    epsilon(out[:, :], T2)
                    pe.wait_ge(s["sq2_ready"], 2 * L + hp + 1)
                    for dc in range(2):
                        last = mm(out[:, :], mean_H[:, :],
                                  sq2[:, hp, :, :].rearrange("p (i d) t -> p d i t", d=2)[:, dc], start=False, stop=dc == 1)
                    close_group(last, g)

                feature_block(L, "af0", hh, hl, S, nothing)
                scores(0)
                scores(1)
                feature_block(L, "af1", hh, hl, S, nothing)
                values(0)
                values(1)
                scores(2)
                scores(3)
                fh, fl = h_hi[:, :, S:T2], h_lo[:, :, S:T2]

                def fourier_ready(i):
                    wait_taken(pe, grp(L, "F2", i))
                feature_block(L, "wf0", fh, fl, S, fourier_ready)
                values(2)
                values(3)
                feature_block(L, "wf1", fh, fl, S, nothing)
                head_means(0)
                head_means(1)
                feature_block(L, "g0", hh, hl, S, nothing)
                head_vars(0)
                head_vars(1)
                for name in ("g1", "ar0", "ar1"):
                    feature_block(L, name, hh, hl, S, nothing)
                feature_block(L, "wr0", r_hi, r_lo, S, lambda i: pe.wait_ge(s["r_ready"], 2 * L + i // 2 + 1))
                feature_block(L, "wr1", r_hi, r_lo, S, nothing)
                feature_block(L, "wo0", hh, hl, S, lambda i: pe.wait_ge(s["mm_ready"], 2 * L + i // 2 + 1))
                feature_block(L, "wo1", hh, hl, S, nothing, before_last=lambda: norm_sums(L, "n2", S, EARLY))
                norm_sums(L, "n2", S, LATE)
                feature_block(L, "up0", hh, hl, S, h_ready(L, "n2"))
                for b in range(1, FC // 2):
                    feature_block(L, f"up{b}", hh, hl, S, nothing)
                feature_block(L, "dn0", u_hi, u_lo, S, lambda i: pe.wait_ge(s["uu_ready"], L * (FC // 2) + i + 1))
                following = (1, "n1") if L == 0 else (1, "nf")
                feature_block(L, "dn1", u_hi, u_lo, S, nothing, before_last=lambda: norm_sums(*following, S, EARLY))
                if L == 1:
                    norm_sums(1, "nf", S, LATE)

            for L in (2, 3):
                with_ctx = L == 2
                T = T2 if with_ctx else S
                norm_sums(L, "n1", T2, range(DC) if L == 2 else LATE)
                feature_block(L, "pu", h_hi, h_lo, T, h_ready(L, "n1"))
                token_block(L, "vs", h_hi, h_lo, nothing, width=2 * P)
                feature_block(L, "q", h_hi, h_lo, T, nothing)
                feature_block(L, "k", h_hi, h_lo, T2, nothing)
                if L == 2:
                    pe.wait_ge(s["loaded2"], 64)
                for name, src, blk in (("rq", q2, "q"), ("rk", k2, "k")):
                    for cc in range(2):
                        g = grp(L, f"{name}{cc}")
                        out = open_group(g)
                        for i in range(2):
                            wait_taken(pe, grp(L, blk, 2 * cc + i))
                            last = mm(out[:, i * S:(i + 1) * S], rotm[:, :], src[:, 2 * cc + i, 0:S], start=True, stop=True)
                        close_group(last, g)
                def pool_and_mix():
                    pe.wait_ge(s["small2"], 48 * (L - 1))
                    pe.wait_ge(s["pooled_ready"], L - 1)
                    for c in range(2):
                        g = grp(L, "pool", c)
                        out = open_group(g)[:, 0:T]
                        close_group(mm(out, wpool[:, c, :], pooled[:, c, 0:T], start=True, stop=True), g)
                    for fc in range(2):
                        g = grp(L, "mix", fc)
                        out = open_group(g)
                        for tk in range(T // P):
                            wait_taken(pe, grp(L, "vs", tk))
                            for e in range(2):
                                hd = 2 * fc + e
                                o = out[64 * e:64 * e + 64, tk * P:(tk + 1) * P]
                                mm(o, vn[:, tk, hd * 64:(hd + 1) * 64], wsgu[:, hd, :], start=True, stop=False)
                                last = mm(o, ones[0:1, 0:64], sgub[0:1, hd * P:(hd + 1) * P], start=False, stop=True)
                        close_group(last, g)

                def scores2(h):
                    rows = slice(64 * (h % 2), 64 * (h % 2) + 64)
                    if h == 0:
                        pe.wait_ge(s["q2_rot"], 4 * (L - 1))
                        for n in range(4):
                            wait_taken(pe, grp(L, "q", n))
                            wait_taken(pe, grp(L, "k", n))
                    for qt, tag in enumerate("ab"):
                        g = grp(L, f"X{h}{tag}")
                        out = open_group(g)
                        close_group(mm(out[:, :], q2[rows, h // 2, qt * P:(qt + 1) * P], k2[rows, h // 2, :],
                                       start=True, stop=True), g)
                    if with_ctx:
                        g = grp(L, f"C{h}")
                        out = open_group(g)
                        for qt in range(2):
                            last = mm(out[:, qt * S:(qt + 1) * S], q2[rows, h // 2, S + qt * P:S + (qt + 1) * P],
                                      k2[rows, h // 2, S:T2], start=True, stop=True)
                        close_group(last, g)

                def transposes(h):
                    for qt, tag in enumerate("ab"):
                        g = grp(L, f"T{h}{tag}")
                        out = open_group(g)
                        pe.wait_ge(s["p_ready"], PREADY[L] + PPER[L] * h + qt + 1)
                        for kc in range(4):
                            last = nc.tensor.transpose(out[:, kc * P:(kc + 1) * P], sc[:, qt, kc * P:(kc + 1) * P], ident[:, :])
                        close_group(last, g)
                    if with_ctx:
                        g = grp(L, f"U{h}")
                        out = open_group(g)
                        pe.wait_ge(s["p_ready"], PREADY[L] + PPER[L] * h + 3)
                        for qt in range(2):
                            for kc in range(2):
                                last = nc.tensor.transpose(out[:, kc * S + qt * P:kc * S + (qt + 1) * P],
                                                           scc[:, qt, kc * P:(kc + 1) * P], ident[:, :])
                        close_group(last, g)

                def attend(h):
                    g = grp(L, f"O{h}")
                    bank = open_group(g)
                    rows = slice(64 * (h % 2), 64 * (h % 2) + 64)
                    if h == 0:
                        for n in range(4):
                            wait_taken(pe, grp(L, "v", n))
                    wait_taken(pe, grp(L, f"T{h}a"))
                    wait_taken(pe, grp(L, f"T{h}b"))
                    for kc in range(4):
                        last = mm(bank[rows, 0:S], v2[:, kc, h * DK2:(h + 1) * DK2], pT[:, kc, :],
                                  start=kc == 0, stop=kc == 3)
                    if with_ctx:
                        wait_taken(pe, grp(L, f"U{h}"))
                        for kc in range(2):
                            last = mm(bank[rows, S:T2], v2[:, 2 + kc, h * DK2:(h + 1) * DK2], pTc[:, kc, :],
                                      start=kc == 0, stop=kc == 1)
                    close_group(last, g)

                def run(name):
                    if name == "v":
                        token_block(L, "v", h_hi, h_lo, nothing)
                        pool_and_mix()
                    elif name[0] == "g":
                        feature_block(L, name, h_hi, h_lo, T, nothing)
                    elif name[0] == "p":
                        def pool_ready(i):
                            for c in range(2):
                                wait_taken(pe, grp(L, "pool", c))
                        feature_block(L, name, b_hi, b_lo, T, pool_ready)
                    else:
                        feature_block(L, name, b_hi, b_lo, T, lambda i: pe.wait_ge(s["b_ready"], 2 * (L - 1)), k0=2)

                for h in range(HEADS2):
                    scores2(h)
                    if h:
                        attend(h - 1)
                    for name in ATTENTION_FILL[h]:
                        run(name)
                    transposes(h)
                attend(HEADS2 - 1)
                feature_block(L, "ao0", b_hi, b_lo, T, lambda i: pe.wait_ge(s["a_ready"], 4 * (L - 2) + 2 * i + 2))
                feature_block(L, "ao1", b_hi, b_lo, T, nothing)
                feature_block(L, "wo0", h_hi, h_lo, T, lambda i: pe.wait_ge(s["mm_ready"], 4 + DC * (L - 2) + 2 * i + 2))
                feature_block(L, "wo1", h_hi, h_lo, T, nothing, before_last=lambda: norm_sums(L, "n2", T, EARLY))
                norm_sums(L, "n2", T, LATE)
                for half in range(2):
                    for b in range(4 * half, 4 * half + 4):
                        feature_block(L, f"f{b}", h_hi, h_lo, T, h_ready(L, "n2") if b == 0 else nothing)
                    base = 32 * (L - 2) + 16 * half
                    feature_block(L, f"d{half}0", f_hi, f_lo, T, count("ff_ready", base))
                    following = (3, "n1", T2) if L == 2 else (3, "nf", S)
                    feature_block(L, f"d{half}1", f_hi, f_lo, T, nothing,
                                  before_last=(lambda: norm_sums(*following, EARLY)) if half else None)
                if L == 3:
                    norm_sums(3, "nf", S, LATE)

        @block.scalar
        def _(act):
            A = nc.scalar.activation
            split = [0]
            used = [0]

            def make_hi(m):
                n = PLAN.index[m]
                act.wait_ge(arrived[n % NS], 16 * (n // NS + 1))
                if m >= NR:
                    kind, v = PLAN.free_at[m - NR]
                    if kind == "used":
                        act.wait_ge(units_used, v)
                    else:
                        wait_filled(act, v)
                A(w_hi[:, m % NR, :], stage[:, n % NS, :], ACT.Copy).then_inc(hi_ready, 1)

            def advance(n):
                for _ in range(n):
                    used[0] += 1
                    while split[0] < min(used[0] + NR, PLAN.units):
                        make_hi(split[0])
                        split[0] += 1

            def block_of(layer, name):
                advance(PLAN.step[layer, name][1])
                return PLAN.step[layer, name][2]

            def each(layer, name, do):
                g0 = block_of(layer, name)
                for n in range(PLAN.step[layer, name][3]):
                    wait_filled(act, g0 + n)
                    do(n, bank_of(g0 + n)).then_inc(taken[(g0 + n) % 8], 1)

            def squares(layer, name, T, ready, chunks):
                nth = NORMS.index((layer, name))
                if 0 in chunks:
                    A(idle[0:1, nth:nth + 1], ones[0:1, 0:1], ACT.Sqrt).then_inc(s["idle"], 1)
                for c in chunks:
                    ready(c)
                    if c >= 4:
                        act.wait_ge(s["sq_used"], nth * (DC - 1) + c - 3)
                    elif nth:
                        wait_filled(act, grp(*NORMS[nth - 1]))
                    A(sq[:, c % 4, 0:T], X[:, c, 0:T], ACT.Square).then_inc(s["sq_ready"], 1)

            def norm(layer, name, T, ready, n=0):
                if n:
                    advance(n - 1)
                squares(layer, name, T, ready, range(DC))
                if n:
                    advance(1)
                wait_taken(act, grp(layer, name))
                A(rstd[:, 0:T], var[:, 0:T], ACT.Sqrt).then_inc(s["rstd_ready"], 1)
                if (layer, name) == (0, "n1"):
                    for m in range(NR):
                        make_hi(m)
                    split[0] = NR
                if name == "nf":
                    return
                base = HREADY[layer, name]
                shift = 0 if name == "n1" else 3 * DC
                for c in range(DC):
                    act.wait_ge(s["t_ready"], base + c + 1)
                    for v, tok in halves(T):
                        ins = A(h_hi[:, c, tok], tt[:, c % 4, tok], ACT.Identity,
                                bias=MOD[:, layer % 2, v, shift + c:shift + c + 1])
                    ins.then_inc(s["hhi_ready"], 1)

            act.wait_ge(s["const_ready"], 4)
            act.wait_ge(s["loaded"], 16)
            A(csil[:, :], col("c", 0, 3 * DC), ACT.Silu).then_inc(s["csil_ready"], 1)
            act.wait_ge(s["x_loaded"], 16)
            for L in range(2):
                def x_ready(c, L=L):
                    if L:
                        wait_taken(act, grp(L - 1, f"dn{c // 4}", c % 4))
                norm(L, "n1", S, x_ready, n=FC // 2 if L else 0)
                for nb in range(2):
                    each(L, f"uf{nb}", lambda n, b: A(uf[:, 4 * nb + n, :], b[:, 0:S], ACT.Copy))
                for nb in range(2):
                    each(L, f"q{nb}", lambda n, b: A(q1[:, 4 * nb + n, :], b[:, 0:S], ACT.Copy))
                each(L, "F1", lambda n, b: A(AB[:, :, n, :], b[:, :].rearrange("p (s c) -> p s c", s=2), ACT.Copy))
                for nb in range(2):
                    each(L, f"k{nb}", lambda n, b: A(k1[:, 4 * nb + n, :], b[:, 0:S], ACT.Copy))
                for cc in range(DC // 2):
                    g = grp(L, "F2", cc)
                    wait_filled(act, g)
                    A(h_hi[:, 2 * cc:2 * cc + 2, S:T2], bank_of(g)[:, :].rearrange("p (c t) -> p c t", c=2),
                      ACT.Copy).then_inc(s["fhi_ready"], 1)
                for nb in range(2):
                    each(L, f"v{nb}", lambda n, b: A(v1[:, n, nb * COLS:(nb + 1) * COLS], b[:, :], ACT.Copy))
                each(L, "af0", lambda n, b: A(y1[:, n, :], b[:, 0:S], ACT.Sigmoid))
                each(L, "af1", lambda n, b: A(y1[:, 4 + n, :], b[:, 0:S], ACT.Sigmoid))

                def head_out(h):
                    g = grp(L, f"V{h}")
                    wait_filled(act, g)
                    A(q1[:, 2 * h:2 * h + 2, :], bank_of(g)[:, :].rearrange("p (c t) -> p c t", c=2),
                      ACT.Copy).then_inc(taken[g % 8], 1)
                head_out(0)
                head_out(1)
                advance(4)
                head_out(2)
                head_out(3)
                advance(4)
                for hp in range(2):
                    wait_taken(act, grp(L, f"M{hp}"))
                    A(sq2[:, hp, :, :], q1[:, 4 * hp:4 * hp + 4, :], ACT.Square).then_inc(s["sq2_ready"], 1)

                def gate_sigmoid(nb):
                    g0 = block_of(L, f"g{nb}")
                    for n in range(4):
                        wait_filled(act, g0 + n)
                        A(g1[:, 4 * nb + n, :], bank_of(g0 + n)[:, 0:S], ACT.Sigmoid).then_inc(s["g_sig"], 1)
                gate_sigmoid(0)
                for hp in range(2):
                    wait_taken(act, grp(L, f"R{hp}"))
                    A(rstd2[:, hp, :, :], var2[:, hp, :, :], ACT.Sqrt).then_inc(s["rstd2_ready"], 1)
                gate_sigmoid(1)
                for hp in range(2):
                    act.wait_ge(s["yn_ready"], 2 * L + hp + 1)
                    A(r_hi[:, 4 * hp:4 * hp + 4, :], q1[:, 4 * hp:4 * hp + 4, :], ACT.Copy).then_inc(s["rhi_ready"], 1)
                each(L, "ar0", lambda n, b: A(k1[:, n, :], b[:, 0:S], ACT.Sigmoid))
                each(L, "ar1", lambda n, b: A(k1[:, 4 + n, :], b[:, 0:S], ACT.Sigmoid))
                for nb in range(2):
                    advance(4)
                    act.wait_ge(s["m_ready"], 2 * L + nb + 1)
                    A(h_hi[:, 4 * nb:4 * nb + 4, 0:S], y1[:, 4 * nb:4 * nb + 4, :], ACT.Copy).then_inc(s["mhi_ready"], 1)
                norm(L, "n2", S, lambda c: wait_taken(act, grp(L, f"wo{c // 4}", c % 4)), n=8)
                for b in range(FC // 2):
                    g0 = block_of(L, f"up{b}")
                    it = L * (FC // 2) + b
                    for n in range(4):
                        ch = 2 * b + n if n < 2 else FC + 2 * b + n - 2
                        wait_filled(act, g0 + n)
                        if n == 0 and b >= 2:
                            act.wait_ge(s["uu_ready"], it - 1)
                        A(conv[:, b % 2, n, :], bank_of(g0 + n)[:, 0:S], ACT.Identity,
                          bias=col(f"convb_{L}", ch), scale=col(f"convw_{L}", 2 * FC + ch)).then_inc(s["lin_ready"], 1)
                    wait_taken(act, g0 + 1)
                    A(conv[:, b % 2, 0:2, :], conv[:, b % 2, 0:2, :], ACT.Gelu).then_inc(s["gelu_ready"], 1)
                    act.wait_ge(s["u_ready"], it + 1)
                    A(u_hi[:, 2 * b:2 * b + 2, :], conv[:, b % 2, 2:4, :], ACT.Copy).then_inc(s["uhi_ready"], 1)
                advance(FC // 2)
                if L == 1:
                    norm(1, "nf", S, lambda c: wait_taken(act, grp(1, f"dn{c // 4}", c % 4)), n=FC // 2)

            for L in (2, 3):
                with_ctx = L == 2
                T = T2 if with_ctx else S

                def x_ready(c, L=L):
                    if L == 2:
                        act.wait_ge(s["xf_ready"], c + 1)
                    else:
                        wait_taken(act, grp(2, f"d1{c // 4}", c % 4))
                norm(L, "n1", T2, x_ready, n=8 if L == 3 else 0)
                g0 = block_of(L, "pu")
                for n in range(4):
                    wait_filled(act, g0 + n)
                    if n < 2:
                        act.wait_ge(s["pad_ready"], L - 1)
                        ins = A(pp[:, n, 0:T // S, 8:8 + S], bank_of(g0 + n)[:, 0:T].rearrange("p (s t) -> p s t", t=S), ACT.Copy)
                    else:
                        ins = A(u2[:, n - 2, 0:T], bank_of(g0 + n)[:, 0:T], ACT.Copy)
                    ins.then_inc(taken[(g0 + n) % 8], 1)
                advance(2)
                for tk in range(T // P):
                    nth = (0 if L == 2 else 4) + tk + 1
                    act.wait_ge(s["vvar_ready"], nth)
                    A(stats[:, tk, 10:11], stats[:, tk, 9:10], ACT.Sqrt).then_inc(s["vstd_ready"], 1)
                each(L, "q", lambda n, b: A(q2[:, n, 0:T], b[:, 0:T], ACT.Copy, scale=DK2 ** -0.5))
                each(L, "k", lambda n, b: A(k2[:, n, :], b[:, :], ACT.Copy))

                def values_and_branches():
                    each(L, "v", lambda n, b: A(v2[:, n, :], b[:, :], ACT.Copy))
                    for c in range(2):
                        g = grp(L, "pool", c)
                        wait_filled(act, g)
                        A(b_hi[:, c, 0:T], bank_of(g)[:, 0:T], ACT.Copy, scale=col(f"pscale_{L}", c)).then_inc(s["phi_ready"], 1)
                    for fc in range(2):
                        wait_taken(act, grp(L, "mix", fc))
                        A(b_hi[:, 2 + fc, 0:T], u2[:, fc, 0:T], ACT.Copy).then_inc(s["sohi_ready"], 1)

                per = PPER[L]

                def softmax(h):
                    for qt, tag in enumerate("ab"):
                        g = grp(L, f"X{h}{tag}")
                        wait_filled(act, g)
                        if h:
                            wait_filled(act, grp(L, f"T{h - 1}{tag}"))
                        A(sc[:, qt, S:T2], bank_of(g)[:, S:T2], ACT.Copy).then_inc(s["ctx_copied"], 1)
                    if with_ctx:
                        g = grp(L, f"C{h}")
                        wait_filled(act, g)
                    for i in range(per):
                        at = PREADY[L] + per * h + i + 1
                        act.wait_ge(s["nmax_ready"], at)
                        if i < 2:
                            A(sc[:, i, :], sc[:, i, :], ACT.Exp, bias=small[:, 0, i:i + 1],
                              accum_out=small[:, 1, i:i + 1]).then_inc(s["exp_ready"], 1)
                        else:
                            g = grp(L, f"C{h}")
                            if h:
                                wait_filled(act, grp(L, f"U{h - 1}"))
                            for qt in range(2):
                                ins = A(scc[:, qt, :], bank_of(g)[:, qt * S:(qt + 1) * S], ACT.Exp,
                                        bias=small[:, 0, 2 + qt:3 + qt], accum_out=small[:, 1, 2 + qt:3 + qt])
                                if qt == 0:
                                    ins.then_inc(s["exp_ready"], 1)
                            ins.then_inc(taken[g % 8], 1)

                def take_transposed(h):
                    if h:
                        wait_filled(act, grp(L, f"O{h - 1}"))
                    for qt, tag in enumerate("ab"):
                        g = grp(L, f"T{h}{tag}")
                        wait_filled(act, g)
                        A(pT[:, :, qt * P:(qt + 1) * P], bank_of(g)[:, :].rearrange("p (k q) -> p k q", k=4),
                          ACT.Copy).then_inc(taken[g % 8], 1)
                    if with_ctx:
                        g = grp(L, f"U{h}")
                        wait_filled(act, g)
                        A(pTc[:, :, :], bank_of(g)[:, :].rearrange("p (k q) -> p k q", k=2),
                          ACT.Copy).then_inc(taken[g % 8], 1)

                def take_out(h):
                    g = grp(L, f"O{h}")
                    wait_filled(act, g)
                    rows = slice(64 * (h % 2), 64 * (h % 2) + 64)
                    A(q2[rows, h // 2, 0:T], bank_of(g)[rows, 0:T], ACT.Copy).then_inc(taken[g % 8], 1)

                def gate_block(name):
                    g0 = block_of(L, name)
                    before = {"gs0": "po0", "gp1": "so0", "gs1": "po1", "ga0": "so1"}.get(name)
                    if name == "gp0":
                        act.wait_ge(s["b_ready"], 2 * (L - 1))
                    dst = gtb if name == "ga1" else gt
                    for n in range(4):
                        wait_filled(act, g0 + n)
                        if before:
                            wait_taken(act, grp(L, before, n))
                        A(dst[:, n, 0:T], bank_of(g0 + n)[:, 0:T], ACT.Sigmoid).then_inc(taken[(g0 + n) % 8], 1)

                for h in range(HEADS2):
                    softmax(h)
                    if h:
                        take_out(h - 1)
                    for name in ATTENTION_FILL[h]:
                        if name == "v":
                            values_and_branches()
                        elif name[0] == "g":
                            gate_block(name)
                        else:
                            advance(1)
                    take_transposed(h)
                take_out(HEADS2 - 1)
                for c in range(4):
                    if c == 0:
                        wait_filled(act, grp(L, "so1", 3))
                    wait_taken(act, grp(L, f"O{2 * c + 1}"))
                    A(b_hi[:, c, 0:T], q2[:, c, 0:T], ACT.Copy).then_inc(s["aohi_ready"], 1)
                advance(4)
                for c in range(DC):
                    act.wait_ge(s["y_added"], 16 * (L - 2) + 8 + c + 1)
                    A(h_hi[:, c, 0:T], y2[:, c, 0:T], ACT.Copy, scale=1.0).then_inc(s["mhi_ready"], 1)
                norm(L, "n2", T, lambda c: wait_taken(act, grp(L, f"wo{c // 4}", c % 4)), n=8)
                for half in range(2):
                    for b in range(4 * half, 4 * half + 4):
                        g0 = block_of(L, f"f{b}")
                        for n in range(4):
                            i = 32 * (L - 2) + 4 * b + n
                            wait_filled(act, g0 + n)
                            if i >= 4:
                                act.wait_ge(s["ff_ready"], i - 3)
                            A(relu[:, n, 0:T], bank_of(g0 + n)[:, 0:T], ACT.Relu).then_inc(taken[(g0 + n) % 8], 1)
                        for n in range(4):
                            i = 32 * (L - 2) + 4 * b + n
                            act.wait_ge(s["fhid_ready"], i + 1)
                            A(f_hi[:, (4 * b + n) % 16, 0:T], relu[:, n, 0:T], ACT.Copy).then_inc(s["fhihi_ready"], 1)
                    advance(8 if half else 16)
                if L == 3:
                    norm(3, "nf", S, lambda c: wait_taken(act, grp(3, f"d1{c // 4}", c % 4)), n=8)

        @block.vector
        def _(dve):
            V = nc.vector
            steps = sem("dve_steps")
            count = [0]
            last = [None]

            def do(ins, sm=None, value=None):
                if sm is None:
                    count[0] += 1
                    ins.then_inc(steps, 1)
                    last[0] = (steps, count[0])
                else:
                    ins.then_inc(sm, 1)
                    last[0] = (sm, value)

            def settle():
                dve.wait_ge(*last[0])

            def take(ins, g):
                do(ins, taken[g % 8], g // 8 + 1)

            done = [0]
            used = [0]

            def stream_unit():
                n = done[0]
                kind, *at = PLAN.stream[n]
                if kind == "weights":
                    m = STREAM_UNIT[n]
                    dve.wait_ge(hi_ready, m + 1)
                    do(V.tensor_tensor(w_lo[:, m % NR, :], stage[:, n % NS, :], w_hi[:, m % NR, :].bitcast(F32),
                                       ALU.subtract), unit_done, n + 1)
                else:
                    layer, j, i = at
                    dve.wait_ge(arrived[n % NS], 16 * (n // NS + 1))
                    vecs = mod_vectors(layer, j)
                    for k in range(KC):
                        for v, vec in enumerate(vecs):
                            w = stage[:, n % NS, k * COLS:(k + 1) * COLS]
                            cc = csil[:, vec * DC + KC * i + k:vec * DC + KC * i + k + 1]
                            if k == 0 or v == 0:
                                settle()
                            row = PLAN.rows[layer, j] + v
                            if i == 0 and k == 0:
                                ins = V.tensor_scalar(acc[:, row, :], w, cc, None, ALU.mult)
                            else:
                                ins = V.scalar_tensor_tensor(acc[:, row, :], w, cc, acc[:, row, :], ALU.mult, ALU.add)
                            if k == KC - 1 and v == len(vecs) - 1:
                                do(ins, unit_done, n + 1)
                            else:
                                do(ins)
                done[0] += 1

            def take_mod(g, target, j):
                vecs = len(mod_vectors(target, j))
                wait_filled(dve, g)
                for v in range(vecs):
                    ins = V.tensor_tensor(MOD[:, target % 2, v, 4 * j:4 * j + 4], bank_of(g)[:, 4 * v:4 * v + 4],
                                          col(f"bmod_{target}", 4 * j, 4), ALU.add)
                    if v == vecs - 1:
                        take(ins, g)
                    else:
                        do(ins)
                if j in (2, 3, 8, 9):
                    which, c = (0, 4 * j - 8) if j < 4 else (1, 4 * j - 32)
                    settle()
                    for v in range(vecs):
                        do(V.scalar_tensor_tensor(MUL[:, target % 2, v, which, c:c + 4], MOD[:, target % 2, v, 4 * j:4 * j + 4],
                                                  1.0, col(f"n{which + 1}_{target}", c, 4), ALU.add, ALU.mult))

            def advance(n):
                for _ in range(n):
                    used[0] += 1
                    if used[0] + NR <= PLAN.units:
                        while done[0] <= PLAN.index[used[0] + NR - 1]:
                            stream_unit()

            def block_of(layer, name):
                for i in range(PLAN.step[layer, name][1]):
                    unit_of_block(layer, name, i)
                return PLAN.step[layer, name][2]

            def unit_of_block(layer, name, i):
                advance(1)
                if (layer, name, i) in PLAN.mods:
                    take_mod(grp(layer, name, at=i), *PLAN.mods[layer, name, i])

            def invert(layer, name, T):
                g = grp(layer, name)
                wait_filled(dve, g)
                settle()
                take(V.reciprocal(var[:, 0:T], bank_of(g)[:, 0:T]), g)

            def norm(layer, name, T, behind=None):
                nth = NORMS.index((layer, name))
                if (layer, name) != (0, "n1"):
                    invert(layer, name, T)
                dve.wait_ge(s["rstd_ready"], nth + 1)
                settle()
                if name == "nf":
                    last_norm = layer == 3
                    for c in range(DC):
                        do(V.scalar_tensor_tensor(X[:, c, 0:S], X[:, c, 0:S], col("final2" if last_norm else "final1", c),
                                                  rstd[:, 0:S], ALU.mult, ALU.mult),
                           s["out_ready" if last_norm else "xf_ready"], c + 1)
                    if behind:
                        unit_of_block(*behind)
                    return
                which = 0 if name == "n1" else 1
                base = HREADY[layer, name]
                par = layer % 2

                def scaled(c):
                    if c >= 4:
                        dve.wait_ge(s["h_ready"], base + c - 3)
                    for v, tok in halves(T):
                        ins = V.scalar_tensor_tensor(tt[:, c % 4, tok], X[:, c, tok], MUL[:, par, v, which, c:c + 1],
                                                     rstd[:, tok], ALU.mult, ALU.mult)
                        if T == T2 and v == 0:
                            do(ins)
                        else:
                            do(ins, s["t_ready"], base + c + 1)

                def rest(c):
                    dve.wait_ge(s["hhi_ready"], base + c + 1)
                    for v, tok in halves(T):
                        ins = V.scalar_tensor_tensor(h_lo[:, c, tok], tt[:, c % 4, tok],
                                                     MOD[:, par, v, 3 * DC * which + c:3 * DC * which + c + 1],
                                                     h_hi[:, c, tok].bitcast(F32), ALU.add, ALU.subtract)
                        if T == T2 and v == 0:
                            do(ins)
                        else:
                            do(ins, s["h_ready"], base + c + 1)
                scaled(0)
                scaled(1)
                for c in range(2, DC):
                    if (layer, name) == (0, "n1") and c % 2 == 0:
                        while done[0] <= PLAN.index[c // 2 - 1]:
                            stream_unit()
                    scaled(c)
                    rest(c - 2)
                rest(DC - 2)
                rest(DC - 1)
                if (layer, name) == (0, "n1"):
                    while done[0] <= PLAN.index[NR - 1]:
                        stream_unit()
                if behind:
                    unit_of_block(*behind)

            def residual(layer, name, nb, gate, T):
                g0 = PLAN.step[layer, name][2]
                nu = PLAN.step[layer, name][1]
                for i in range(nu - 1 if name in ("wo1", "dn1", "d11") else nu):
                    unit_of_block(layer, name, i)
                for n in range(4):
                    c = 4 * nb + n
                    wait_filled(dve, g0 + n)
                    if n == 0:
                        settle()
                    if T == T2:
                        do(V.scalar_tensor_tensor(X[:, c, S:T2], bank_of(g0 + n)[:, S:T2], MOD[:, layer % 2, 1, gate * DC + c:gate * DC + c + 1],
                                                  X[:, c, S:T2], ALU.mult, ALU.add))
                    take(V.scalar_tensor_tensor(X[:, c, 0:S], bank_of(g0 + n)[:, 0:S], MOD[:, layer % 2, 0, gate * DC + c:gate * DC + c + 1],
                                                X[:, c, 0:S], ALU.mult, ALU.add), g0 + n)

            do(V.memset(mean_D[:, :], 1.0 / D), s["const_ready"], 1)
            do(V.memset(mean_H[:, :], 1.0 / DK1), s["const_ready"], 2)
            do(V.memset(ones[:, :], 1.0), s["const_ready"], 3)
            do(V.memset(eps[:, :], EPS), s["const_ready"], 4)
            dve.wait_ge(s["loaded"], 16)
            dve.wait_ge(s["csil_ready"], 1)
            for j in range(4):
                for _ in range(4):
                    stream_unit()
                if j:
                    take_mod(grp("pro", j - 1), 0, j - 1)
                if j == 2:
                    invert(0, "n1", S)
            take_mod(grp("pro", 3), 0, 3)

            for L in range(2):
                norm(L, "n1", S, behind=(0, "dn1", FC // 2 - 1) if L else None)
                for name in ("uf0", "uf1", "q0", "q1", "k0", "k1"):
                    block_of(L, name)
                for cc in range(DC // 2):
                    g = grp(L, "F2", cc)
                    dve.wait_ge(s["fhi_ready"], 4 * L + cc + 1)
                    take(V.tensor_tensor(h_lo[:, 2 * cc:2 * cc + 2, S:T2], bank_of(g)[:, :].rearrange("p (c t) -> p c t", c=2),
                                         h_hi[:, 2 * cc:2 * cc + 2, S:T2].bitcast(F32), ALU.subtract), g)
                for name in ("v0", "v1", "af0"):
                    block_of(L, name)

                def decayed(h):
                    g = grp(L, f"S{h}")
                    wait_filled(dve, g)
                    if h >= 2:
                        wait_filled(dve, grp(L, f"V{h - 2}"))
                    if h == 0 and L == 0:
                        dve.wait_ge(s["loaded1"], 64)
                    take(V.tensor_tensor(probs1[:, h % 2, :, :], bank_of(g)[:, :].rearrange("p (j t) -> p j t", j=2),
                                         decay[:, h, :, :], ALU.mult), g)
                decayed(0)
                decayed(1)
                block_of(L, "af1")
                decayed(2)
                decayed(3)

                def gated_fourier(nb):
                    g0 = block_of(L, f"wf{nb}")
                    for n in range(4):
                        wait_filled(dve, g0 + n)
                        wait_taken(dve, grp(L, f"af{nb}", n))
                        take(V.tensor_tensor(y1[:, 4 * nb + n, :], bank_of(g0 + n)[:, 0:S], y1[:, 4 * nb + n, :], ALU.mult), g0 + n)
                gated_fourier(0)
                gated_fourier(1)
                for hp in range(2):
                    g = grp(L, f"M{hp}")
                    wait_filled(dve, g)
                    for i in range(2):
                        qh = q1[:, 4 * hp + 2 * i:4 * hp + 2 * i + 2, :]
                        mu = bank_of(g)[:, i * S:(i + 1) * S].rearrange("p (a t) -> p a t", a=1).to_broadcast([P, 2, S])
                        ins = V.tensor_tensor(qh, qh, mu, ALU.subtract)
                        if i == 0:
                            do(ins)
                        else:
                            take(ins, g)
                def silu_gate(nb):
                    g0 = block_of(L, f"g{nb}")
                    for n in range(4):
                        dve.wait_ge(s["g_sig"], DC * L + 4 * nb + n + 1)
                        take(V.tensor_tensor(g1[:, 4 * nb + n, :], bank_of(g0 + n)[:, 0:S], g1[:, 4 * nb + n, :], ALU.mult), g0 + n)

                silu_gate(0)
                for hp in range(2):
                    g = grp(L, f"R{hp}")
                    wait_filled(dve, g)
                    take(V.reciprocal(var2[:, hp, :, :], bank_of(g)[:, :].rearrange("p (i t) -> p i t", i=2)), g)
                silu_gate(1)
                for name in ("ar0", "ar1"):
                    block_of(L, name)
                for nb in range(2):
                    g0 = block_of(L, f"wr{nb}")
                    y = y1[:, 4 * nb:4 * nb + 4, :]
                    a = k1[:, 4 * nb:4 * nb + 4, :]
                    for n in range(4):
                        wait_filled(dve, g0 + n)
                        wait_taken(dve, grp(L, f"ar{nb}", n))
                        take(V.tensor_tensor(k1[:, 4 * nb + n, :], bank_of(g0 + n)[:, 0:S], k1[:, 4 * nb + n, :], ALU.mult), g0 + n)
                    settle()
                    do(V.tensor_tensor(y, y, a, ALU.add), s["m_ready"], 2 * L + nb + 1)
                    dve.wait_ge(s["mhi_ready"], 2 * L + nb + 1)
                    settle()
                    do(V.tensor_tensor(h_lo[:, 4 * nb:4 * nb + 4, 0:S], y, h_hi[:, 4 * nb:4 * nb + 4, 0:S].bitcast(F32),
                                       ALU.subtract), s["mm_ready"], 2 * L + nb + 1)
                for nb in range(2):
                    residual(L, f"wo{nb}", nb, 2, S)
                norm(L, "n2", S, behind=(L, "wo1", 3))
                for b in range(FC // 2):
                    g0 = block_of(L, f"up{b}")
                    it = L * (FC // 2) + b
                    y = conv[:, b % 2, :, :]
                    for n in range(4):
                        ch = 2 * b + n if n < 2 else FC + 2 * b + n - 2
                        u = bank_of(g0 + n)
                        dve.wait_ge(s["lin_ready"], 4 * it + n + 1)
                        do(V.scalar_tensor_tensor(y[:, n, 1:S], u[:, 0:S - 1], col(f"convw_{L}", ch), y[:, n, 1:S],
                                                  ALU.mult, ALU.add))
                    settle()
                    for n in range(4):
                        ch = 2 * b + n if n < 2 else FC + 2 * b + n - 2
                        take(V.scalar_tensor_tensor(y[:, n, 0:S - 1], bank_of(g0 + n)[:, 1:S], col(f"convw_{L}", 4 * FC + ch),
                                                    y[:, n, 0:S - 1], ALU.mult, ALU.add), g0 + n)
                for nb in range(2):
                    residual(L, f"dn{nb}", nb, 5, S)
                if L == 1:
                    norm(1, "nf", S, behind=(1, "dn1", FC // 2 - 1))

            for L in (2, 3):
                with_ctx = L == 2
                T = T2 if with_ctx else S
                ns = T // S
                norm(L, "n1", T2, behind=(2, "d11", 7) if L == 3 else None)
                block_of(L, "pu")
                g0 = block_of(L, "vs")
                for tk in range(T // P):
                    nth = (0 if L == 2 else 4) + tk + 1
                    wait_filled(dve, g0 + tk)
                    if tk == 0:
                        settle()
                    do(V.bn_stats(stats[:, tk, 0:6], bank_of(g0 + tk)[:, 0:2 * P]))
                    settle()
                    do(V.bn_aggr(stats[:, tk, 6:8], stats[:, tk, 0:6]))
                    settle()
                    do(V.tensor_scalar(stats[:, tk, 8:9], stats[:, tk, 7:8], EPS, None, ALU.add))
                    settle()
                    do(V.reciprocal(stats[:, tk, 9:10], stats[:, tk, 8:9]), s["vvar_ready"], nth)
                for tk in range(T // P):
                    nth = (0 if L == 2 else 4) + tk + 1
                    dve.wait_ge(s["vstd_ready"], nth)
                    settle()
                    take(V.tensor_scalar(vn[:, tk, :], bank_of(g0 + tk)[:, 0:2 * P], stats[:, tk, 6:7], stats[:, tk, 10:11],
                                         ALU.subtract, ALU.mult), g0 + tk)
                block_of(L, "q")
                block_of(L, "k")
                if L == 2:
                    dve.wait_ge(s["loaded2"], 64)
                for i, name in enumerate(("rq0", "rq1", "rk0", "rk1")):
                    g = grp(L, name)
                    wait_filled(dve, g)
                    take(V.tensor_tensor(ropeA[:, i, :, :], bank_of(g)[:, :].rearrange("p (c t) -> p c t", c=2),
                                         rope2[:, 1:2, :].to_broadcast([P, 2, S]), ALU.mult), g)

                def values_and_branches():
                    block_of(L, "v")
                    for c in range(2):
                        g = grp(L, "pool", c)
                        dve.wait_ge(s["phi_ready"], 2 * (L - 2) + c + 1)
                        take(V.scalar_tensor_tensor(b_lo[:, c, 0:T], bank_of(g)[:, 0:T], col(f"pscale_{L}", c),
                                                    b_hi[:, c, 0:T].bitcast(F32), ALU.mult, ALU.subtract), g)
                    for fc in range(2):
                        g = grp(L, "mix", fc)
                        wait_filled(dve, g)
                        take(V.tensor_tensor(u2[:, fc, 0:T], bank_of(g)[:, 0:T], u2[:, fc, 0:T], ALU.mult), g)
                    for fc in range(2):
                        dve.wait_ge(s["sohi_ready"], 2 * (L - 2) + fc + 1)
                        do(V.tensor_tensor(b_lo[:, 2 + fc, 0:T], u2[:, fc, 0:T], b_hi[:, 2 + fc, 0:T].bitcast(F32),
                                           ALU.subtract), s["b_ready"], 2 * (L - 2) + fc + 1)

                per = PPER[L]

                def maxima(h):
                    nth = HEADS2 * (L - 2) + h
                    dve.wait_ge(s[f"bias_in{nth % 2}"], 16 * (nth // 2 + 1))
                    settle()
                    for qt, tag in enumerate("ab"):
                        g = grp(L, f"X{h}{tag}")
                        dve.wait_ge(s["ctx_copied"], 2 * nth + qt + 1)
                        take(V.tensor_tensor(sc[:, qt, 0:S], bank_of(g)[:, 0:S], bias[:, nth % 2, qt, :], ALU.add), g)
                    settle()
                    for qt in range(2):
                        do(V.tensor_reduce(small[:, 0, qt:qt + 1], sc[:, qt, :], AX_X, ALU.max, negate=True),
                           s["nmax_ready"], PREADY[L] + per * h + qt + 1)
                    if with_ctx:
                        g = grp(L, f"C{h}")
                        wait_filled(dve, g)
                        do(V.tensor_reduce(small[:, 0, 2:4], bank_of(g)[:, :].rearrange("p (q k) -> p q k", q=2), AX_X,
                                           ALU.max, negate=True), s["nmax_ready"], PREADY[L] + per * h + 3)

                def normalise(h):
                    nth = HEADS2 * (L - 2) + h
                    dve.wait_ge(s["exp_ready"], PREADY[L] + per * h + per)
                    if with_ctx:
                        wait_taken(dve, grp(L, f"C{h}"))
                    settle()
                    n = 4 if with_ctx else 2
                    do(V.reciprocal(small[:, 2, 0:n], small[:, 1, 0:n]))
                    settle()
                    for qt in range(2):
                        do(V.tensor_scalar(sc[:, qt, :], sc[:, qt, :], small[:, 2, qt:qt + 1], None, ALU.mult),
                           s["p_ready"], PREADY[L] + per * h + qt + 1)
                    if with_ctx:
                        do(V.tensor_scalar(scc[:, 0, :], scc[:, 0, :], small[:, 2, 2:3], None, ALU.mult))
                        do(V.tensor_scalar(scc[:, 1, :], scc[:, 1, :], small[:, 2, 3:4], None, ALU.mult),
                           s["p_ready"], PREADY[L] + per * h + 3)

                def gated(name):
                    g0 = block_of(L, name)
                    nb = int(name[2])
                    gate = {"p": "gp", "s": "gs", "a": "ga"}[name[0]] + name[2]
                    src = gtb if gate == "ga1" else gt
                    for n in range(4):
                        wait_filled(dve, g0 + n)
                        wait_taken(dve, grp(L, gate, n))
                        if name[0] == "p":
                            dst = y2[:, 4 * nb + n, 0:T]
                        else:
                            i = 16 * (L - 2) + (8 if name[0] == "a" else 0) + 4 * nb + n
                            if i >= 2:
                                dve.wait_ge(s["y_added"], i - 1)
                            dst = gt2[:, i % 2, 0:T]
                        take(V.tensor_tensor(dst, bank_of(g0 + n)[:, 0:T], src[:, n, 0:T], ALU.mult), g0 + n)

                for h in range(HEADS2):
                    maxima(h)
                    normalise(h)
                    for name in ATTENTION_FILL[h]:
                        if name == "v":
                            values_and_branches()
                        elif name[0] == "g":
                            block_of(L, name)
                        else:
                            gated(name)
                for c in range(4):
                    dve.wait_ge(s["aohi_ready"], 4 * (L - 2) + c + 1)
                    do(V.tensor_tensor(b_lo[:, c, 0:T], q2[:, c, 0:T], b_hi[:, c, 0:T].bitcast(F32), ALU.subtract),
                       s["a_ready"], 4 * (L - 2) + c + 1)
                gated("ao0")
                gated("ao1")
                for c in range(DC):
                    i = 4 + DC * (L - 2) + c + 1
                    dve.wait_ge(s["mhi_ready"], i)
                    do(V.tensor_tensor(h_lo[:, c, 0:T], y2[:, c, 0:T], h_hi[:, c, 0:T].bitcast(F32), ALU.subtract),
                       s["mm_ready"], i)
                for nb in range(2):
                    residual(L, f"wo{nb}", nb, 2, T)
                norm(L, "n2", T, behind=(L, "wo1", 3))
                for half in range(2):
                    for b in range(4 * half, 4 * half + 4):
                        g0 = block_of(L, f"f{b}")
                        for n in range(4):
                            i = 32 * (L - 2) + 4 * b + n + 1
                            dve.wait_ge(s["fhihi_ready"], i)
                            do(V.tensor_tensor(f_lo[:, (4 * b + n) % 16, 0:T], relu[:, n, 0:T],
                                               f_hi[:, (4 * b + n) % 16, 0:T].bitcast(F32), ALU.subtract), s["ff_ready"], i)
                    for nb in range(2):
                        residual(L, f"d{half}{nb}", nb, 5, T)
                if L == 3:
                    norm(3, "nf", S, behind=(3, "d11", 7))

        @block.gpsimd
        def _(pool):
            G = nc.gpsimd
            steps = sem("pool_steps")
            count = [0]

            def do(ins):
                count[0] += 1
                ins.then_inc(steps, 1)

            def settle():
                pool.wait_ge(steps, count[0])

            for L in range(2):
                if L == 0:
                    pool.wait_ge(s["loaded1"], 64)
                sin4 = rope1[:, 1:2, :].to_broadcast([P, 4, S])
                for x, blk, tmp_, sm in ((q1, "q", rope_q, "uq_rot"), (k1, "k", rope_k, "uk_rot")):
                    for n in range(DC):
                        wait_taken(pool, grp(L, f"{blk}{n // 4}", n % 4))
                    xv = x[:, :, :].rearrange("p (h e) t -> p e h t", e=2)
                    tv = tmp_[:, :, :].rearrange("p (h e) t -> p e h t", e=2)
                    do(G.tensor_tensor(tv[:, 0], xv[:, 1], sin4, ALU.mult))
                    do(G.tensor_tensor(tv[:, 1], xv[:, 0], sin4, ALU.mult))
                    settle()
                    for half in range(2):
                        xx = x[:, 4 * half:4 * half + 4, :]
                        do(G.tensor_tensor(xx, xx, rope1[:, 0:1, :].to_broadcast([P, 4, S]), ALU.mult))
                    settle()
                    do(G.tensor_tensor(xv[:, 0], xv[:, 0], tv[:, 0], ALU.subtract))
                    G.tensor_tensor(xv[:, 1], xv[:, 1], tv[:, 1], ALU.add).then_inc(s[sm], 1)
                for hp in range(2):
                    pool.wait_ge(s["rstd2_ready"], 2 * L + hp + 1)
                    qh = q1[:, 4 * hp:4 * hp + 4, :]
                    for i in range(2):
                        qi = qh[:, 2 * i:2 * i + 2, :]
                        do(G.tensor_tensor(qi, qi, rstd2[:, hp, i:i + 1, :].to_broadcast([P, 2, S]), ALU.mult))
                    settle()
                    for n in range(4):
                        wait_taken(pool, grp(L, f"g{hp}", n))
                    G.tensor_tensor(qh, qh, g1[:, 4 * hp:4 * hp + 4, :], ALU.mult).then_inc(s["yn_ready"], 1)
                    pool.wait_ge(s["rhi_ready"], 2 * L + hp + 1)
                    G.tensor_tensor(r_lo[:, 4 * hp:4 * hp + 4, :], qh, r_hi[:, 4 * hp:4 * hp + 4, :].bitcast(F32),
                                    ALU.subtract).then_inc(s["r_ready"], 1)
                for b in range(FC // 2):
                    it = L * (FC // 2) + b
                    y = conv[:, b % 2, :, :]
                    pool.wait_ge(s["gelu_ready"], it + 1)
                    wait_taken(pool, grp(L, f"up{b}", 3))
                    G.tensor_tensor(y[:, 2:4, :], y[:, 0:2, :], y[:, 2:4, :], ALU.mult).then_inc(s["u_ready"], 1)
                    pool.wait_ge(s["uhi_ready"], it + 1)
                    G.tensor_tensor(u_lo[:, 2 * b:2 * b + 2, :], y[:, 2:4, :], u_hi[:, 2 * b:2 * b + 2, :].bitcast(F32),
                                    ALU.subtract).then_inc(s["uu_ready"], 1)

            for L in (2, 3):
                T = T2 if L == 2 else S
                ns = T // S
                wait_filled(pool, grp(1, "nf") if L == 2 else grp(3, "n1"))
                do(G.memset(ps2[:, :, :, :], 0.0))
                do(G.memset(ps4[:, :, :, :], 0.0))
                G.memset(pp[:, :, :, :], 0.0).then_inc(s["pad_ready"], 1)
                settle()
                for n in range(2):
                    wait_taken(pool, grp(L, "pu", n))
                W = S + 2 * 8
                do(G.tensor_tensor(ps2[:, :, 0:ns, 1:W], pp[:, :, 0:ns, 0:W - 1], pp[:, :, 0:ns, 1:W], ALU.add))
                settle()
                do(G.tensor_tensor(ps4[:, :, 0:ns, 1:W - 1], ps2[:, :, 0:ns, 0:W - 2], ps2[:, :, 0:ns, 2:W], ALU.add))
                pl = pooled[:, :, 0:T].rearrange("p c (s t) -> p c s t", t=S)

                def window(rows, c, src):
                    for si in range(ns):
                        do(G.tensor_tensor(pl[rows, c, si, :], src[rows, c, si, 8:8 + S], rinv[rows, c, :], ALU.mult))
                lo, up = slice(0, 64), slice(64, 128)
                if L == 2:
                    pool.wait_ge(s["loaded2"], 64)
                settle()
                window(lo, 0, ps2)
                settle()
                window(up, 0, ps4)
                settle()
                do(G.tensor_tensor(ps2[:, 1, 0:ns, 2:W - 2], ps4[:, 1, 0:ns, 0:W - 4], ps4[:, 1, 0:ns, 4:W], ALU.add))
                settle()
                window(lo, 1, ps2)
                settle()
                do(G.tensor_tensor(ps4[up, 1, 0:ns, 6:W - 6], ps2[up, 1, 0:ns, 2:W - 10], ps2[up, 1, 0:ns, 10:W - 2], ALU.add))
                settle()
                window(up, 1, ps4)
                settle()
                do(G.tensor_tensor(pl[:, 0], pl[:, 0], pp[:, 0, 0:ns, 8:8 + S], ALU.subtract))
                G.tensor_tensor(pl[:, 1], pl[:, 1], pp[:, 1, 0:ns, 8:8 + S], ALU.subtract).then_inc(s["pooled_ready"], 1)
                for i, (name, src) in enumerate((("rq0", q2), ("rq1", q2), ("rk0", k2), ("rk1", k2))):
                    x = src[:, 2 * (i % 2):2 * (i % 2) + 2, 0:S]
                    wait_taken(pool, grp(L, name))
                    do(G.tensor_tensor(x, x, rope2[:, 0:1, :].to_broadcast([P, 2, S]), ALU.mult))
                    settle()
                    G.tensor_tensor(x, x, ropeA[:, i, :, :], ALU.add).then_inc(s["q2_rot"], 1)

                def load_bias(h):
                    nth = HEADS2 * (L - 2) + h
                    if h >= 2:
                        wait_taken(pool, grp(L, f"X{h - 2}a"))
                        wait_taken(pool, grp(L, f"X{h - 2}b"))
                    pool.dma_start(bias[:, nth % 2, :, :], t["bias"][L - 2, h]).then_inc(s[f"bias_in{nth % 2}"], 16)

                def add_branch(name):
                    nb = int(name[2])
                    for n in range(4):
                        i = 16 * (L - 2) + (8 if name[0] == "a" else 0) + 4 * nb + n
                        c = 4 * nb + n
                        wait_taken(pool, grp(L, name, n))
                        if i:
                            pool.wait_ge(s["y_added"], i)
                        G.tensor_tensor(y2[:, c, 0:T], y2[:, c, 0:T], gt2[:, i % 2, 0:T], ALU.add).then_inc(s["y_added"], 1)

                pool.wait_ge(s["q2_rot"], 4 * (L - 1))
                load_bias(0)
                load_bias(1)
                for h in range(HEADS2):
                    if 2 <= h + 1 < HEADS2:
                        load_bias(h + 1)
                    for name in ATTENTION_FILL[h]:
                        if name[0] == "s":
                            add_branch(name)
                add_branch("ao0")
                add_branch("ao1")
                for b in range(8):
                    for n in range(4):
                        i = 32 * (L - 2) + 4 * b + n
                        wait_taken(pool, grp(L, f"f{b}", n))
                        G.tensor_tensor(relu[:, n, 0:T], relu[:, n, 0:T], relu[:, n, 0:T], ALU.mult).then_inc(s["fhid_ready"], 1)


NORMS = [(0, "n1"), (0, "n2"), (1, "n1"), (1, "n2"), (1, "nf"), (2, "n1"), (2, "n2"), (3, "n1"), (3, "n2"), (3, "nf")]
HREADY = {k: DC * i for i, k in enumerate(k for k in NORMS if k[1] != "nf")}
PPER = {2: 3, 3: 2}
PREADY = {2: 0, 3: 3 * HEADS2}
MOD_LAST, STREAM_UNIT = {}, {}
for _n, _e in enumerate(PLAN.stream):
    if _e[0] == "mod":
        MOD_LAST[_e[1], _e[2]] = _n
for _m, _n in enumerate(PLAN.index):
    STREAM_UNIT[_n] = _m


def unit_of(inputs, entry):
    if entry[0] == "mod":
        _, layer, j, i = entry
        w = inputs["ada_w"][layer] if layer < 2 else inputs["w_mod_2"][layer - 2]
        return w[256 * i:256 * i + 256, COLS * j:COLS * (j + 1)].reshape(KC, P, COLS).transpose(1, 0, 2)
    _, layer, name, i = entry
    if layer < 2:
        order = ["uf", "q", "k", "v", "g", "af", "ar"]
        if name[:-1] in order and name[-1] in "01":
            w, c = inputs["w_in"][layer], D * order.index(name[:-1]) + COLS * int(name[-1])
        elif name[:2] in ("wf", "wr", "wo"):
            w, c = inputs[{"wf": "w_fourier", "wr": "w_ret", "wo": "w_out"}[name[:2]]][layer], COLS * int(name[2:])
        elif name[:2] == "dn":
            w, c = inputs["ffn_down"][layer], COLS * int(name[2:])
        else:
            b = int(name[2:])
            w = inputs["ffn_up"][layer][256 * i:256 * i + 256]
            w = np.concatenate([w[:, 256 * b:256 * b + 256], w[:, D_FF + 256 * b:D_FF + 256 * b + 256]], axis=1)
            return w.reshape(KC, P, COLS).transpose(1, 0, 2)
        return w[256 * i:256 * i + 256, c:c + COLS].reshape(KC, P, COLS).transpose(1, 0, 2)
    l = layer - 2
    if name == "vs":
        w = inputs["w_in_2"][l][512 * i:512 * i + 512, 512:768]
        return w.reshape(4, P, 2 * P).transpose(1, 0, 2)
    first = {"pu": 0, "q": 768, "k": 1280, "v": 1792, "gp0": 2304, "gp1": 2816, "gs0": 3328, "gs1": 3840,
             "ga0": 4352, "ga1": 4864}
    if name in first:
        w, c = inputs["w_in_2"][l], first[name]
    elif name[0] == "f":
        w, c = inputs["w_ff1_2"][l], COLS * int(name[1:])
    elif name[0] == "d":
        w, c = inputs["w_ff2_2"][l][2048 * int(name[1]):2048 * (int(name[1]) + 1)], COLS * int(name[2])
    else:
        w = inputs[{"po": "w_pool_out_2", "so": "w_sgu_out_2", "ao": "w_attn_out_2", "wo": "w_o_2"}[name[:2]]][l]
        c = COLS * int(name[2])
    return w[256 * i:256 * i + 256, c:c + COLS].reshape(KC, P, COLS).transpose(1, 0, 2)


def to_columns(v):
    return np.asarray(v).reshape(-1, P).T


def shape_constants():
    f = np.float64
    inv = 10000.0 ** (-np.arange(P, dtype=f) / P)
    ang = inv[:, None] * np.arange(S, dtype=f)[None, :]
    rope1 = np.stack([np.cos(ang), np.sin(ang)], axis=1)
    j, i = np.arange(S, dtype=f)[:, None], np.arange(S, dtype=f)[None, :]
    dec = []
    for h in range(HEADS1):
        gf, gb = 1 - 2.0 ** -(5.0 + h), 1 - 2.0 ** -(5.5 + h)
        dec.append(np.where(j <= i, gf ** np.maximum(i - j, 0), gb ** np.maximum(j - i, 0)) * DK1 ** -0.5)
    decay = np.stack(dec).reshape(HEADS1, 2, P, S).transpose(2, 0, 1, 3)
    a = 2 * np.pi * np.outer(np.arange(P), np.arange(P)) / P
    dftg = np.concatenate([np.cos(a), np.sin(a)], axis=1)
    b = 2 * np.pi * (np.outer(np.arange(S), np.arange(S)) % S) / S
    dfts = (np.stack([np.cos(b), -np.sin(b)]) / np.sqrt(S * P)).reshape(2, 2, P, S).transpose(2, 0, 1, 3)
    nf = DK2 // 4
    inv2 = 10000.0 ** (-np.arange(nf, dtype=f) / nf)
    tok = np.arange(S)
    ang2 = np.concatenate([(tok // GRID_W)[:, None] * inv2, (tok % GRID_W)[:, None] * inv2], axis=1)
    ang2 = ang2[:, (np.arange(P) % DK2) // 2].T
    rope2 = np.stack([np.cos(ang2), np.sin(ang2)], axis=1)
    rot = np.zeros((P, P))
    even = np.arange(0, P, 2)
    rot[even + 1, even], rot[even, even + 1] = -1.0, 1.0
    rinv = np.zeros((P, 2, S))
    for g, w in enumerate((2, 4, 8, 16)):
        cnt = np.clip(tok + (w - w // 2), 0, S) - np.clip(tok - w // 2, 0, S)
        rinv[64 * (g % 2):64 * (g % 2) + 64, g // 2, :] = 1.0 / cnt
    out = dict(rope1=rope1, decay=decay, dftg=dftg, dfts=dfts, rope2=rope2, rotm=rot, rinv=rinv, ident=np.eye(P))
    return {k: np.ascontiguousarray(v, np.float32) for k, v in out.items()}


def bias_layout(rpb):
    tok = np.arange(S)
    row, c = tok // GRID_W, tok % GRID_W
    dr = row[None, :] - row[:, None] + NA_KH - 1
    start = np.clip(c - NA_KW // 2, 0, GRID_W - NA_KW)
    inside = (c[None, :] >= start[:, None]) & (c[None, :] < start[:, None] + NA_KW)
    dc = np.clip(c[None, :] - c[:, None] + NA_KW - 1, 0, 2 * NA_KW - 2)
    full = np.where(inside, rpb[:, :, dr, dc], np.float32(MASKED)).astype(np.float32)
    return full.reshape(2, HEADS2, 2, P, S).transpose(0, 1, 3, 2, 4)


def layouts(inputs):
    a = {k: np.asarray(v) for k, v in inputs.items()}
    stream = np.empty((len(PLAN.stream), P, UNIT), np.float32)
    for n, entry in enumerate(PLAN.stream):
        stream[n] = unit_of(a, entry).reshape(P, UNIT)
    cols = np.zeros((P, NCOL), np.float32)

    def put(name, v, at=0):
        v = to_columns(v)
        cols[:, COLUMNS[name] + at:COLUMNS[name] + at + v.shape[1]] = v

    for i, name in enumerate(("c", "c_2", "c_ctx_2")):
        put("c", a[name], i * DC)
    for layer in range(4):
        sfx, l = ("", layer) if layer < 2 else ("_2", layer - 2)
        put(f"n1_{layer}", a["norm1_g" + sfx][l])
        put(f"n2_{layer}", a["norm2_g" + sfx][l])
        put(f"bmod_{layer}", a["ada_b" if layer < 2 else "b_mod_2"][l])
        if layer < 2:
            put(f"convw_{layer}", a["conv_w"][l])
            put(f"convb_{layer}", a["conv_b"][l])
        else:
            put(f"pscale_{layer}", a["pool_scale_2"][l])
    put("final1", a["final_g"])
    put("final2", a["final_g_2"])
    both = np.concatenate([a["x"][0], a["ctx_2"][0]], axis=0)
    wpool = np.zeros((2, P, 2, P), np.float32)
    for g in range(4):
        r = slice(64 * (g % 2), 64 * (g % 2) + 64)
        wpool[:, r, g // 2, r] = a["w_pool_2"][:, g]
    out = dict(stream=stream, cols=cols,
               x=np.ascontiguousarray(both.T.reshape(DC, P, T2).transpose(1, 0, 2)),
               wpool=wpool, wsgu=np.ascontiguousarray(a["sgu_w_2"].transpose(0, 3, 1, 2)),
               sgub=np.ascontiguousarray(a["sgu_b_2"].reshape(2, 1, 4 * P)),
               bias=np.ascontiguousarray(bias_layout(a["na_rpb_2"])))
    out.update(shape_constants())
    return out


def kernel(**inputs):
    import concourse.bacc as bacc
    from concourse.bass_utils import run_bass_kernel_spmd

    nc = bacc.Bacc("TRN2", target_bir_lowering=False, num_devices=1)
    arrays = layouts(inputs)
    t = {k: nc.dram_tensor(f"in_{k}", v.shape, F32, kind="ExternalInput").ap() for k, v in arrays.items()}
    t["out"] = nc.dram_tensor("out_0", (P, DC, S), F32, kind="ExternalOutput").ap()
    program(nc, t)
    r = run_bass_kernel_spmd(nc, [{f"in_{k}": v for k, v in arrays.items()}], core_ids=[0])
    out = np.asarray(r.results[0]["out_0"])
    return np.ascontiguousarray(out.transpose(1, 0, 2).reshape(D, S).T.reshape(1, S, D))
```

```python
from contextlib import ExitStack

import numpy as np

import concourse.bass as bass
from concourse import mybir

F32 = mybir.dt.float32
F32R = mybir.dt.float32r
ALU = mybir.AluOpType
ACT = mybir.ActivationFunctionType
AX_X = mybir.AxisListType.X

P = 128
D = 1024
DC = D // P
S = 256
T2 = 2 * S
COLS = 512
KC = 2
UNIT = KC * COLS
D_FF = 2816
FC = D_FF // P
D_FF2 = 4096
EPS = 1e-6
HEADS1, DK1 = 4, 256
HEADS2, DK2 = 8, 64
GRID_W, NA_KW, NA_KH = 64, 16, 8
N_MOD = 6
MODC = N_MOD * DC
NS = 5
NR = 4
MASKED = -1.0e30


ATTENTION_FILL = [["v"], ["gp0"], ["po0", "gs0"], ["so0", "gp1"], ["po1", "gs1"], ["so1"], ["ga0"], ["ga1"]]


def layer_steps(layer):
    if layer < 2:
        s = [("n1", 0, 1)]
        s += [("uf0", 4, 4), ("uf1", 4, 4), ("q0", 4, 4), ("q1", 4, 4), ("F1", 0, 8)]
        s += [("k0", 4, 4), ("k1", 4, 4), ("F2", 0, 4), ("v0", 4, 2), ("v1", 4, 2)]
        s += [("af0", 4, 4), ("S0", 0, 1), ("S1", 0, 1), ("af1", 4, 4), ("V0", 0, 1), ("V1", 0, 1)]
        s += [("S2", 0, 1), ("S3", 0, 1), ("wf0", 4, 4), ("V2", 0, 1), ("V3", 0, 1), ("wf1", 4, 4)]
        s += [("M0", 0, 1), ("M1", 0, 1), ("g0", 4, 4), ("R0", 0, 1), ("R1", 0, 1)]
        s += [("g1", 4, 4), ("ar0", 4, 4), ("ar1", 4, 4), ("wr0", 4, 4), ("wr1", 4, 4)]
        s += [("wo0", 4, 4), ("wo1", 4, 4), ("n2", 0, 1)]
        s += [(f"up{b}", 4, 4) for b in range(FC // 2)] + [("dn0", FC // 2, 4), ("dn1", FC // 2, 4)]
        if layer == 1:
            s += [("nf", 0, 1)]
        return s
    s = [("n1", 0, 1), ("pu", 4, 4), ("vs", 4 // 2, 4 if layer == 2 else 2), ("q", 4, 4)]
    s += [("k", 4, 4), ("rq0", 0, 1), ("rq1", 0, 1), ("rk0", 0, 1), ("rk1", 0, 1), ("pool", 0, 2), ("mix", 0, 2)]
    fill = [[("v", 4, 4)]] + [
        [(n, 4 if n[0] == "g" else 1, 4) for n in names] for names in ATTENTION_FILL[1:]]
    ctx = layer == 2
    for h in range(HEADS2):
        s += [(f"X{h}a", 0, 1), (f"X{h}b", 0, 1)] + ([(f"C{h}", 0, 1)] if ctx else [])
        s += ([(f"O{h - 1}", 0, 1)] if h else []) + fill[h]
        s += [(f"T{h}a", 0, 1), (f"T{h}b", 0, 1)] + ([(f"U{h}", 0, 1)] if ctx else [])
    s += [(f"O{HEADS2 - 1}", 0, 1)]
    s += [("ao0", 2, 4), ("ao1", 2, 4), ("wo0", 4, 4), ("wo1", 4, 4), ("n2", 0, 1)]
    for half in range(2):
        s += [(f"f{b}", 4, 4) for b in range(4 * half, 4 * half + 4)]
        s += [(f"d{half}0", 8, 4), (f"d{half}1", 8, 4)]
    if layer == 3:
        s += [("nf", 0, 1)]
    return s


SCHEDULE = [
    (0, "uf1", 3, [(0, j) for j in range(4, 12)] + [(1, 0), (1, 1)]), (0, "dn0", 2, [(1, 2), (1, 3)]),
    (1, "uf1", 2, [(1, j) for j in range(4, 12)]), (1, "up1", 5, [(2, 0), (2, 1)]), (1, "dn0", 2, [(2, 2), (2, 3)]),
    (2, "q", 1, [(2, j) for j in range(4, 11)]), (2, "f1", 1, [(2, 11)] + [(3, j) for j in range(8)]),
    (3, "v", 2, [(3, 8), (3, 9), (3, 10), (3, 11)]),
]


def mod_vectors(layer, j):
    if layer < 2:
        return (0,)
    return (1, 2) if layer == 2 or j < 4 else (1,)


PRO = 16


def multiplied_by_pe(n):
    return n < PRO and n % 4 == 0


def done_value(n):
    return n + 1 - sum(multiplied_by_pe(i) for i in range(min(n + 1, PRO)))


class Plan:

    def __init__(self):
        self.step, self.stream = {}, []
        steps = [(layer,) + x for layer in range(4) for x in layer_steps(layer)]
        first, unit = {}, 0
        for layer, name, units, groups in steps:
            first[layer, name] = unit
            unit += units
        self.units = unit
        self.schedule(first)
        self.index, self.free_at, self.mods = [], [], {}
        unit = group = partial = 0
        for j in range(4):
            self.step["pro", j] = (0, 0, group, 1)
            self.stream += [("mod", 0, j, i) for i in range(4)]
            group += 1
        for layer, name, units, groups in steps:
            ends = []
            self.step[layer, name] = (unit, units, group, groups)
            for i in range(units):
                if unit + i in self.ahead:
                    target, j, part = self.ahead[unit + i]
                    self.stream.append(("mod", target, j, part))
                    if part == 3:
                        ends.append(i)
                        self.mods[layer, name, i] = (target, j)
                self.index.append(len(self.stream))
                self.stream.append(("weights", layer, name, i))
                partial += i < units - 1
                self.free_at.append(("used", partial) if i < units - 1 else ("group", group + groups - 1))
            unit += units
            group += groups
            for i in ends:
                self.step[layer, name, i] = (0, 0, group, 1)
                group += 1

    def schedule(self, first):
        self.ahead, self.rows = {}, {(0, j): j % 2 for j in range(4)}
        behind_norm = {first[key] + NR - i for key in first if key[1] in ("uf0", "up0", "pu", "f0") for i in (1, 2)}
        end = [-NR - 1, -NR - 1]
        at = 0
        for layer, name, rate, blocks in SCHEDULE:
            at = max(at, first[layer, name])
            for n, (target, j) in enumerate(blocks):
                both = len(mod_vectors(target, j)) == 2
                row = 0 if both else (0 if end[0] < end[1] else 1)
                rows = (0, 1) if both else (row,)
                at = max([at] + [end[r] + NR + 1 for r in rows])
                while any(at + rate * part in behind_norm for part in range(4)):
                    at += 1
                for part in range(4):
                    self.ahead[at + rate * part] = (target, j, part)
                for r in rows:
                    end[r] = at + 3 * rate
                self.rows[target, j] = row
                at += 4 * rate
                need = (first[target, "n1"] if j < 4 else first[target, "n2"] if j < 10 else first[target, "dn0" if target < 2 else "d00"])
                if j in (4, 5):
                    need = first[target, "wo0"]
                assert end[row] < need - 1, (target, j, end, need)


PLAN = Plan()


COLUMNS = {}


def _columns():
    at = 0

    def add(name, n):
        nonlocal at
        COLUMNS[name] = at
        at += n

    add("c", 3 * DC)
    for layer in range(4):
        add(f"n1_{layer}", DC)
        add(f"n2_{layer}", DC)
        add(f"bmod_{layer}", MODC)
    for layer in range(2):
        add(f"convw_{layer}", 3 * 2 * FC)
        add(f"convb_{layer}", 2 * FC)
    for layer in range(2, 4):
        add(f"pscale_{layer}", 2)
    add("final1", DC)
    add("final2", DC)
    return at


NCOL = _columns()


def program(nc, t):
    with ExitStack() as ctx:
        where = [nc.sbuf_base]

        def sb(name, shape, dt=F32, at=None):
            size = int(np.prod(shape[1:])) * 4
            if at is None:
                at = -(-where[0] // 32) * 32
                where[0] = at + size
            return nc.alloc_sbuf_tensor_at(name, shape, dt, offset=at)

        stage = sb("stage", [P, NS, UNIT])
        w_hi = sb("w_hi", [P, NR, UNIT], F32R)
        w_lo = sb("w_lo", [P, NR, UNIT], F32R)
        X = sb("X", [P, DC, T2])
        h_hi = sb("h_hi", [P, DC, T2], F32R)
        h_lo = sb("h_lo", [P, DC, T2], F32R)
        cols = sb("cols", [P, NCOL])
        csil = sb("csil", [P, 3 * DC])
        acc = sb("acc", [P, 2, COLS])
        MOD = sb("MOD", [P, 2, 2, MODC])
        MUL = sb("MUL", [P, 2, 2, 2, DC])
        eps = sb("eps", [1, P])
        mean_D = sb("mean_D", [P, P])
        mean_H = sb("mean_H", [P, P])
        ones = sb("ones", [P, P])
        idle = sb("idle", [1, 16])
        rstd = sb("rstd", [P, T2])

        tmp = -(-where[0] // 32) * 32
        KB = 1024
        sq = sb("sq", [P, 4, T2], F32, tmp)
        tt = sb("tt", [P, 4, T2], F32, tmp + 8 * KB)
        var = sb("var", [P, T2], F32, tmp + 16 * KB)
        ssum = sb("ssum", [P, T2], F32, tmp + 18 * KB)
        rope_q = sb("rope_q", [P, DC, S], F32, tmp)
        rope_k = sb("rope_k", [P, DC, S], F32, tmp + 8 * KB)
        probs1 = sb("probs1", [P, 2, 2, S], F32, tmp + 16 * KB)
        sq2 = sb("sq2", [P, 2, 4, S], F32, tmp)
        var2 = sb("var2", [P, 2, 2, S], F32, tmp + 8 * KB)
        rstd2 = sb("rstd2", [P, 2, 2, S], F32, tmp + 12 * KB)
        conv = sb("conv", [P, 2, 4, S], F32, tmp)
        relu = sb("relu", [P, 4, T2], F32, tmp)
        ropeA = sb("ropeA", [P, 4, 2, S], F32, tmp)
        stats = sb("stats", [P, 4, 12], F32, tmp + 20 * KB + 512)
        sc = sb("sc", [P, 2, T2], F32, tmp)
        scc = sb("scc", [P, 2, S], F32, tmp + 4 * KB)
        pT = sb("pT", [P, 4, S], F32, tmp + 6 * KB)
        pTc = sb("pTc", [P, 2, S], F32, tmp + 10 * KB)
        bias = sb("bias", [P, 2, 2, S], F32, tmp + 12 * KB)
        small = sb("small", [P, 4, 4], F32, tmp + 16 * KB)
        gt2 = sb("gt2", [P, 2, T2], F32, tmp + 16 * KB + 512)
        where[0] = tmp + 21 * KB

        ph = where[0]
        q1 = sb("q1", [P, DC, S], F32, ph)
        k1 = sb("k1", [P, DC, S], F32, ph + 8 * KB)
        v1 = sb("v1", [P, 2, D], F32, ph + 16 * KB)
        uf = sb("uf", [P, DC, S], F32, ph + 24 * KB)
        AB = sb("AB", [P, 2, DC, 2 * P], F32, ph + 32 * KB)
        r_hi = sb("r_hi", [P, DC, S], F32R, ph + 24 * KB)
        r_lo = sb("r_lo", [P, DC, S], F32R, ph + 32 * KB)
        g1 = sb("g1", [P, DC, S], F32, ph + 40 * KB)
        y1 = sb("y1", [P, DC, S], F32, ph + 48 * KB)
        rope1 = sb("rope1", [P, 2, S], F32, ph + 56 * KB)
        decay = sb("decay", [P, HEADS1, 2, S], F32, ph + 58 * KB)
        dftg = sb("dftg", [P, 2 * P], F32, ph + 66 * KB)
        dfts = sb("dfts", [P, 2, 2, S], F32, ph + 67 * KB)
        u_hi = sb("u_hi", [P, FC, S], F32R, ph)
        u_lo = sb("u_lo", [P, FC, S], F32R, ph + 22 * KB)

        q2 = sb("q2", [P, 4, T2], F32, ph)
        k2 = sb("k2", [P, 4, T2], F32, ph + 8 * KB)
        v2 = sb("v2", [P, 4, COLS], F32, ph + 16 * KB)
        y2 = sb("y2", [P, DC, T2], F32, ph + 24 * KB)
        b_hi = sb("b_hi", [P, 4, T2], F32R, ph + 40 * KB)
        b_lo = sb("b_lo", [P, 4, T2], F32R, ph + 48 * KB)
        PADW = S + 2 * 8
        pp = sb("pp", [P, 2, 2, PADW], F32, ph + 24 * KB)
        ps2 = sb("ps2", [P, 2, 2, PADW], F32, ph + 24 * KB + 4352)
        ps4 = sb("ps4", [P, 2, 2, PADW], F32, ph + 24 * KB + 2 * 4352)
        u2 = sb("u2", [P, 2, T2], F32, ph + 56 * KB)
        vn = sb("vn", [P, 4, 2 * P], F32, ph + 60 * KB)
        pooled = sb("pooled", [P, 2, T2], F32, tmp + 8 * KB)
        gt = sb("gt", [P, 4, T2], F32, ph + 56 * KB)
        gtb = sb("gtb", [P, 4, T2], F32, ph + 8 * KB)
        f_hi = sb("f_hi", [P, 16, T2], F32R, ph)
        f_lo = sb("f_lo", [P, 16, T2], F32R, ph + 32 * KB)
        rope2 = sb("rope2", [P, 2, S], F32, ph + 64 * KB)
        rinv = sb("rinv", [P, 2, S], F32, ph + 66 * KB)
        rotm = sb("rotm", [P, P], F32, ph + 68 * KB)
        wpool = sb("wpool", [P, 2, P], F32, ph + 68 * KB + 512)
        wsgu = sb("wsgu", [P, 4, P], F32, ph + 69 * KB + 512)
        ident = sb("ident", [P, P], F32, ph + 71 * KB + 512)
        sgub = sb("sgub", [1, 4 * P], F32, ph + 72 * KB)
        assert ph + 74 * KB <= nc.sbuf_usable_end, (ph + 74 * KB, nc.sbuf_usable_end)

        banks = [ctx.enter_context(nc.psum_tensor(f"bank{b}", [P, 512], F32)) for b in range(8)]

        def sem(name):
            return ctx.enter_context(nc.semaphore(name))

        filled = [sem(f"filled{b}") for b in range(8)]
        taken = [sem(f"taken{b}") for b in range(8)]
        arrived = [sem(f"arrived{i}") for i in range(NS)]
        hi_ready = sem("hi_ready")
        unit_done = sem("unit_done")
        units_used = sem("units_used")
        s = {n: sem(n) for n in (
            "loaded", "idle", "y_added", "x_loaded", "pro_used", "loaded1", "loaded2", "small2", "bias_in0",
            "bias_in1", "csil_ready", "const_ready", "sq_ready", "sq_used", "sq_added", "var_ready", "rstd_ready",
            "t_ready", "hhi_ready", "h_ready", "xf_ready", "uq_rot", "uk_rot", "fhi_ready", "g_sig", "sq2_ready",
            "rstd2_ready", "yn_ready", "rhi_ready", "r_ready", "m_ready", "mhi_ready", "mm_ready", "lin_ready",
            "gelu_ready", "u_ready", "uhi_ready", "uu_ready", "pooled_ready", "phi_ready", "vvar_ready",
            "vstd_ready", "sohi_ready", "b_ready", "pad_ready", "q2_rot", "k2_rot", "ctx_copied", "nmax_ready",
            "exp_ready", "p_ready", "aohi_ready", "a_ready", "fhid_ready", "fhihi_ready", "ff_ready", "out_ready",
            "stored")}

        def bank_of(g):
            return banks[g % 8]

        def wait_filled(eng, g):
            eng.wait_ge(filled[g % 8], g // 8 + 1)

        def wait_taken(eng, g):
            eng.wait_ge(taken[g % 8], g // 8 + 1)

        def grp(layer, name, i=0, at=None):
            return PLAN.step[(layer, name) if at is None else (layer, name, at)][2] + i

        def halves(T):
            return [(0, slice(0, S))] + ([(1, slice(S, T2))] if T == T2 else [])

        def col(name, i, n=1):
            return cols[:, COLUMNS[name] + i:COLUMNS[name] + i + n]

        block = ctx.enter_context(nc.Block())

        @block.sync
        def _(sp):
            sp.dma_start(cols[:, :], t["cols"]).then_inc(s["loaded"], 16)
            for n in range(NS):
                sp.dma_start(stage[:, n, :], t["stream"][n]).then_inc(arrived[n], 16)
            sp.dma_start(X[:, :, :], t["x"]).then_inc(s["x_loaded"], 16)
            total = len(PLAN.stream)

            def refills(a, b):
                with sp.Fori(a, b) as it:
                    for i in range(NS):
                        slot = i % NS
                        sp.wait_ge(unit_done, it * NS + (i + 1 - PRO // 4))
                        sp.dma_start(stage[:, slot, :],
                                     t["stream"][bass.ds(it * NS + (i + NS), 1)].rearrange("a p n -> (a p) n")
                                     ).then_inc(arrived[slot], 16)

            left = total - NS
            cut = (PLAN.index[PLAN.step[2, "pu"][0]] - NS) // NS
            for n in range(4 * NS):
                if multiplied_by_pe(n):
                    sp.wait_ge(s["pro_used"], n // 4 + 1)
                else:
                    sp.wait_ge(unit_done, done_value(n))
                sp.dma_start(stage[:, n % NS, :], t["stream"][n + NS]).then_inc(arrived[n % NS], 16)
            for dst, name in ((rope1, "rope1"), (decay, "decay"), (dftg, "dftg"), (dfts, "dfts")):
                sp.dma_start(dst.ap(), t[name]).then_inc(s["loaded1"], 16)
            refills(4, cut)
            wait_taken(sp, grp(1, "up0"))
            for dst, name in ((rope2, "rope2"), (rinv, "rinv"), (rotm, "rotm"), (ident, "ident")):
                sp.dma_start(dst.ap(), t[name]).then_inc(s["loaded2"], 16)

            def small_tables(layer):
                sp.dma_start(wpool[:, :, :], t["wpool"][layer - 2]).then_inc(s["small2"], 16)
                sp.dma_start(wsgu[:, :, :], t["wsgu"][layer - 2]).then_inc(s["small2"], 16)
                sp.dma_start(sgub[:, :], t["sgub"][layer - 2]).then_inc(s["small2"], 16)

            small_tables(2)
            cut2 = PLAN.index[PLAN.step[2, "f0"][0]] // NS
            refills(cut, cut2)
            wait_taken(sp, grp(2, "mix", 1))
            wait_taken(sp, grp(2, "pool", 1))
            small_tables(3)
            refills(cut2, left // NS)
            for r in range(left // NS * NS, left):
                sp.wait_ge(unit_done, done_value(r))
                n = r + NS
                sp.dma_start(stage[:, n % NS, :], t["stream"][n]).then_inc(arrived[n % NS], 16)
            sp.wait_ge(s["out_ready"], DC)
            sp.dma_start(t["out"], X[:, :, 0:S]).then_inc(s["stored"], 16)
            sp.wait_ge(s["stored"], 16)

        @block.tensor
        def _(pe):
            mm = nc.tensor.matmul

            def open_group(g):
                if g >= 8:
                    pe.wait_ge(taken[g % 8], g // 8)
                return banks[g % 8]

            def close_group(ins, g):
                ins.then_inc(filled[g % 8], 1)

            def unit_ready(m):
                pe.wait_ge(unit_done, done_value(PLAN.index[m]))

            def mod_sums(layer, name, unit):
                if (layer, name, unit) in PLAN.mods:
                    sum_partitions(grp(layer, name, at=unit), *PLAN.mods[layer, name, unit])

            def sum_partitions(g, target, j):
                row = PLAN.rows[target, j]
                bank = open_group(g)
                pe.wait_ge(unit_done, done_value(MOD_LAST[target, j]))
                for v in range(len(mod_vectors(target, j))):
                    for n in range(4):
                        last = mm(bank[:, 4 * v + n:4 * v + n + 1], acc[:, row + v, n * P:(n + 1) * P], ones[:, 0:1],
                                  start=True, stop=True)
                close_group(last, g)

            def multiply_first(j):
                n = 4 * j
                bank = open_group(grp("pro", j))
                pe.wait_ge(arrived[n % NS], 16 * (n // NS + 1))
                for k in range(KC):
                    for q in range(4):
                        last = mm(bank[:, q:q + 1], stage[:, n % NS, k * COLS + q * P:k * COLS + (q + 1) * P],
                                  csil[:, k:k + 1], start=(k, q) == (0, 0), stop=False, skip_group_check=True)
                last.then_inc(s["pro_used"], 1)

            def add_partitions(j):
                g = grp("pro", j)
                pe.wait_ge(unit_done, done_value(MOD_LAST[0, j]))
                for q in range(4):
                    last = mm(bank_of(g)[:, q:q + 1], acc[:, PLAN.rows[0, j], q * P:(q + 1) * P], ones[:, 0:1],
                              start=False, stop=True, skip_group_check=True)
                close_group(last, g)

            def first_unit(g0, ng, slot, xh, xl, tok, norm):
                for k in range(KC):
                    w = [slice(k * COLS + n * P, k * COLS + (n + 1) * P) for n in range(ng)]
                    pe.wait_ge(s["hhi_ready"], HREADY[norm] + k + 1)
                    for n in range(ng):
                        if k == 0:
                            open_group(g0 + n)
                        mm(bank_of(g0 + n)[:, tok], w_hi[:, slot, w[n]], xh[:, k, tok], start=k == 0, stop=False)
                        mm(bank_of(g0 + n)[:, tok], w_lo[:, slot, w[n]], xh[:, k, tok], start=False, stop=False)
                    pe.wait_ge(s["h_ready"], HREADY[norm] + k + 1)
                    for n in range(ng):
                        last_mm[0] = mm(bank_of(g0 + n)[:, tok], w_hi[:, slot, w[n]], xl[:, k, tok], start=False, stop=False)

            last_mm = [None]

            def last_used(sm):
                last_mm[0].then_inc(sm, 1)

            def feature_block(layer, name, xh, xl, T, x_ready, k0=0, before_last=None,
                              after_norm=None):
                m0, nu, g0, ng = PLAN.step[layer, name]
                for i in range(nu):
                    if i == nu - 1 and before_last:
                        before_last()
                    unit_ready(m0 + i)
                    slot = (m0 + i) % NR
                    if i == 0 and after_norm:
                        first_unit(g0, ng, slot, xh, xl, slice(0, T), after_norm)
                        last_used(units_used)
                        mod_sums(layer, name, i)
                        continue
                    x_ready(i)
                    for n in range(ng):
                        if i == 0:
                            open_group(g0 + n)
                        out = bank_of(g0 + n)[:, 0:T]
                        for k in range(KC):
                            c = k0 + KC * i + k
                            w = slice(k * COLS + n * P, k * COLS + (n + 1) * P)
                            first, final = i == 0 and k == 0, i == nu - 1 and k == KC - 1
                            mm(out, w_hi[:, slot, w], xh[:, c, 0:T], start=first, stop=False)
                            mm(out, w_hi[:, slot, w], xl[:, c, 0:T], start=False, stop=False)
                            last = mm(out, w_lo[:, slot, w], xh[:, c, 0:T], start=False, stop=final)
                        if i == nu - 1:
                            close_group(last, g0 + n)
                    if i < nu - 1:
                        last.then_inc(units_used, 1)
                    mod_sums(layer, name, i)

            def feature_block_halves(layer, name, xh, xl, norm):
                m0, nu, g0, ng = PLAN.step[layer, name]
                assert nu <= NR
                base = HREADY[norm]
                for v, tok in halves(T2):
                    for i in range(nu):
                        slot = (m0 + i) % NR
                        if v == 0:
                            unit_ready(m0 + i)
                            if i == 0:
                                first_unit(g0, ng, slot, xh, xl, tok, norm)
                                continue
                        pe.wait_ge(s["h_ready"], base + DC * v + KC * (i + 1))
                        for n in range(ng):
                            out = bank_of(g0 + n)[:, tok]
                            for k in range(KC):
                                c = KC * i + k
                                w = slice(k * COLS + n * P, k * COLS + (n + 1) * P)
                                first, final = i == 0 and k == 0, i == nu - 1 and k == KC - 1
                                mm(out, w_hi[:, slot, w], xh[:, c, tok], start=first, stop=False)
                                mm(out, w_hi[:, slot, w], xl[:, c, tok], start=False, stop=False)
                                last = mm(out, w_lo[:, slot, w], xh[:, c, tok], start=False, stop=final)
                            if v == 1 and i == nu - 1:
                                close_group(last, g0 + n)
                        if v == 1 and i < nu - 1:
                            last.then_inc(units_used, 1)
                        if v == 1:
                            mod_sums(layer, name, i)

            def token_block(layer, name, xh, xl, x_ready, width=COLS):
                m0, nu, g0, ng = PLAN.step[layer, name]
                kc = UNIT // width
                for i in range(nu):
                    unit_ready(m0 + i)
                    slot = (m0 + i) % NR
                    x_ready(i)
                    for n in range(ng):
                        if i == 0:
                            open_group(g0 + n)
                        out = bank_of(g0 + n)[:, 0:width]
                        tok = slice(n * P, (n + 1) * P)
                        for k in range(kc):
                            c = kc * i + k
                            w = slice(k * width, (k + 1) * width)
                            first, final = i == 0 and k == 0, i == nu - 1 and k == kc - 1
                            mm(out, xh[:, c, tok], w_hi[:, slot, w], start=first, stop=False)
                            mm(out, xh[:, c, tok], w_lo[:, slot, w], start=False, stop=False)
                            last = mm(out, xl[:, c, tok], w_hi[:, slot, w], start=False, stop=final)
                        if i == nu - 1:
                            close_group(last, g0 + n)
                    if i < nu - 1:
                        last.then_inc(units_used, 1)
                    mod_sums(layer, name, i)

            def epsilon(out, T):
                row = ones[0:1, :].rearrange("p (a n) -> p a n", a=1).to_broadcast([1, T // P, P])
                mm(out, eps[0:1, :], row, start=True, stop=False)

            def first_sums(layer, name, T):
                g = grp(layer, name)
                open_group(g)
                epsilon(bank_of(g)[:, 0:T], T)
                if (layer, name) in ADDED:
                    pe.wait_ge(s["sq_added"], 3 * ADDED.index((layer, name)) + 3)
                    mm(bank_of(g)[:, 0:T], mean_D[:, :], ssum[:, 0:T], start=False, stop=False)

            def norm_sums(layer, name, T):
                g = grp(layer, name)
                parts = SQUARES[layer, name]
                added = (layer, name) in ADDED
                if not (added and (layer, name) in BOTH):
                    first_sums(layer, name, T)
                for i, (c, tok) in enumerate(parts):
                    if added and c < DC // 2:
                        continue
                    pe.wait_ge(s["sq_ready"], SQ_BEFORE[layer, name] + i + 1)
                    ins = mm(bank_of(g)[:, tok], mean_D[:, :], sq[:, c % 4, tok], start=False, stop=i == len(parts) - 1)
                    if i == len(parts) - 1:
                        close_group(ins, g)
                    elif not added:
                        ins.then_inc(s["sq_used"], 1)

            def h_ready(layer, name, per=KC):
                base = HREADY[layer, name]
                return lambda i: pe.wait_ge(s["h_ready"], base + min(per * (i + 1), DC))

            def nothing(i):
                pass

            def count(name, base, per=KC):
                return lambda i: pe.wait_ge(s[name], base + per * (i + 1))

            pe.wait_ge(s["const_ready"], 4)
            pe.wait_ge(s["csil_ready"], 1)
            multiply_first(0)
            multiply_first(1)
            add_partitions(0)
            norm_sums(0, "n1", S)
            multiply_first(2)
            add_partitions(1)
            multiply_first(3)
            add_partitions(2)
            add_partitions(3)

            for L in range(2):
                hh, hl = h_hi[:, :, 0:S], h_lo[:, :, 0:S]
                if L:
                    norm_sums(L, "n1", S)
                feature_block(L, "uf0", hh, hl, S, h_ready(L, "n1"), after_norm=(L, "n1"))
                for name in ("uf1", "q0", "q1"):
                    feature_block(L, name, hh, hl, S, nothing)
                if L == 0:
                    pe.wait_ge(s["loaded1"], 64)
                for c in range(DC):
                    g = grp(L, "F1", c)
                    wait_taken(pe, grp(L, f"uf{c // 4}", c % 4))
                    out = open_group(g)
                    for st in range(2):
                        last = mm(out[:, st * S:(st + 1) * S], uf[:, c, st * P:(st + 1) * P], dftg[:, :],
                                  start=True, stop=True)
                    close_group(last, g)
                for name in ("k0", "k1"):
                    feature_block(L, name, hh, hl, S, nothing)
                for cc in range(DC // 2):
                    g = grp(L, "F2", cc)
                    out = open_group(g)
                    for half in range(2):
                        c = 2 * cc + half
                        wait_taken(pe, grp(L, "F1", c))
                        for st in range(2):
                            for part in range(2):
                                last = mm(out[:, half * S:(half + 1) * S], AB[:, st, c, part * P:(part + 1) * P],
                                          dfts[:, part, st, :], start=st == 0 and part == 0,
                                          stop=st == 1 and part == 1)
                    close_group(last, g)
                for name in ("v0", "v1"):
                    token_block(L, name, hh, hl, nothing)

                def scores(h):
                    if h == 0:
                        pe.wait_ge(s["uq_rot"], L + 1)
                        pe.wait_ge(s["uk_rot"], L + 1)
                    g = grp(L, f"S{h}")
                    out = open_group(g)
                    for jt in range(2):
                        for dc in range(2):
                            last = mm(out[:, jt * S:(jt + 1) * S], k1[:, 2 * h + dc, jt * P:(jt + 1) * P],
                                      q1[:, 2 * h + dc, :], start=dc == 0, stop=dc == 1)
                    close_group(last, g)

                def values(h):
                    if h == 0:
                        for nb in range(2):
                            for tk in range(2):
                                wait_taken(pe, grp(L, f"v{nb}", tk))
                    wait_taken(pe, grp(L, f"S{h}"))
                    g = grp(L, f"V{h}")
                    out = open_group(g)
                    for dc in range(2):
                        for jt in range(2):
                            last = mm(out[:, dc * S:(dc + 1) * S],
                                      v1[:, jt, h * DK1 + dc * P:h * DK1 + (dc + 1) * P],
                                      probs1[:, h % 2, jt, :], start=jt == 0, stop=jt == 1)
                    close_group(last, g)

                def head_means(hp):
                    g = grp(L, f"M{hp}")
                    out = open_group(g)
                    for i in range(2):
                        wait_taken(pe, grp(L, f"V{2 * hp + i}"))
                        for dc in range(2):
                            last = mm(out[:, i * S:(i + 1) * S], mean_H[:, :], q1[:, 4 * hp + 2 * i + dc, :],
                                      start=dc == 0, stop=dc == 1)
                    close_group(last, g)

                def head_vars(hp):
                    g = grp(L, f"R{hp}")
                    out = open_group(g)
                    epsilon(out[:, :], T2)
                    pe.wait_ge(s["sq2_ready"], 2 * L + hp + 1)
                    for dc in range(2):
                        last = mm(out[:, :], mean_H[:, :],
                                  sq2[:, hp, :, :].rearrange("p (i d) t -> p d i t", d=2)[:, dc], start=False, stop=dc == 1)
                    close_group(last, g)

                feature_block(L, "af0", hh, hl, S, nothing)
                scores(0)
                scores(1)
                feature_block(L, "af1", hh, hl, S, nothing)
                values(0)
                values(1)
                scores(2)
                scores(3)
                fh, fl = h_hi[:, :, S:T2], h_lo[:, :, S:T2]

                def fourier_ready(i):
                    wait_taken(pe, grp(L, "F2", i))
                feature_block(L, "wf0", fh, fl, S, fourier_ready)
                values(2)
                values(3)
                feature_block(L, "wf1", fh, fl, S, nothing)
                head_means(0)
                head_means(1)
                feature_block(L, "g0", hh, hl, S, nothing)
                head_vars(0)
                head_vars(1)
                for name in ("g1", "ar0", "ar1"):
                    feature_block(L, name, hh, hl, S, nothing)
                feature_block(L, "wr0", r_hi, r_lo, S, lambda i: pe.wait_ge(s["r_ready"], 2 * L + i // 2 + 1))
                feature_block(L, "wr1", r_hi, r_lo, S, nothing)
                feature_block(L, "wo0", hh, hl, S, lambda i: pe.wait_ge(s["mm_ready"], 2 * L + i // 2 + 1))
                feature_block(L, "wo1", hh, hl, S, nothing)
                norm_sums(L, "n2", S)
                feature_block(L, "up0", hh, hl, S, h_ready(L, "n2"), after_norm=(L, "n2"))
                for b in range(1, FC // 2):
                    feature_block(L, f"up{b}", hh, hl, S, nothing)
                feature_block(L, "dn0", u_hi, u_lo, S, lambda i: pe.wait_ge(s["uu_ready"], L * (FC // 2) + i + 1))
                feature_block(L, "dn1", u_hi, u_lo, S, nothing)
                if L == 1:
                    norm_sums(1, "nf", S)

            for L in (2, 3):
                with_ctx = L == 2
                T = T2 if with_ctx else S
                norm_sums(L, "n1", T2)
                if L == 2:
                    feature_block_halves(L, "pu", h_hi, h_lo, (2, "n1"))
                else:
                    feature_block(L, "pu", h_hi, h_lo, T, h_ready(L, "n1"), after_norm=(L, "n1"))
                token_block(L, "vs", h_hi, h_lo, nothing, width=2 * P)
                feature_block(L, "q", h_hi, h_lo, T, nothing)

                def rotated(name, src, blk):
                    for cc in range(2):
                        g = grp(L, f"{name}{cc}")
                        out = open_group(g)
                        for i in range(2):
                            wait_taken(pe, grp(L, blk, 2 * cc + i))
                            last = mm(out[:, i * S:(i + 1) * S], rotm[:, :], src[:, 2 * cc + i, 0:S], start=True, stop=True)
                        close_group(last, g)

                if L == 2:
                    pe.wait_ge(s["loaded2"], 64)
                feature_block(L, "k", h_hi, h_lo, T2, lambda i: pe.wait_ge(s["h_ready"], HREADY[L, "n1"] + 2 * DC),
                              before_last=lambda: rotated("rq", q2, "q"))
                rotated("rk", k2, "k")

                def pool_and_mix():
                    pe.wait_ge(s["small2"], 48 * (L - 1))
                    pe.wait_ge(s["pooled_ready"], L - 1)
                    for c in range(2):
                        g = grp(L, "pool", c)
                        out = open_group(g)[:, 0:T]
                        close_group(mm(out, wpool[:, c, :], pooled[:, c, 0:T], start=True, stop=True), g)
                    for fc in range(2):
                        g = grp(L, "mix", fc)
                        out = open_group(g)
                        for tk in range(T // P):
                            wait_taken(pe, grp(L, "vs", tk))
                            for e in range(2):
                                hd = 2 * fc + e
                                o = out[64 * e:64 * e + 64, tk * P:(tk + 1) * P]
                                mm(o, vn[:, tk, hd * 64:(hd + 1) * 64], wsgu[:, hd, :], start=True, stop=False)
                                last = mm(o, ones[0:1, 0:64], sgub[0:1, hd * P:(hd + 1) * P], start=False, stop=True)
                        close_group(last, g)

                pool_and_mix()

                def scores2(h):
                    rows = slice(64 * (h % 2), 64 * (h % 2) + 64)
                    if h == 0:
                        pe.wait_ge(s["q2_rot"], 2 * (L - 1))
                        pe.wait_ge(s["k2_rot"], 2 * (L - 1))
                        for n in range(4):
                            wait_taken(pe, grp(L, "q", n))
                            wait_taken(pe, grp(L, "k", n))
                    for qt, tag in enumerate("ab"):
                        g = grp(L, f"X{h}{tag}")
                        out = open_group(g)
                        close_group(mm(out[:, :], q2[rows, h // 2, qt * P:(qt + 1) * P], k2[rows, h // 2, :],
                                       start=True, stop=True), g)
                    if with_ctx:
                        g = grp(L, f"C{h}")
                        out = open_group(g)
                        for qt in range(2):
                            last = mm(out[:, qt * S:(qt + 1) * S], q2[rows, h // 2, S + qt * P:S + (qt + 1) * P],
                                      k2[rows, h // 2, S:T2], start=True, stop=True)
                        close_group(last, g)

                def transposes(h):
                    for qt, tag in enumerate("ab"):
                        g = grp(L, f"T{h}{tag}")
                        out = open_group(g)
                        pe.wait_ge(s["p_ready"], PREADY[L] + PPER[L] * h + qt + 1)
                        for kc in range(4):
                            last = nc.tensor.transpose(out[:, kc * P:(kc + 1) * P], sc[:, qt, kc * P:(kc + 1) * P], ident[:, :])
                        close_group(last, g)
                    if with_ctx:
                        g = grp(L, f"U{h}")
                        out = open_group(g)
                        pe.wait_ge(s["p_ready"], PREADY[L] + PPER[L] * h + 3)
                        for qt in range(2):
                            for kc in range(2):
                                last = nc.tensor.transpose(out[:, kc * S + qt * P:kc * S + (qt + 1) * P],
                                                           scc[:, qt, kc * P:(kc + 1) * P], ident[:, :])
                        close_group(last, g)

                def attend(h):
                    g = grp(L, f"O{h}")
                    bank = open_group(g)
                    rows = slice(64 * (h % 2), 64 * (h % 2) + 64)
                    if h == 0:
                        for n in range(4):
                            wait_taken(pe, grp(L, "v", n))
                    wait_taken(pe, grp(L, f"T{h}a"))
                    wait_taken(pe, grp(L, f"T{h}b"))
                    for kc in range(4):
                        last = mm(bank[rows, 0:S], v2[:, kc, h * DK2:(h + 1) * DK2], pT[:, kc, :],
                                  start=kc == 0, stop=kc == 3)
                    if with_ctx:
                        wait_taken(pe, grp(L, f"U{h}"))
                        for kc in range(2):
                            last = mm(bank[rows, S:T2], v2[:, 2 + kc, h * DK2:(h + 1) * DK2], pTc[:, kc, :],
                                      start=kc == 0, stop=kc == 1)
                    close_group(last, g)

                def run(name):
                    if name == "v":
                        token_block(L, "v", h_hi, h_lo, nothing)
                    elif name[0] == "g":
                        feature_block(L, name, h_hi, h_lo, T, nothing)
                    elif name[0] == "p":
                        def pool_ready(i):
                            for c in range(2):
                                wait_taken(pe, grp(L, "pool", c))
                        feature_block(L, name, b_hi, b_lo, T, pool_ready)
                    else:
                        feature_block(L, name, b_hi, b_lo, T, lambda i: pe.wait_ge(s["b_ready"], 2 * (L - 1)), k0=2)

                for h in range(HEADS2):
                    scores2(h)
                    if h:
                        attend(h - 1)
                    for name in ATTENTION_FILL[h]:
                        run(name)
                    transposes(h)
                attend(HEADS2 - 1)
                feature_block(L, "ao0", b_hi, b_lo, T, lambda i: pe.wait_ge(s["a_ready"], 4 * (L - 2) + 2 * i + 2))
                feature_block(L, "ao1", b_hi, b_lo, T, nothing)
                feature_block(L, "wo0", h_hi, h_lo, T, lambda i: pe.wait_ge(s["mm_ready"], 4 + DC * (L - 2) + 2 * i + 2))
                feature_block(L, "wo1", h_hi, h_lo, T, nothing,
                              before_last=(lambda: first_sums(2, "n2", T2)) if L == 2 else None)
                norm_sums(L, "n2", T)
                for half in range(2):
                    for b in range(4 * half, 4 * half + 4):
                        if L == 2 and b == 0:
                            feature_block_halves(L, "f0", h_hi, h_lo, (2, "n2"))
                        else:
                            feature_block(L, f"f{b}", h_hi, h_lo, T, h_ready(L, "n2") if b == 0 else nothing,
                                          after_norm=None if b else (L, "n2"))
                    base = 32 * (L - 2) + 16 * half
                    feature_block(L, f"d{half}0", f_hi, f_lo, T, count("ff_ready", base))
                    feature_block(L, f"d{half}1", f_hi, f_lo, T, nothing,
                                  before_last=(lambda: first_sums(3, "n1", T2)) if L == 2 and half else None)
                if L == 3:
                    norm_sums(3, "nf", S)

        @block.scalar
        def _(act):
            A = nc.scalar.activation
            split = [0]
            used = [0]

            def make_hi(m):
                n = PLAN.index[m]
                act.wait_ge(arrived[n % NS], 16 * (n // NS + 1))
                if m >= NR:
                    kind, v = PLAN.free_at[m - NR]
                    if kind == "used":
                        act.wait_ge(units_used, v)
                    else:
                        wait_filled(act, v)
                A(w_hi[:, m % NR, :], stage[:, n % NS, :], ACT.Copy).then_inc(hi_ready, 1)

            def advance(n):
                for _ in range(n):
                    used[0] += 1
                    while split[0] < min(used[0] + NR, PLAN.units):
                        make_hi(split[0])
                        split[0] += 1

            def most_of(layer, name):
                advance(PLAN.step[layer, name][1] - 1)
                return PLAN.step[layer, name][2]

            def each(layer, name, do):
                g0 = most_of(layer, name)
                for n in range(PLAN.step[layer, name][3]):
                    wait_filled(act, g0 + n)
                    do(n, bank_of(g0 + n)).then_inc(taken[(g0 + n) % 8], 1)
                if PLAN.step[layer, name][1]:
                    advance(1)

            def squares(layer, name, T, ready, chunks, first_tokens=None):
                nth = NORMS.index((layer, name))
                if 0 in chunks:
                    A(idle[0:1, nth:nth + 1], ones[0:1, 0:1], ACT.Sqrt).then_inc(s["idle"], 1)
                for i, (c, tok) in enumerate(SQUARES[layer, name]):
                    if c not in chunks or first_tokens not in (None, tok.start):
                        continue
                    if tok.start == 0:
                        ready(c)
                    if i >= 4 and (layer, name) in ADDED:
                        act.wait_ge(s["sq_added"], 3 * ADDED.index((layer, name)) + max(1, i - 4))
                    elif i >= 4:
                        act.wait_ge(s["sq_used"], (DC - 1 if layer == 2 else 0) + i - 3)
                    elif nth:
                        wait_filled(act, grp(*NORMS[nth - 1]))
                    A(sq[:, c % 4, tok], X[:, c, tok], ACT.Square).then_inc(s["sq_ready"], 1)

            def norm(layer, name, T, ready, n=0):
                if n:
                    advance(n - 3)
                    squares(layer, name, T, ready, range(DC // 2))
                    advance(2)
                    squares(layer, name, T, ready, range(DC // 2, DC))
                    advance(1)
                else:
                    squares(layer, name, T, ready, range(DC), 0)
                if name == "nf" and layer == 1:
                    squares(2, "n1", T2, None, range(DC), S)

                def root(v, tok):
                    if (layer, name) in BOTH and v == 0:
                        act.wait_ge(s["var_ready"], BOTH.index((layer, name)) + 1)
                    else:
                        wait_taken(act, grp(layer, name))
                    A(rstd[:, tok], var[:, tok], ACT.Sqrt).then_inc(s["rstd_ready"], 1)
                root(*halves(T)[0])
                if (layer, name) == (0, "n1"):
                    for m in range(NR):
                        make_hi(m)
                    split[0] = NR
                if name == "nf":
                    return
                base = HREADY[layer, name]
                shift = 0 if name == "n1" else 3 * DC
                for v, tok in halves(T):
                    if v:
                        root(v, tok)
                    for c in range(DC):
                        act.wait_ge(s["t_ready"], base + DC * v + c + 1)
                        A(h_hi[:, c, tok], tt[:, c % 4, tok], ACT.Identity,
                          bias=MOD[:, layer % 2, v, shift + c:shift + c + 1]).then_inc(s["hhi_ready"], 1)
                        if v and layer == 3 and c % 2 == 1 and c > 1:
                            advance(1)

            act.wait_ge(s["const_ready"], 4)
            act.wait_ge(s["loaded"], 16)
            A(csil[:, :], col("c", 0, 3 * DC), ACT.Silu).then_inc(s["csil_ready"], 1)
            act.wait_ge(s["x_loaded"], 16)
            for L in range(2):
                def x_ready(c, L=L):
                    if L:
                        wait_taken(act, grp(L - 1, f"dn{c // 4}", c % 4))
                norm(L, "n1", S, x_ready, n=FC // 2 if L else 0)
                for nb in range(2):
                    each(L, f"uf{nb}", lambda n, b: A(uf[:, 4 * nb + n, :], b[:, 0:S], ACT.Copy))
                for nb in range(2):
                    each(L, f"q{nb}", lambda n, b: A(q1[:, 4 * nb + n, :], b[:, 0:S], ACT.Copy))
                each(L, "F1", lambda n, b: A(AB[:, :, n, :], b[:, :].rearrange("p (s c) -> p s c", s=2), ACT.Copy))
                for nb in range(2):
                    each(L, f"k{nb}", lambda n, b: A(k1[:, 4 * nb + n, :], b[:, 0:S], ACT.Copy))
                for cc in range(DC // 2):
                    g = grp(L, "F2", cc)
                    wait_filled(act, g)
                    A(h_hi[:, 2 * cc:2 * cc + 2, S:T2], bank_of(g)[:, :].rearrange("p (c t) -> p c t", c=2),
                      ACT.Copy).then_inc(s["fhi_ready"], 1)
                for nb in range(2):
                    each(L, f"v{nb}", lambda n, b: A(v1[:, n, nb * COLS:(nb + 1) * COLS], b[:, :], ACT.Copy))
                each(L, "af0", lambda n, b: A(y1[:, n, :], b[:, 0:S], ACT.Sigmoid))
                each(L, "af1", lambda n, b: A(y1[:, 4 + n, :], b[:, 0:S], ACT.Sigmoid))

                def head_out(h):
                    g = grp(L, f"V{h}")
                    wait_filled(act, g)
                    A(q1[:, 2 * h:2 * h + 2, :], bank_of(g)[:, :].rearrange("p (c t) -> p c t", c=2),
                      ACT.Copy).then_inc(taken[g % 8], 1)
                head_out(0)
                head_out(1)
                advance(4)
                head_out(2)
                head_out(3)
                advance(4)
                for hp in range(2):
                    wait_taken(act, grp(L, f"M{hp}"))
                    A(sq2[:, hp, :, :], q1[:, 4 * hp:4 * hp + 4, :], ACT.Square).then_inc(s["sq2_ready"], 1)

                def gate_sigmoid(nb):
                    g0 = most_of(L, f"g{nb}")
                    for n in range(4):
                        wait_filled(act, g0 + n)
                        A(g1[:, 4 * nb + n, :], bank_of(g0 + n)[:, 0:S], ACT.Sigmoid).then_inc(s["g_sig"], 1)
                    advance(1)
                gate_sigmoid(0)
                for hp in range(2):
                    wait_taken(act, grp(L, f"R{hp}"))
                    A(rstd2[:, hp, :, :], var2[:, hp, :, :], ACT.Sqrt).then_inc(s["rstd2_ready"], 1)
                gate_sigmoid(1)
                for hp in range(2):
                    act.wait_ge(s["yn_ready"], 2 * L + hp + 1)
                    A(r_hi[:, 4 * hp:4 * hp + 4, :], q1[:, 4 * hp:4 * hp + 4, :], ACT.Copy).then_inc(s["rhi_ready"], 1)
                    each(L, f"ar{hp}", lambda n, b: A(k1[:, 4 * hp + n, :], b[:, 0:S], ACT.Sigmoid))
                for nb in range(2):
                    advance(4)
                    act.wait_ge(s["m_ready"], 2 * L + nb + 1)
                    A(h_hi[:, 4 * nb:4 * nb + 4, 0:S], y1[:, 4 * nb:4 * nb + 4, :], ACT.Copy).then_inc(s["mhi_ready"], 1)
                norm(L, "n2", S, lambda c: wait_taken(act, grp(L, f"wo{c // 4}", c % 4)), n=8)

                def gelu(b):
                    wait_taken(act, grp(L, f"up{b}", 1))
                    A(conv[:, b % 2, 0:2, :], conv[:, b % 2, 0:2, :], ACT.Gelu).then_inc(s["gelu_ready"], 1)

                def hidden_hi(b):
                    act.wait_ge(s["u_ready"], L * (FC // 2) + b + 1)
                    A(u_hi[:, 2 * b:2 * b + 2, :], conv[:, b % 2, 2:4, :], ACT.Copy).then_inc(s["uhi_ready"], 1)

                for b in range(FC // 2):
                    it = L * (FC // 2) + b
                    advance(2)
                    if b:
                        gelu(b - 1)
                    advance(1)
                    if b:
                        hidden_hi(b - 1)
                    for n in range(4):
                        g = grp(L, f"up{b}", n)
                        ch = 2 * b + n if n < 2 else FC + 2 * b + n - 2
                        wait_filled(act, g)
                        if n == 0 and b >= 2:
                            act.wait_ge(s["uu_ready"], it - 1)
                        A(conv[:, b % 2, n, :], bank_of(g)[:, 0:S], ACT.Identity,
                          bias=col(f"convb_{L}", ch), scale=col(f"convw_{L}", 2 * FC + ch)).then_inc(s["lin_ready"], 1)
                    advance(1)
                advance(2)
                gelu(FC // 2 - 1)
                advance(1)
                hidden_hi(FC // 2 - 1)
                advance(FC // 2 - 3)
                if L == 1:
                    norm(1, "nf", S, lambda c: wait_taken(act, grp(1, f"dn{c // 4}", c % 4)), n=FC // 2)

            for L in (2, 3):
                with_ctx = L == 2
                T = T2 if with_ctx else S

                def x_ready(c, L=L):
                    if L == 2:
                        act.wait_ge(s["xf_ready"], c + 1)
                    else:
                        wait_taken(act, grp(2, f"d1{c // 4}", c % 4))
                norm(L, "n1", T2, x_ready, n=8 if L == 3 else 0)
                if L == 2:
                    most_of(2, "pu")
                g0 = grp(L, "pu")
                for n in range(4):
                    wait_filled(act, g0 + n)
                    if n < 2:
                        act.wait_ge(s["pad_ready"], L - 1)
                        ins = A(pp[:, n, 0:T // S, 8:8 + S], bank_of(g0 + n)[:, 0:T].rearrange("p (s t) -> p s t", t=S), ACT.Copy)
                    else:
                        ins = A(u2[:, n - 2, 0:T], bank_of(g0 + n)[:, 0:T], ACT.Copy)
                    ins.then_inc(taken[(g0 + n) % 8], 1)
                advance(1)
                advance(2)
                for tk in range(T // P):
                    nth = (0 if L == 2 else 4) + tk + 1
                    act.wait_ge(s["vvar_ready"], nth)
                    A(stats[:, tk, 10:11], stats[:, tk, 9:10], ACT.Sqrt).then_inc(s["vstd_ready"], 1)
                each(L, "q", lambda n, b: A(q2[:, n, 0:T], b[:, 0:T], ACT.Copy, scale=DK2 ** -0.5))
                each(L, "k", lambda n, b: A(k2[:, n, :], b[:, :], ACT.Copy))
                for c in range(2):
                    g = grp(L, "pool", c)
                    wait_filled(act, g)
                    A(b_hi[:, c, 0:T], bank_of(g)[:, 0:T], ACT.Copy, scale=col(f"pscale_{L}", c)).then_inc(s["phi_ready"], 1)

                def values_and_branches():
                    for fc in range(2):
                        wait_taken(act, grp(L, "mix", fc))
                        A(b_hi[:, 2 + fc, 0:T], u2[:, fc, 0:T], ACT.Copy).then_inc(s["sohi_ready"], 1)
                    each(L, "v", lambda n, b: A(v2[:, n, :], b[:, :], ACT.Copy))

                per = PPER[L]

                def softmax(h):
                    for qt, tag in enumerate("ab"):
                        g = grp(L, f"X{h}{tag}")
                        wait_filled(act, g)
                        if h:
                            wait_filled(act, grp(L, f"T{h - 1}{tag}"))
                        A(sc[:, qt, S:T2], bank_of(g)[:, S:T2], ACT.Copy).then_inc(s["ctx_copied"], 1)
                    if with_ctx:
                        g = grp(L, f"C{h}")
                        wait_filled(act, g)
                    for i in range(per):
                        at = PREADY[L] + per * h + i + 1
                        act.wait_ge(s["nmax_ready"], at)
                        if i < 2:
                            A(sc[:, i, :], sc[:, i, :], ACT.Exp, bias=small[:, 0, i:i + 1],
                              accum_out=small[:, 1, i:i + 1]).then_inc(s["exp_ready"], 1)
                        else:
                            g = grp(L, f"C{h}")
                            if h:
                                wait_filled(act, grp(L, f"U{h - 1}"))
                            for qt in range(2):
                                ins = A(scc[:, qt, :], bank_of(g)[:, qt * S:(qt + 1) * S], ACT.Exp,
                                        bias=small[:, 0, 2 + qt:3 + qt], accum_out=small[:, 1, 2 + qt:3 + qt])
                                if qt == 0:
                                    ins.then_inc(s["exp_ready"], 1)
                            ins.then_inc(taken[g % 8], 1)

                def take_transposed(h):
                    if h:
                        wait_filled(act, grp(L, f"O{h - 1}"))
                    for qt, tag in enumerate("ab"):
                        g = grp(L, f"T{h}{tag}")
                        wait_filled(act, g)
                        A(pT[:, :, qt * P:(qt + 1) * P], bank_of(g)[:, :].rearrange("p (k q) -> p k q", k=4),
                          ACT.Copy).then_inc(taken[g % 8], 1)
                    if with_ctx:
                        g = grp(L, f"U{h}")
                        wait_filled(act, g)
                        A(pTc[:, :, :], bank_of(g)[:, :].rearrange("p (k q) -> p k q", k=2),
                          ACT.Copy).then_inc(taken[g % 8], 1)

                def take_out(h):
                    g = grp(L, f"O{h}")
                    wait_filled(act, g)
                    rows = slice(64 * (h % 2), 64 * (h % 2) + 64)
                    A(q2[rows, h // 2, 0:T], bank_of(g)[rows, 0:T], ACT.Copy).then_inc(taken[g % 8], 1)

                def gate_block(name):
                    g0 = most_of(L, name)
                    before = {"gs0": "po0", "gp1": "so0", "gs1": "po1", "ga0": "so1"}.get(name)
                    if name == "gp0":
                        act.wait_ge(s["b_ready"], 2 * (L - 1))
                    dst = gtb if name == "ga1" else gt
                    for n in range(4):
                        wait_filled(act, g0 + n)
                        if before:
                            wait_taken(act, grp(L, before, n))
                        A(dst[:, n, 0:T], bank_of(g0 + n)[:, 0:T], ACT.Sigmoid).then_inc(taken[(g0 + n) % 8], 1)
                    advance(1)

                def attention_hi(c):
                    wait_taken(act, grp(L, f"O{2 * c + 1}"))
                    A(b_hi[:, c, 0:T], q2[:, c, 0:T], ACT.Copy).then_inc(s["aohi_ready"], 1)

                for h in range(HEADS2):
                    softmax(h)
                    if h:
                        take_out(h - 1)
                    if h == HEADS2 - 1:
                        wait_filled(act, grp(L, "so1", 3))
                        for c in range(3):
                            attention_hi(c)
                    for name in ATTENTION_FILL[h]:
                        if name == "v":
                            values_and_branches()
                        elif name[0] == "g":
                            gate_block(name)
                        else:
                            advance(1)
                    take_transposed(h)
                take_out(HEADS2 - 1)
                attention_hi(3)
                for nb in range(2):
                    advance(2 if nb else 3)
                    for c in range(4 * nb, 4 * nb + 4):
                        act.wait_ge(s["y_added"], 16 * (L - 2) + 8 + c + 1)
                        A(h_hi[:, c, 0:T], y2[:, c, 0:T], ACT.Copy).then_inc(s["mhi_ready"], 1)
                norm(L, "n2", T, lambda c: wait_taken(act, grp(L, f"wo{c // 4}", c % 4)), n=7)

                def hidden2_hi(b, part):
                    for n in range(2 * part, 2 * part + 2):
                        act.wait_ge(s["fhid_ready"], 32 * (L - 2) + 4 * b + n + 1)
                        A(f_hi[:, (4 * b + n) % 16, 0:T], relu[:, n, 0:T], ACT.Copy).then_inc(s["fhihi_ready"], 1)

                for half in range(2):
                    for b in range(4 * half, 4 * half + 4):
                        for part in range(2):
                            advance(1)
                            if b % 4:
                                hidden2_hi(b - 1, part)
                        advance(1)
                        for n in range(4):
                            i = 32 * (L - 2) + 4 * b + n
                            g = grp(L, f"f{b}", n)
                            wait_filled(act, g)
                            if i >= 4:
                                act.wait_ge(s["ff_ready"], i - 3)
                            A(relu[:, n, 0:T], bank_of(g)[:, 0:T], ACT.Relu).then_inc(taken[g % 8], 1)
                        advance(1)
                    for part in range(2):
                        advance(1)
                        hidden2_hi(4 * half + 3, part)
                    advance(6 if half else 14)
                if L == 3:
                    norm(3, "nf", S, lambda c: wait_taken(act, grp(3, f"d1{c // 4}", c % 4)), n=8)

        @block.vector
        def _(dve):
            V = nc.vector
            steps = sem("dve_steps")
            count = [0]
            last = [None]

            def do(ins, sm=None, value=None):
                if sm is None:
                    count[0] += 1
                    ins.then_inc(steps, 1)
                    last[0] = (steps, count[0])
                else:
                    ins.then_inc(sm, 1)
                    last[0] = (sm, value)

            def settle():
                dve.wait_ge(*last[0])

            def take(ins, g):
                do(ins, taken[g % 8], g // 8 + 1)

            done = [0]
            used = [0]

            def stream_unit():
                n = done[0]
                kind, *at = PLAN.stream[n]
                if multiplied_by_pe(n):
                    pass
                elif kind == "weights":
                    m = STREAM_UNIT[n]
                    dve.wait_ge(hi_ready, m + 1)
                    do(V.tensor_tensor(w_lo[:, m % NR, :], stage[:, n % NS, :], w_hi[:, m % NR, :].bitcast(F32),
                                       ALU.subtract), unit_done, done_value(n))
                else:
                    layer, j, i = at
                    dve.wait_ge(arrived[n % NS], 16 * (n // NS + 1))
                    vecs = mod_vectors(layer, j)
                    first_part = 1 if n < PRO else 0
                    for k in range(KC):
                        for v, vec in enumerate(vecs):
                            w = stage[:, n % NS, k * COLS:(k + 1) * COLS]
                            cc = csil[:, vec * DC + KC * i + k:vec * DC + KC * i + k + 1]
                            if k == 0 or v == 0:
                                settle()
                            row = PLAN.rows[layer, j] + v
                            if i == first_part and k == 0:
                                ins = V.tensor_scalar(acc[:, row, :], w, cc, None, ALU.mult)
                            else:
                                ins = V.scalar_tensor_tensor(acc[:, row, :], w, cc, acc[:, row, :], ALU.mult, ALU.add)
                            if k == KC - 1 and v == len(vecs) - 1:
                                do(ins, unit_done, done_value(n))
                            else:
                                do(ins)
                done[0] += 1

            def take_mod(g, target, j):
                vecs = len(mod_vectors(target, j))
                wait_filled(dve, g)
                for v in range(vecs):
                    ins = V.tensor_tensor(MOD[:, target % 2, v, 4 * j:4 * j + 4], bank_of(g)[:, 4 * v:4 * v + 4],
                                          col(f"bmod_{target}", 4 * j, 4), ALU.add)
                    if v == vecs - 1:
                        take(ins, g)
                    else:
                        do(ins)
                if j in (2, 3, 8, 9):
                    which, c = (0, 4 * j - 8) if j < 4 else (1, 4 * j - 32)
                    settle()
                    for v in range(vecs):
                        do(V.scalar_tensor_tensor(MUL[:, target % 2, v, which, c:c + 4], MOD[:, target % 2, v, 4 * j:4 * j + 4],
                                                  1.0, col(f"n{which + 1}_{target}", c, 4), ALU.add, ALU.mult))

            def advance(n):
                for _ in range(n):
                    used[0] += 1
                    if used[0] + NR <= PLAN.units:
                        while done[0] <= PLAN.index[used[0] + NR - 1]:
                            stream_unit()

            def block_of(layer, name):
                for i in range(PLAN.step[layer, name][1]):
                    unit_of_block(layer, name, i)
                return PLAN.step[layer, name][2]

            def most_of(layer, name, start=0):
                for i in range(start, PLAN.step[layer, name][1] - 1):
                    unit_of_block(layer, name, i)
                return PLAN.step[layer, name][2]

            def last_of(layer, name):
                unit_of_block(layer, name, PLAN.step[layer, name][1] - 1)

            def unit_of_block(layer, name, i):
                advance(1)
                if (layer, name, i) in PLAN.mods:
                    take_mod(grp(layer, name, at=i), *PLAN.mods[layer, name, i])

            def invert(layer, name, v, tok):
                g = grp(layer, name)
                wait_filled(dve, g)
                settle()
                ins = V.reciprocal(var[:, tok], bank_of(g)[:, tok])
                if (layer, name) in BOTH and v == 0:
                    do(ins, s["var_ready"], BOTH.index((layer, name)) + 1)
                else:
                    take(ins, g)

            def norm(layer, name, T, behind=None):
                def scale_of(v, tok):
                    if (layer, name) != (0, "n1"):
                        invert(layer, name, v, tok)
                    dve.wait_ge(s["rstd_ready"], HALF_OF[layer, name] + v + 1)
                    settle()
                scale_of(*halves(T)[0])
                if name == "nf":
                    last_norm = layer == 3
                    for c in range(DC):
                        do(V.scalar_tensor_tensor(X[:, c, 0:S], X[:, c, 0:S], col("final2" if last_norm else "final1", c),
                                                  rstd[:, 0:S], ALU.mult, ALU.mult),
                           s["out_ready" if last_norm else "xf_ready"], c + 1)
                    if behind:
                        unit_of_block(*behind)
                    return
                which = 0 if name == "n1" else 1
                base = HREADY[layer, name]
                par = layer % 2

                def scaled(c, v, tok):
                    if DC * v + c >= 4:
                        dve.wait_ge(s["h_ready"], base + DC * v + c - 3)
                    do(V.scalar_tensor_tensor(tt[:, c % 4, tok], X[:, c, tok], MUL[:, par, v, which, c:c + 1],
                                              rstd[:, tok], ALU.mult, ALU.mult), s["t_ready"], base + DC * v + c + 1)

                def rest(c, v, tok):
                    dve.wait_ge(s["hhi_ready"], base + DC * v + c + 1)
                    do(V.scalar_tensor_tensor(h_lo[:, c, tok], tt[:, c % 4, tok],
                                              MOD[:, par, v, 3 * DC * which + c:3 * DC * which + c + 1],
                                              h_hi[:, c, tok].bitcast(F32), ALU.add, ALU.subtract),
                       s["h_ready"], base + DC * v + c + 1)

                for v, tok in halves(T):
                    if v:
                        scale_of(v, tok)
                    scaled(0, v, tok)
                    scaled(1, v, tok)
                    for c in range(2, DC):
                        if (layer, name) == (0, "n1") and c % 2 == 0:
                            while done[0] <= PLAN.index[c // 2 - 1]:
                                stream_unit()
                        scaled(c, v, tok)
                        rest(c - 2, v, tok)
                        if v and layer == 3 and c % 2 == 1 and c > 1:
                            unit_of_block(3, "pu", c // 2 - 1)
                    rest(DC - 2, v, tok)
                    rest(DC - 1, v, tok)
                    if v == 0 and behind:
                        unit_of_block(*behind)
                if (layer, name) == (0, "n1"):
                    while done[0] <= PLAN.index[NR - 1]:
                        stream_unit()

            def residual(layer, name, nb, gate, T, start=0):
                g0, nu = PLAN.step[layer, name][2], PLAN.step[layer, name][1]
                before_norm = name in ("wo1", "dn1", "d11")
                for i in range(start, nu - 2 if before_norm else nu - 1):
                    unit_of_block(layer, name, i)
                for n in range(4):
                    c = 4 * nb + n
                    wait_filled(dve, g0 + n)
                    if n == 0:
                        settle()
                    if T == T2:
                        do(V.scalar_tensor_tensor(X[:, c, S:T2], bank_of(g0 + n)[:, S:T2], MOD[:, layer % 2, 1, gate * DC + c:gate * DC + c + 1],
                                                  X[:, c, S:T2], ALU.mult, ALU.add))
                    take(V.scalar_tensor_tensor(X[:, c, 0:S], bank_of(g0 + n)[:, 0:S], MOD[:, layer % 2, 0, gate * DC + c:gate * DC + c + 1],
                                                X[:, c, 0:S], ALU.mult, ALU.add), g0 + n)
                if before_norm:
                    unit_of_block(layer, name, nu - 2)
                elif name != "d01":
                    last_of(layer, name)

            do(V.memset(mean_D[:, :], 1.0 / D), s["const_ready"], 1)
            do(V.memset(mean_H[:, :], 1.0 / DK1), s["const_ready"], 2)
            do(V.memset(ones[:, :], 1.0), s["const_ready"], 3)
            do(V.memset(eps[:, :], EPS), s["const_ready"], 4)
            dve.wait_ge(s["loaded"], 16)
            dve.wait_ge(s["csil_ready"], 1)
            for j in range(4):
                for _ in range(4):
                    stream_unit()
                if j:
                    take_mod(grp("pro", j - 1), 0, j - 1)
                if j == 2:
                    invert(0, "n1", *halves(S)[0])
            take_mod(grp("pro", 3), 0, 3)

            for L in range(2):
                norm(L, "n1", S, behind=(0, "dn1", FC // 2 - 1) if L else None)
                for name in ("uf0", "uf1", "q0", "q1", "k0", "k1"):
                    block_of(L, name)
                for cc in range(DC // 2):
                    g = grp(L, "F2", cc)
                    dve.wait_ge(s["fhi_ready"], 4 * L + cc + 1)
                    take(V.tensor_tensor(h_lo[:, 2 * cc:2 * cc + 2, S:T2], bank_of(g)[:, :].rearrange("p (c t) -> p c t", c=2),
                                         h_hi[:, 2 * cc:2 * cc + 2, S:T2].bitcast(F32), ALU.subtract), g)
                for name in ("v0", "v1", "af0"):
                    block_of(L, name)

                def decayed(h):
                    g = grp(L, f"S{h}")
                    wait_filled(dve, g)
                    if h >= 2:
                        wait_filled(dve, grp(L, f"V{h - 2}"))
                    if h == 0 and L == 0:
                        dve.wait_ge(s["loaded1"], 64)
                    take(V.tensor_tensor(probs1[:, h % 2, :, :], bank_of(g)[:, :].rearrange("p (j t) -> p j t", j=2),
                                         decay[:, h, :, :], ALU.mult), g)
                decayed(0)
                decayed(1)
                block_of(L, "af1")
                decayed(2)
                decayed(3)

                def gated_fourier(nb):
                    g0 = most_of(L, f"wf{nb}")
                    for n in range(4):
                        wait_filled(dve, g0 + n)
                        wait_taken(dve, grp(L, f"af{nb}", n))
                        take(V.tensor_tensor(y1[:, 4 * nb + n, :], bank_of(g0 + n)[:, 0:S], y1[:, 4 * nb + n, :], ALU.mult), g0 + n)
                    last_of(L, f"wf{nb}")
                gated_fourier(0)
                gated_fourier(1)
                for hp in range(2):
                    g = grp(L, f"M{hp}")
                    wait_filled(dve, g)
                    for i in range(2):
                        qh = q1[:, 4 * hp + 2 * i:4 * hp + 2 * i + 2, :]
                        mu = bank_of(g)[:, i * S:(i + 1) * S].rearrange("p (a t) -> p a t", a=1).to_broadcast([P, 2, S])
                        ins = V.tensor_tensor(qh, qh, mu, ALU.subtract)
                        if i == 0:
                            do(ins)
                        else:
                            take(ins, g)
                def silu_gate(nb):
                    g0 = most_of(L, f"g{nb}")
                    for n in range(4):
                        dve.wait_ge(s["g_sig"], DC * L + 4 * nb + n + 1)
                        take(V.tensor_tensor(g1[:, 4 * nb + n, :], bank_of(g0 + n)[:, 0:S], g1[:, 4 * nb + n, :], ALU.mult), g0 + n)
                    last_of(L, f"g{nb}")

                silu_gate(0)
                for hp in range(2):
                    g = grp(L, f"R{hp}")
                    wait_filled(dve, g)
                    take(V.reciprocal(var2[:, hp, :, :], bank_of(g)[:, :].rearrange("p (i t) -> p i t", i=2)), g)
                silu_gate(1)
                for name in ("ar0", "ar1"):
                    block_of(L, name)
                for nb in range(2):
                    g0 = most_of(L, f"wr{nb}")
                    y = y1[:, 4 * nb:4 * nb + 4, :]
                    a = k1[:, 4 * nb:4 * nb + 4, :]
                    for n in range(4):
                        wait_filled(dve, g0 + n)
                        wait_taken(dve, grp(L, f"ar{nb}", n))
                        take(V.tensor_tensor(k1[:, 4 * nb + n, :], bank_of(g0 + n)[:, 0:S], k1[:, 4 * nb + n, :], ALU.mult), g0 + n)
                    settle()
                    do(V.tensor_tensor(y, y, a, ALU.add), s["m_ready"], 2 * L + nb + 1)
                    dve.wait_ge(s["mhi_ready"], 2 * L + nb + 1)
                    settle()
                    do(V.tensor_tensor(h_lo[:, 4 * nb:4 * nb + 4, 0:S], y, h_hi[:, 4 * nb:4 * nb + 4, 0:S].bitcast(F32),
                                       ALU.subtract), s["mm_ready"], 2 * L + nb + 1)
                    last_of(L, f"wr{nb}")
                for nb in range(2):
                    residual(L, f"wo{nb}", nb, 2, S)
                norm(L, "n2", S, behind=(L, "wo1", 3))
                for b in range(FC // 2):
                    g0 = most_of(L, f"up{b}")
                    it = L * (FC // 2) + b
                    y = conv[:, b % 2, :, :]
                    for n in range(4):
                        ch = 2 * b + n if n < 2 else FC + 2 * b + n - 2
                        u = bank_of(g0 + n)
                        dve.wait_ge(s["lin_ready"], 4 * it + n + 1)
                        do(V.scalar_tensor_tensor(y[:, n, 1:S], u[:, 0:S - 1], col(f"convw_{L}", ch), y[:, n, 1:S],
                                                  ALU.mult, ALU.add))
                    settle()
                    for n in range(4):
                        ch = 2 * b + n if n < 2 else FC + 2 * b + n - 2
                        take(V.scalar_tensor_tensor(y[:, n, 0:S - 1], bank_of(g0 + n)[:, 1:S], col(f"convw_{L}", 4 * FC + ch),
                                                    y[:, n, 0:S - 1], ALU.mult, ALU.add), g0 + n)
                    last_of(L, f"up{b}")
                for nb in range(2):
                    residual(L, f"dn{nb}", nb, 5, S)
                if L == 1:
                    norm(1, "nf", S, behind=(1, "dn1", FC // 2 - 1))

            for L in (2, 3):
                with_ctx = L == 2
                T = T2 if with_ctx else S
                ns = T // S
                norm(L, "n1", T2, behind=(2, "d11", 7) if L == 3 else None)
                if L == 2:
                    block_of(L, "pu")
                else:
                    last_of(L, "pu")
                g0 = block_of(L, "vs")
                for tk in range(T // P):
                    nth = (0 if L == 2 else 4) + tk + 1
                    wait_filled(dve, g0 + tk)
                    if tk == 0:
                        settle()
                    do(V.bn_stats(stats[:, tk, 0:6], bank_of(g0 + tk)[:, 0:2 * P]))
                    settle()
                    do(V.bn_aggr(stats[:, tk, 6:8], stats[:, tk, 0:6]))
                    settle()
                    do(V.tensor_scalar(stats[:, tk, 8:9], stats[:, tk, 7:8], EPS, None, ALU.add))
                    settle()
                    do(V.reciprocal(stats[:, tk, 9:10], stats[:, tk, 8:9]), s["vvar_ready"], nth)
                for tk in range(T // P):
                    nth = (0 if L == 2 else 4) + tk + 1
                    dve.wait_ge(s["vstd_ready"], nth)
                    settle()
                    take(V.tensor_scalar(vn[:, tk, :], bank_of(g0 + tk)[:, 0:2 * P], stats[:, tk, 6:7], stats[:, tk, 10:11],
                                         ALU.subtract, ALU.mult), g0 + tk)
                if L == 2:
                    dve.wait_ge(s["loaded2"], 64)

                def rotary(i, name):
                    g = grp(L, name)
                    wait_filled(dve, g)
                    take(V.tensor_tensor(ropeA[:, i, :, :], bank_of(g)[:, :].rearrange("p (c t) -> p c t", c=2),
                                         rope2[:, 1:2, :].to_broadcast([P, 2, S]), ALU.mult), g)
                block_of(L, "q")
                most_of(L, "k")
                rotary(0, "rq0")
                rotary(1, "rq1")
                last_of(L, "k")
                for i in range(2):
                    rotary(2 + i, f"rk{i}")
                    x = k2[:, 2 * i:2 * i + 2, 0:S]
                    do(V.tensor_tensor(x, x, rope2[:, 0:1, :].to_broadcast([P, 2, S]), ALU.mult))
                    settle()
                    do(V.tensor_tensor(x, x, ropeA[:, 2 + i, :, :], ALU.add), s["k2_rot"], 2 * (L - 2) + i + 1)
                for c in range(2):
                    g = grp(L, "pool", c)
                    dve.wait_ge(s["phi_ready"], 2 * (L - 2) + c + 1)
                    take(V.scalar_tensor_tensor(b_lo[:, c, 0:T], bank_of(g)[:, 0:T], col(f"pscale_{L}", c),
                                                b_hi[:, c, 0:T].bitcast(F32), ALU.mult, ALU.subtract), g)
                for fc in range(2):
                    g = grp(L, "mix", fc)
                    wait_filled(dve, g)
                    take(V.tensor_tensor(u2[:, fc, 0:T], bank_of(g)[:, 0:T], u2[:, fc, 0:T], ALU.mult), g)

                def values_and_branches():
                    for fc in range(2):
                        dve.wait_ge(s["sohi_ready"], 2 * (L - 2) + fc + 1)
                        do(V.tensor_tensor(b_lo[:, 2 + fc, 0:T], u2[:, fc, 0:T], b_hi[:, 2 + fc, 0:T].bitcast(F32),
                                           ALU.subtract), s["b_ready"], 2 * (L - 2) + fc + 1)
                    block_of(L, "v")

                per = PPER[L]

                def maxima(h):
                    nth = HEADS2 * (L - 2) + h
                    dve.wait_ge(s[f"bias_in{nth % 2}"], 16 * (nth // 2 + 1))
                    settle()
                    for qt, tag in enumerate("ab"):
                        g = grp(L, f"X{h}{tag}")
                        dve.wait_ge(s["ctx_copied"], 2 * nth + qt + 1)
                        take(V.tensor_tensor(sc[:, qt, 0:S], bank_of(g)[:, 0:S], bias[:, nth % 2, qt, :], ALU.add), g)
                    settle()
                    for qt in range(2):
                        do(V.tensor_reduce(small[:, 0, qt:qt + 1], sc[:, qt, :], AX_X, ALU.max, negate=True),
                           s["nmax_ready"], PREADY[L] + per * h + qt + 1)
                    if with_ctx:
                        g = grp(L, f"C{h}")
                        wait_filled(dve, g)
                        do(V.tensor_reduce(small[:, 0, 2:4], bank_of(g)[:, :].rearrange("p (q k) -> p q k", q=2), AX_X,
                                           ALU.max, negate=True), s["nmax_ready"], PREADY[L] + per * h + 3)

                def normalise(h):
                    nth = HEADS2 * (L - 2) + h
                    dve.wait_ge(s["exp_ready"], PREADY[L] + per * h + per)
                    if with_ctx:
                        wait_taken(dve, grp(L, f"C{h}"))
                    settle()
                    n = 4 if with_ctx else 2
                    do(V.reciprocal(small[:, 2, 0:n], small[:, 1, 0:n]))
                    settle()
                    for qt in range(2):
                        do(V.tensor_scalar(sc[:, qt, :], sc[:, qt, :], small[:, 2, qt:qt + 1], None, ALU.mult),
                           s["p_ready"], PREADY[L] + per * h + qt + 1)
                    if with_ctx:
                        do(V.tensor_scalar(scc[:, 0, :], scc[:, 0, :], small[:, 2, 2:3], None, ALU.mult))
                        do(V.tensor_scalar(scc[:, 1, :], scc[:, 1, :], small[:, 2, 3:4], None, ALU.mult),
                           s["p_ready"], PREADY[L] + per * h + 3)

                def gated(name, start=0):
                    g0 = most_of(L, name, start)
                    nb = int(name[2])
                    gate = {"p": "gp", "s": "gs", "a": "ga"}[name[0]] + name[2]
                    src = gtb if gate == "ga1" else gt
                    for n in range(4):
                        wait_filled(dve, g0 + n)
                        wait_taken(dve, grp(L, gate, n))
                        if name[0] == "p":
                            dst = y2[:, 4 * nb + n, 0:T]
                        else:
                            i = 16 * (L - 2) + (8 if name[0] == "a" else 0) + 4 * nb + n
                            if i >= 2:
                                dve.wait_ge(s["y_added"], i - 1)
                            dst = gt2[:, i % 2, 0:T]
                        take(V.tensor_tensor(dst, bank_of(g0 + n)[:, 0:T], src[:, n, 0:T], ALU.mult), g0 + n)
                    last_of(L, name)

                def attention_lo(c):
                    dve.wait_ge(s["aohi_ready"], 4 * (L - 2) + c + 1)
                    do(V.tensor_tensor(b_lo[:, c, 0:T], q2[:, c, 0:T], b_hi[:, c, 0:T].bitcast(F32), ALU.subtract),
                       s["a_ready"], 4 * (L - 2) + c + 1)

                for h in range(HEADS2):
                    maxima(h)
                    normalise(h)
                    if h == HEADS2 - 1:
                        for c in range(3):
                            attention_lo(c)
                    for name in ATTENTION_FILL[h]:
                        if name == "v":
                            values_and_branches()
                        elif name[0] == "g":
                            block_of(L, name)
                        else:
                            gated(name)
                attention_lo(3)

                def merged_lo(nb):
                    for c in range(4 * nb, 4 * nb + 4):
                        i = 4 + DC * (L - 2) + c + 1
                        dve.wait_ge(s["mhi_ready"], i)
                        do(V.tensor_tensor(h_lo[:, c, 0:T], y2[:, c, 0:T], h_hi[:, c, 0:T].bitcast(F32), ALU.subtract),
                           s["mm_ready"], i)
                gated("ao0")
                unit_of_block(L, "ao1", 0)
                merged_lo(0)
                gated("ao1", start=1)
                unit_of_block(L, "wo0", 0)
                merged_lo(1)
                for nb in range(2):
                    residual(L, f"wo{nb}", nb, 2, T, start=1 - nb)
                norm(L, "n2", T, behind=(L, "wo1", 3))

                def hidden2_lo(b, part):
                    for n in range(2 * part, 2 * part + 2):
                        i = 32 * (L - 2) + 4 * b + n + 1
                        dve.wait_ge(s["fhihi_ready"], i)
                        do(V.tensor_tensor(f_lo[:, (4 * b + n) % 16, 0:T], relu[:, n, 0:T],
                                           f_hi[:, (4 * b + n) % 16, 0:T].bitcast(F32), ALU.subtract), s["ff_ready"], i)

                for half in range(2):
                    for b in range(4 * half, 4 * half + 4):
                        for i in range(4):
                            unit_of_block(L, f"f{b}", i)
                            if b % 4 and i < 2:
                                hidden2_lo(b - 1, i)
                    for part in range(2):
                        unit_of_block(L, f"d{half}0", part)
                        hidden2_lo(4 * half + 3, part)
                    residual(L, f"d{half}0", 0, 5, T, start=2)
                    residual(L, f"d{half}1", 1, 5, T)
                    if not half:
                        last_of(L, "d01")
                if L == 3:
                    norm(3, "nf", S, behind=(3, "d11", 7))

        @block.gpsimd
        def _(pool):
            G = nc.gpsimd
            steps = sem("pool_steps")
            count = [0]

            def do(ins):
                count[0] += 1
                ins.then_inc(steps, 1)

            def settle():
                pool.wait_ge(steps, count[0])

            def add_squares(layer, name, T):
                nth = NORMS.index((layer, name))
                at = 3 * ADDED.index((layer, name))
                wait_filled(pool, grp(*NORMS[nth - 1]))
                for c in range(1, DC // 2):
                    pool.wait_ge(s["sq_ready"], SQ_BEFORE[layer, name] + c + 1)
                    if c > 1:
                        pool.wait_ge(s["sq_added"], at + c - 1)
                    G.tensor_tensor(ssum[:, 0:T], sq[:, 0, 0:T] if c == 1 else ssum[:, 0:T], sq[:, c, 0:T],
                                    ALU.add).then_inc(s["sq_added"], 1)

            for L in range(2):
                if L:
                    add_squares(1, "n1", S)
                if L == 0:
                    pool.wait_ge(s["loaded1"], 64)
                sin4 = rope1[:, 1:2, :].to_broadcast([P, 4, S])
                for x, blk, tmp_, sm in ((q1, "q", rope_q, "uq_rot"), (k1, "k", rope_k, "uk_rot")):
                    for n in range(DC):
                        wait_taken(pool, grp(L, f"{blk}{n // 4}", n % 4))
                    xv = x[:, :, :].rearrange("p (h e) t -> p e h t", e=2)
                    tv = tmp_[:, :, :].rearrange("p (h e) t -> p e h t", e=2)
                    do(G.tensor_tensor(tv[:, 0], xv[:, 1], sin4, ALU.mult))
                    do(G.tensor_tensor(tv[:, 1], xv[:, 0], sin4, ALU.mult))
                    settle()
                    for half in range(2):
                        xx = x[:, 4 * half:4 * half + 4, :]
                        do(G.tensor_tensor(xx, xx, rope1[:, 0:1, :].to_broadcast([P, 4, S]), ALU.mult))
                    settle()
                    do(G.tensor_tensor(xv[:, 0], xv[:, 0], tv[:, 0], ALU.subtract))
                    G.tensor_tensor(xv[:, 1], xv[:, 1], tv[:, 1], ALU.add).then_inc(s[sm], 1)
                for hp in range(2):
                    pool.wait_ge(s["rstd2_ready"], 2 * L + hp + 1)
                    qh = q1[:, 4 * hp:4 * hp + 4, :]
                    for i in range(2):
                        qi = qh[:, 2 * i:2 * i + 2, :]
                        do(G.tensor_tensor(qi, qi, rstd2[:, hp, i:i + 1, :].to_broadcast([P, 2, S]), ALU.mult))
                    settle()
                    for n in range(4):
                        wait_taken(pool, grp(L, f"g{hp}", n))
                    G.tensor_tensor(qh, qh, g1[:, 4 * hp:4 * hp + 4, :], ALU.mult).then_inc(s["yn_ready"], 1)
                    pool.wait_ge(s["rhi_ready"], 2 * L + hp + 1)
                    G.tensor_tensor(r_lo[:, 4 * hp:4 * hp + 4, :], qh, r_hi[:, 4 * hp:4 * hp + 4, :].bitcast(F32),
                                    ALU.subtract).then_inc(s["r_ready"], 1)
                add_squares(L, "n2", S)
                for b in range(FC // 2):
                    it = L * (FC // 2) + b
                    y = conv[:, b % 2, :, :]
                    pool.wait_ge(s["gelu_ready"], it + 1)
                    wait_taken(pool, grp(L, f"up{b}", 3))
                    G.tensor_tensor(y[:, 2:4, :], y[:, 0:2, :], y[:, 2:4, :], ALU.mult).then_inc(s["u_ready"], 1)
                    pool.wait_ge(s["uhi_ready"], it + 1)
                    G.tensor_tensor(u_lo[:, 2 * b:2 * b + 2, :], y[:, 2:4, :], u_hi[:, 2 * b:2 * b + 2, :].bitcast(F32),
                                    ALU.subtract).then_inc(s["uu_ready"], 1)

            for L in (2, 3):
                T = T2 if L == 2 else S
                ns = T // S
                if L == 2:
                    add_squares(1, "nf", S)
                else:
                    add_squares(3, "n1", T2)
                wait_filled(pool, grp(1, "nf") if L == 2 else grp(3, "n1"))
                do(G.memset(ps2[:, :, :, :], 0.0))
                do(G.memset(ps4[:, :, :, :], 0.0))
                G.memset(pp[:, :, :, :], 0.0).then_inc(s["pad_ready"], 1)
                settle()
                for n in range(2):
                    wait_taken(pool, grp(L, "pu", n))
                W = S + 2 * 8
                do(G.tensor_tensor(ps2[:, :, 0:ns, 1:W], pp[:, :, 0:ns, 0:W - 1], pp[:, :, 0:ns, 1:W], ALU.add))
                settle()
                do(G.tensor_tensor(ps4[:, :, 0:ns, 1:W - 1], ps2[:, :, 0:ns, 0:W - 2], ps2[:, :, 0:ns, 2:W], ALU.add))
                pl = pooled[:, :, 0:T].rearrange("p c (s t) -> p c s t", t=S)

                def window(rows, c, src):
                    for si in range(ns):
                        do(G.tensor_tensor(pl[rows, c, si, :], src[rows, c, si, 8:8 + S], rinv[rows, c, :], ALU.mult))
                lo, up = slice(0, 64), slice(64, 128)
                if L == 2:
                    pool.wait_ge(s["loaded2"], 64)
                settle()
                window(lo, 0, ps2)
                settle()
                window(up, 0, ps4)
                settle()
                do(G.tensor_tensor(ps2[:, 1, 0:ns, 2:W - 2], ps4[:, 1, 0:ns, 0:W - 4], ps4[:, 1, 0:ns, 4:W], ALU.add))
                settle()
                window(lo, 1, ps2)
                settle()
                do(G.tensor_tensor(ps4[up, 1, 0:ns, 6:W - 6], ps2[up, 1, 0:ns, 2:W - 10], ps2[up, 1, 0:ns, 10:W - 2], ALU.add))
                settle()
                window(up, 1, ps4)
                settle()
                do(G.tensor_tensor(pl[:, 0], pl[:, 0], pp[:, 0, 0:ns, 8:8 + S], ALU.subtract))
                G.tensor_tensor(pl[:, 1], pl[:, 1], pp[:, 1, 0:ns, 8:8 + S], ALU.subtract).then_inc(s["pooled_ready"], 1)
                for i in range(2):
                    x = q2[:, 2 * i:2 * i + 2, 0:S]
                    wait_taken(pool, grp(L, f"rq{i}"))
                    do(G.tensor_tensor(x, x, rope2[:, 0:1, :].to_broadcast([P, 2, S]), ALU.mult))
                    settle()
                    G.tensor_tensor(x, x, ropeA[:, i, :, :], ALU.add).then_inc(s["q2_rot"], 1)

                def load_bias(h):
                    nth = HEADS2 * (L - 2) + h
                    if h >= 2:
                        wait_taken(pool, grp(L, f"X{h - 2}a"))
                        wait_taken(pool, grp(L, f"X{h - 2}b"))
                    pool.dma_start(bias[:, nth % 2, :, :], t["bias"][L - 2, h]).then_inc(s[f"bias_in{nth % 2}"], 16)

                def add_branch(name):
                    nb = int(name[2])
                    for n in range(4):
                        i = 16 * (L - 2) + (8 if name[0] == "a" else 0) + 4 * nb + n
                        c = 4 * nb + n
                        wait_taken(pool, grp(L, name, n))
                        if i:
                            pool.wait_ge(s["y_added"], i)
                        G.tensor_tensor(y2[:, c, 0:T], y2[:, c, 0:T], gt2[:, i % 2, 0:T], ALU.add).then_inc(s["y_added"], 1)

                pool.wait_ge(s["q2_rot"], 2 * (L - 1))
                load_bias(0)
                load_bias(1)
                for h in range(HEADS2):
                    if 2 <= h + 1 < HEADS2:
                        load_bias(h + 1)
                    for name in ATTENTION_FILL[h]:
                        if name[0] == "s":
                            add_branch(name)
                add_branch("ao0")
                add_branch("ao1")
                pool.wait_ge(s["y_added"], 16 * (L - 1))
                add_squares(L, "n2", T)
                for b in range(8):
                    for n in range(4):
                        i = 32 * (L - 2) + 4 * b + n
                        wait_taken(pool, grp(L, f"f{b}", n))
                        G.tensor_tensor(relu[:, n, 0:T], relu[:, n, 0:T], relu[:, n, 0:T], ALU.mult).then_inc(s["fhid_ready"], 1)
                if L == 3:
                    add_squares(3, "nf", S)


NORMS = [(0, "n1"), (0, "n2"), (1, "n1"), (1, "n2"), (1, "nf"), (2, "n1"), (2, "n2"), (3, "n1"), (3, "n2"), (3, "nf")]
ADDED = [_k for _k in NORMS if _k not in ((0, "n1"), (2, "n1"))]
BOTH = [(2, "n1"), (2, "n2"), (3, "n1")]
HALF_OF, HREADY = {}, {}
SQUARES = {_k: [(_c, slice(0, T2 if _k in BOTH else S)) for _c in range(DC)] for _k in NORMS}
SQUARES[2, "n1"] = [(_c, slice(_a, _a + S)) for _a in (S, 0) for _c in range(DC)]
SQ_BEFORE = {_k: sum(len(SQUARES[_m]) for _m in NORMS[:NORMS.index(_k)]) for _k in NORMS}
_halves = _chunks = 0
for _k in NORMS:
    HALF_OF[_k], HREADY[_k] = _halves, _chunks
    _halves += 2 if _k in BOTH else 1
    _chunks += 0 if _k[1] == "nf" else 2 * DC if _k in BOTH else DC
PPER = {2: 3, 3: 2}
PREADY = {2: 0, 3: 3 * HEADS2}
MOD_LAST, STREAM_UNIT = {}, {}
for _n, _e in enumerate(PLAN.stream):
    if _e[0] == "mod":
        MOD_LAST[_e[1], _e[2]] = _n
for _m, _n in enumerate(PLAN.index):
    STREAM_UNIT[_n] = _m


def unit_of(inputs, entry):
    if entry[0] == "mod":
        _, layer, j, i = entry
        w = inputs["ada_w"][layer] if layer < 2 else inputs["w_mod_2"][layer - 2]
        return w[256 * i:256 * i + 256, COLS * j:COLS * (j + 1)].reshape(KC, P, COLS).transpose(1, 0, 2)
    _, layer, name, i = entry
    if layer < 2:
        order = ["uf", "q", "k", "v", "g", "af", "ar"]
        if name[:-1] in order and name[-1] in "01":
            w, c = inputs["w_in"][layer], D * order.index(name[:-1]) + COLS * int(name[-1])
        elif name[:2] in ("wf", "wr", "wo"):
            w, c = inputs[{"wf": "w_fourier", "wr": "w_ret", "wo": "w_out"}[name[:2]]][layer], COLS * int(name[2:])
        elif name[:2] == "dn":
            w, c = inputs["ffn_down"][layer], COLS * int(name[2:])
        else:
            b = int(name[2:])
            w = inputs["ffn_up"][layer][256 * i:256 * i + 256]
            w = np.concatenate([w[:, 256 * b:256 * b + 256], w[:, D_FF + 256 * b:D_FF + 256 * b + 256]], axis=1)
            return w.reshape(KC, P, COLS).transpose(1, 0, 2)
        return w[256 * i:256 * i + 256, c:c + COLS].reshape(KC, P, COLS).transpose(1, 0, 2)
    l = layer - 2
    if name == "vs":
        w = inputs["w_in_2"][l][512 * i:512 * i + 512, 512:768]
        return w.reshape(4, P, 2 * P).transpose(1, 0, 2)
    first = {"pu": 0, "q": 768, "k": 1280, "v": 1792, "gp0": 2304, "gp1": 2816, "gs0": 3328, "gs1": 3840,
             "ga0": 4352, "ga1": 4864}
    if name in first:
        w, c = inputs["w_in_2"][l], first[name]
    elif name[0] == "f":
        w, c = inputs["w_ff1_2"][l], COLS * int(name[1:])
    elif name[0] == "d":
        w, c = inputs["w_ff2_2"][l][2048 * int(name[1]):2048 * (int(name[1]) + 1)], COLS * int(name[2])
    else:
        w = inputs[{"po": "w_pool_out_2", "so": "w_sgu_out_2", "ao": "w_attn_out_2", "wo": "w_o_2"}[name[:2]]][l]
        c = COLS * int(name[2])
    return w[256 * i:256 * i + 256, c:c + COLS].reshape(KC, P, COLS).transpose(1, 0, 2)


def to_columns(v):
    return np.asarray(v).reshape(-1, P).T


def shape_constants():
    f = np.float64
    inv = 10000.0 ** (-np.arange(P, dtype=f) / P)
    ang = inv[:, None] * np.arange(S, dtype=f)[None, :]
    rope1 = np.stack([np.cos(ang), np.sin(ang)], axis=1)
    j, i = np.arange(S, dtype=f)[:, None], np.arange(S, dtype=f)[None, :]
    dec = []
    for h in range(HEADS1):
        gf, gb = 1 - 2.0 ** -(5.0 + h), 1 - 2.0 ** -(5.5 + h)
        dec.append(np.where(j <= i, gf ** np.maximum(i - j, 0), gb ** np.maximum(j - i, 0)) * DK1 ** -0.5)
    decay = np.stack(dec).reshape(HEADS1, 2, P, S).transpose(2, 0, 1, 3)
    a = 2 * np.pi * np.outer(np.arange(P), np.arange(P)) / P
    dftg = np.concatenate([np.cos(a), np.sin(a)], axis=1)
    b = 2 * np.pi * (np.outer(np.arange(S), np.arange(S)) % S) / S
    dfts = (np.stack([np.cos(b), -np.sin(b)]) / np.sqrt(S * P)).reshape(2, 2, P, S).transpose(2, 0, 1, 3)
    nf = DK2 // 4
    inv2 = 10000.0 ** (-np.arange(nf, dtype=f) / nf)
    tok = np.arange(S)
    ang2 = np.concatenate([(tok // GRID_W)[:, None] * inv2, (tok % GRID_W)[:, None] * inv2], axis=1)
    ang2 = ang2[:, (np.arange(P) % DK2) // 2].T
    rope2 = np.stack([np.cos(ang2), np.sin(ang2)], axis=1)
    rot = np.zeros((P, P))
    even = np.arange(0, P, 2)
    rot[even + 1, even], rot[even, even + 1] = -1.0, 1.0
    rinv = np.zeros((P, 2, S))
    for g, w in enumerate((2, 4, 8, 16)):
        cnt = np.clip(tok + (w - w // 2), 0, S) - np.clip(tok - w // 2, 0, S)
        rinv[64 * (g % 2):64 * (g % 2) + 64, g // 2, :] = 1.0 / cnt
    out = dict(rope1=rope1, decay=decay, dftg=dftg, dfts=dfts, rope2=rope2, rotm=rot, rinv=rinv, ident=np.eye(P))
    return {k: np.ascontiguousarray(v, np.float32) for k, v in out.items()}


def bias_layout(rpb):
    tok = np.arange(S)
    row, c = tok // GRID_W, tok % GRID_W
    dr = row[None, :] - row[:, None] + NA_KH - 1
    start = np.clip(c - NA_KW // 2, 0, GRID_W - NA_KW)
    inside = (c[None, :] >= start[:, None]) & (c[None, :] < start[:, None] + NA_KW)
    dc = np.clip(c[None, :] - c[:, None] + NA_KW - 1, 0, 2 * NA_KW - 2)
    full = np.where(inside, rpb[:, :, dr, dc], np.float32(MASKED)).astype(np.float32)
    return full.reshape(2, HEADS2, 2, P, S).transpose(0, 1, 3, 2, 4)


def layouts(inputs):
    a = {k: np.asarray(v) for k, v in inputs.items()}
    stream = np.empty((len(PLAN.stream), P, UNIT), np.float32)
    for n, entry in enumerate(PLAN.stream):
        stream[n] = unit_of(a, entry).reshape(P, UNIT)
    cols = np.zeros((P, NCOL), np.float32)

    def put(name, v, at=0):
        v = to_columns(v)
        cols[:, COLUMNS[name] + at:COLUMNS[name] + at + v.shape[1]] = v

    for i, name in enumerate(("c", "c_2", "c_ctx_2")):
        put("c", a[name], i * DC)
    for layer in range(4):
        sfx, l = ("", layer) if layer < 2 else ("_2", layer - 2)
        put(f"n1_{layer}", a["norm1_g" + sfx][l])
        put(f"n2_{layer}", a["norm2_g" + sfx][l])
        put(f"bmod_{layer}", a["ada_b" if layer < 2 else "b_mod_2"][l])
        if layer < 2:
            put(f"convw_{layer}", a["conv_w"][l])
            put(f"convb_{layer}", a["conv_b"][l])
        else:
            put(f"pscale_{layer}", a["pool_scale_2"][l])
    put("final1", a["final_g"])
    put("final2", a["final_g_2"])
    both = np.concatenate([a["x"][0], a["ctx_2"][0]], axis=0)
    wpool = np.zeros((2, P, 2, P), np.float32)
    for g in range(4):
        r = slice(64 * (g % 2), 64 * (g % 2) + 64)
        wpool[:, r, g // 2, r] = a["w_pool_2"][:, g]
    out = dict(stream=stream, cols=cols,
               x=np.ascontiguousarray(both.T.reshape(DC, P, T2).transpose(1, 0, 2)),
               wpool=wpool, wsgu=np.ascontiguousarray(a["sgu_w_2"].transpose(0, 3, 1, 2)),
               sgub=np.ascontiguousarray(a["sgu_b_2"].reshape(2, 1, 4 * P)),
               bias=np.ascontiguousarray(bias_layout(a["na_rpb_2"])))
    out.update(shape_constants())
    return out


def kernel(**inputs):
    import concourse.bacc as bacc
    from concourse.bass_utils import run_bass_kernel_spmd

    nc = bacc.Bacc("TRN2", target_bir_lowering=False, num_devices=1)
    arrays = layouts(inputs)
    t = {k: nc.dram_tensor(f"in_{k}", v.shape, F32, kind="ExternalInput").ap() for k, v in arrays.items()}
    t["out"] = nc.dram_tensor("out_0", (P, DC, S), F32, kind="ExternalOutput").ap()
    program(nc, t)
    r = run_bass_kernel_spmd(nc, [{f"in_{k}": v for k, v in arrays.items()}], core_ids=[0])
    out = np.asarray(r.results[0]["out_0"])
    return np.ascontiguousarray(out.transpose(1, 0, 2).reshape(D, S).T.reshape(1, S, D))
```
